# Optimizing a Trainium2 kernel written in Bass

```python
import math
import jax, jax.numpy as jnp
from jax import lax
import numpy as np

D_MODEL = 1024
BATCH = 1
SEQ = 512
DEPTH = 2
DEC_BATCH = 8
DEC_SEQ = 1
PAST_LEN = 2048
PAGE_SIZE = 128

EPS = 1e-6
N_SUB = 3
MACARON_W = 0.5
D_FF = 2816
HG_HEADS = 8
HG_KEY = 128
HG_VAL = 128
HG_WIDTH = HG_HEADS * HG_VAL
HG_CHUNK = 64
SSM_HEADS = 16
SSM_HEAD_DIM = 64
SSM_INNER = SSM_HEADS * SSM_HEAD_DIM
SSM_GROUPS = 4
SSM_STATE = 128
SSM_CONV = 4
SSM_CONV_CH = SSM_INNER + 2 * SSM_GROUPS * SSM_STATE
SSM_CHUNK = 64
AB_SIZES = (HG_HEADS * HG_KEY, HG_HEADS * HG_KEY, HG_WIDTH, HG_WIDTH, SSM_INNER, SSM_CONV_CH, SSM_HEADS)
AB_IN = sum(AB_SIZES)
AB_OUT = HG_WIDTH + SSM_INNER
MLA_HEADS = 16
MLA_Q_RANK = 512
MLA_KV_RANK = 256
MLA_NOPE = 128
MLA_ROPE = 64
MLA_V = 128
MLA_SCALE = (MLA_NOPE + MLA_ROPE) ** -0.5
ROPE_THETA = 10000.0
Q_BLOCK = 128

kernel_name = "hgrn2_ssd_mla_macaron_adaln_step"

F32 = jnp.float32

def rmsnorm(x, g):
    xf = x.astype(F32)
    r = lax.rsqrt(jnp.mean(xf * xf, axis=-1, keepdims=True) + EPS)
    return (xf * r).astype(x.dtype) * g

def modulate(x, g, shift, scale):
    return rmsnorm(x, g) * (1 + scale[:, None]) + shift[:, None]

def gated_residual(x, y, g, gate, w):
    return x + w * gate[:, None] * rmsnorm(y, g)

def swiglu(h, wg, wu, wd):
    return (jax.nn.silu(h @ wg) * (h @ wu)) @ wd

def rope(x, pos):
    half = x.shape[-1] // 2
    inv = ROPE_THETA ** (-jnp.arange(half, dtype=F32) / half)
    ang = pos[:, None] * inv[None]
    cos, sin = jnp.cos(ang)[None, :, None], jnp.sin(ang)[None, :, None]
    x1, x2 = x[..., :half].astype(F32), x[..., half:].astype(F32)
    return jnp.concatenate([x1 * cos - x2 * sin, x2 * cos + x1 * sin], axis=-1).astype(x.dtype)

def to_blocks(a, c, n):
    bsz, L = a.shape[:2]
    a = jnp.pad(a, ((0, 0), (0, n * c - L)) + ((0, 0),) * (a.ndim - 2))
    return a.reshape((bsz, n, c) + a.shape[2:]).swapaxes(0, 1)

def hgrn2_chunked(q, k, v, log_f, s0, chunk):
    bsz, L = q.shape[:2]
    c = min(chunk, L)
    n = -(-L // c)
    causal = jnp.tril(jnp.ones((c, c), bool))[None, :, :, None, None]

    def step(s, blk):
        qc, kc, vc, gc = blk
        b = jnp.cumsum(gc, axis=1)
        dec = jnp.exp(jnp.where(causal, b[:, :, None] - b[:, None, :], -jnp.inf))
        att = jnp.einsum('bthk,bshk,btshk->bhts', qc, kc, dec)
        o = jnp.einsum('bhts,bshv->bthv', att, vc) + jnp.einsum('bthk,bhkv->bthv', qc * jnp.exp(b), s)
        b_last = b[:, -1]
        s = jnp.exp(b_last)[..., None] * s + jnp.einsum('bshk,bshv->bhkv', kc * jnp.exp(b_last[:, None] - b), vc)
        return s, o

    blks = (to_blocks(q, c, n), to_blocks(k, c, n), to_blocks(v, c, n), to_blocks(log_f, c, n))
    s, o = lax.scan(step, s0, blks)
    o = o.swapaxes(0, 1).reshape((bsz, n * c) + o.shape[3:])[:, :L]
    return o, s

def ssd_chunked(x, dt, a_neg, bm, cm, s0, chunk):
    bsz, L, nh, pd = x.shape
    ng = bm.shape[2]
    nj = nh // ng
    c = min(chunk, L)
    n = -(-L // c)
    la = (dt * a_neg).reshape(bsz, L, ng, nj)
    xd = (x * dt[..., None]).reshape(bsz, L, ng, nj, pd)
    causal = jnp.tril(jnp.ones((c, c), bool))[None, :, :, None, None]

    def step(s, blk):
        xc, lc, bc, cc = blk
        b = jnp.cumsum(lc, axis=1)
        seg = jnp.exp(jnp.where(causal, b[:, :, None] - b[:, None, :], -jnp.inf))
        cb = jnp.einsum('btgn,bsgn->btsg', cc, bc)
        y = (jnp.einsum('btsg,btsgj,bsgjp->btgjp', cb, seg, xc)
             + jnp.einsum('btgn,bgjnp->btgjp', cc, s) * jnp.exp(b)[..., None])
        b_last = b[:, -1]
        s = (jnp.exp(b_last)[..., None, None] * s
             + jnp.einsum('bsgn,bsgj,bsgjp->bgjnp', bc, jnp.exp(b_last[:, None] - b), xc))
        return s, y

    blks = (to_blocks(xd, c, n), to_blocks(la, c, n), to_blocks(bm, c, n), to_blocks(cm, c, n))
    s, y = lax.scan(step, s0.reshape((bsz, ng, nj) + s0.shape[2:]), blks)
    y = y.swapaxes(0, 1).reshape(bsz, n * c, nh, pd)[:, :L]
    return y, s.reshape((bsz, nh) + s.shape[3:])

def mixer_ab(h, layer, hg_s0, ssm_s0, conv_prev, P):
    bsz, L = h.shape[:2]
    proj = h @ P['w_in_ab']
    q_a, f_a, i_a, g_a, z_b, xbc, dt_raw = jnp.split(proj, np.cumsum(AB_SIZES)[:-1].tolist(), axis=-1)
    lb = jnp.cumsum(jax.nn.softmax(P['hg_lb_logits'].astype(F32), axis=0), axis=0)[layer]
    fr = f_a.astype(F32)
    log_f = jnp.log(lb + (1 - lb) * jax.nn.sigmoid(fr))
    k_a = (1 - lb) * jax.nn.sigmoid(-fr)
    hs = lambda t, d: t.reshape(bsz, L, HG_HEADS, d)
    o_a, hg_s = hgrn2_chunked(hs(jax.nn.silu(q_a.astype(F32)), HG_KEY), hs(k_a, HG_KEY),
                              hs(i_a.astype(F32), HG_VAL), hs(log_f, HG_KEY), hg_s0.astype(F32), HG_CHUNK)
    o_a = rmsnorm(o_a, P['hg_norm'].astype(F32).reshape(HG_HEADS, HG_VAL)).reshape(bsz, L, HG_WIDTH)
    o_a = o_a.astype(h.dtype) * jax.nn.silu(g_a)
    xbc_pad = jnp.concatenate([conv_prev.astype(xbc.dtype), xbc], axis=1)
    conv = lax.conv_general_dilated(xbc_pad, P['ssm_conv_w'][:, None, :], window_strides=(1,),
                                    padding='VALID', dimension_numbers=('NWC', 'WIO', 'NWC'),
                                    feature_group_count=SSM_CONV_CH)
    xbc_c = jax.nn.silu(conv + P['ssm_conv_b'])
    conv_state = xbc_pad[:, -(SSM_CONV - 1):]
    x_b, b_b, c_b = jnp.split(xbc_c, [SSM_INNER, SSM_INNER + SSM_GROUPS * SSM_STATE], axis=-1)
    dt = jax.nn.softplus(dt_raw.astype(F32) + P['ssm_dt_bias'].astype(F32))
    a_neg = -jnp.exp(P['ssm_a_log'].astype(F32))
    xh = x_b.astype(F32).reshape(bsz, L, SSM_HEADS, SSM_HEAD_DIM)
    grp = lambda t: t.astype(F32).reshape(bsz, L, SSM_GROUPS, SSM_STATE)
    y, ssm_s = ssd_chunked(xh, dt, a_neg, grp(b_b), grp(c_b), ssm_s0.astype(F32), SSM_CHUNK)
    y = (y + P['ssm_d'].astype(F32)[:, None] * xh).reshape(bsz, L, SSM_INNER) * jax.nn.silu(z_b.astype(F32))
    y = rmsnorm(y.reshape(bsz, L, SSM_GROUPS, SSM_INNER // SSM_GROUPS),
                P['ssm_norm'].astype(F32).reshape(SSM_GROUPS, -1)).reshape(bsz, L, SSM_INNER).astype(h.dtype)
    out = jnp.concatenate([o_a, y], axis=-1) @ P['w_out_ab']
    return out, hg_s.astype(hg_s0.dtype), ssm_s.astype(ssm_s0.dtype), conv_state

def mla_attention(q_lat, q_pe, ckv, kpe, past_ckv, past_kpe):
    L = q_lat.shape[1]
    outs = []
    for start in range(0, L, Q_BLOCK):
        stop = min(start + Q_BLOCK, L)
        ql, qp = q_lat[:, start:stop], q_pe[:, start:stop]
        kc, kp = ckv[:, :stop], kpe[:, :stop]
        s = (jnp.einsum('bqhr,bkr->bhqk', ql, kc) + jnp.einsum('bqhd,bkd->bhqk', qp, kp)).astype(F32) * MLA_SCALE
        mask = jnp.arange(stop)[None, :] <= jnp.arange(start, stop)[:, None]
        s = jnp.where(mask, s, -jnp.inf)
        if past_ckv is None:
            p = jax.nn.softmax(s, axis=-1).astype(ckv.dtype)
            o = jnp.einsum('bhqk,bkr->bqhr', p, kc)
        else:
            n_past = past_ckv.shape[1]
            sp = (jnp.einsum('bqhr,bkr->bhqk', ql, past_ckv)
                  + jnp.einsum('bqhd,bkd->bhqk', qp, past_kpe)).astype(F32) * MLA_SCALE
            p = jax.nn.softmax(jnp.concatenate([sp, s], axis=-1), axis=-1).astype(ckv.dtype)
            o = (jnp.einsum('bhqk,bkr->bqhr', p[..., :n_past], past_ckv)
                 + jnp.einsum('bhqk,bkr->bqhr', p[..., n_past:], kc))
        outs.append(o)
    return jnp.concatenate(outs, axis=1)

def mixer_mla(h, pos0, past_ckv, past_kpe, P):
    bsz, L = h.shape[:2]
    pos = (pos0 + jnp.arange(L)).astype(F32)
    cq = rmsnorm(h @ P['mla_w_dq'], P['mla_g_q'])
    q = (cq @ P['mla_w_uq']).reshape(bsz, L, MLA_HEADS, MLA_NOPE + MLA_ROPE)
    q_nope, q_pe = q[..., :MLA_NOPE], rope(q[..., MLA_NOPE:], pos)
    kv = h @ P['mla_w_dkv']
    ckv = rmsnorm(kv[..., :MLA_KV_RANK], P['mla_g_kv'])
    kpe = rope(kv[:, :, None, MLA_KV_RANK:], pos)[:, :, 0]
    q_lat = jnp.einsum('blhd,rhd->blhr', q_nope, P['mla_w_uk'])
    o_lat = mla_attention(q_lat, q_pe, ckv, kpe, past_ckv, past_kpe)
    o = jnp.einsum('blhr,rhv->blhv', o_lat, P['mla_w_uv']).reshape(bsz, L, MLA_HEADS * MLA_V)
    return o @ P['mla_w_o'], ckv, kpe

def trunk(x, c, pos0, hg_s, ssm_s, conv_s, past_ckv, past_kpe, P):
    cs = jax.nn.silu(c)
    for layer in range(DEPTH):
        mod = (cs @ P['ada_w'][layer] + P['ada_b'][layer]).reshape(-1, N_SUB, 3, D_MODEL)
        h = modulate(x, P['norm_pre'][layer, 0], mod[:, 0, 0], mod[:, 0, 1])
        y = swiglu(h, P['ffn_wg'][layer, 0], P['ffn_wu'][layer, 0], P['ffn_wd'][layer, 0])
        x = gated_residual(x, y, P['norm_post'][layer, 0], mod[:, 0, 2], MACARON_W)
        h = modulate(x, P['norm_pre'][layer, 1], mod[:, 1, 0], mod[:, 1, 1])
        if layer % 2 == 0:
            y, hg_s, ssm_s, conv_s = mixer_ab(h, layer, hg_s, ssm_s, conv_s, P)
        else:
            y, ckv, kpe = mixer_mla(h, pos0, past_ckv, past_kpe, P)
        x = gated_residual(x, y, P['norm_post'][layer, 1], mod[:, 1, 2], 1.0)
        h = modulate(x, P['norm_pre'][layer, 2], mod[:, 2, 0], mod[:, 2, 1])
        y = swiglu(h, P['ffn_wg'][layer, 1], P['ffn_wu'][layer, 1], P['ffn_wd'][layer, 1])
        x = gated_residual(x, y, P['norm_post'][layer, 2], mod[:, 2, 2], MACARON_W)
    return x, hg_s, ssm_s, conv_s, ckv, kpe

def setup_inputs(seed: int = 0) -> dict:
    key = jax.random.key(seed)
    ks = iter(jax.random.split(key, 48))
    nrm = lambda shape, s=1.0: s * jax.random.normal(next(ks), shape, F32)
    n_pages = PAST_LEN // PAGE_SIZE
    n_used = DEC_BATCH * n_pages
    n_phys = n_used + max(1, n_used // 4)
    page_table = jax.random.permutation(next(ks), n_phys)[:n_used].reshape(DEC_BATCH, n_pages).astype(jnp.int32)
    dt0 = jnp.exp(jax.random.uniform(next(ks), (SSM_HEADS,), F32, math.log(1e-3), math.log(1e-1)))
    dt_bias = dt0 + jnp.log(-jnp.expm1(-dt0))
    a_log = jnp.log(jax.random.uniform(next(ks), (SSM_HEADS,), F32, 1.0, 16.0))
    d = D_MODEL
    return {
        'x_prompt': nrm((BATCH, SEQ, d)),
        'x_sample': nrm((DEC_BATCH, DEC_SEQ, d)),
        'c_prompt': nrm((BATCH, d)),
        'c_sample': nrm((DEC_BATCH, d)),
        'state_hgrn': nrm((DEC_BATCH, HG_HEADS, HG_KEY, HG_VAL), 0.5),
        'state_ssm': nrm((DEC_BATCH, SSM_HEADS, SSM_STATE, SSM_HEAD_DIM), 0.5),
        'state_conv': nrm((DEC_BATCH, SSM_CONV - 1, SSM_CONV_CH)),
        'cache_ckv': nrm((n_phys, PAGE_SIZE, MLA_KV_RANK)),
        'cache_kpe': nrm((n_phys, PAGE_SIZE, MLA_ROPE)),
        'page_table': page_table,
        'ada_w': nrm((DEPTH, d, N_SUB * 3 * d), 0.5 * d ** -0.5),
        'ada_b': nrm((DEPTH, N_SUB * 3 * d), 0.01),
        'norm_pre': 1.0 + nrm((DEPTH, N_SUB, d), 0.05),
        'norm_post': 1.0 + nrm((DEPTH, N_SUB, d), 0.05),
        'ffn_wg': nrm((DEPTH, 2, d, D_FF), d ** -0.5),
        'ffn_wu': nrm((DEPTH, 2, d, D_FF), d ** -0.5),
        'ffn_wd': nrm((DEPTH, 2, D_FF, d), D_FF ** -0.5),
        'w_in_ab': nrm((d, AB_IN), d ** -0.5),
        'w_out_ab': nrm((AB_OUT, d), AB_OUT ** -0.5),
        'hg_lb_logits': nrm((DEPTH + 1, HG_HEADS * HG_KEY), 0.1),
        'hg_norm': 1.0 + nrm((HG_WIDTH,), 0.05),
        'ssm_conv_w': nrm((SSM_CONV, SSM_CONV_CH), SSM_CONV ** -0.5),
        'ssm_conv_b': nrm((SSM_CONV_CH,), 0.01),
        'ssm_dt_bias': dt_bias,
        'ssm_a_log': a_log,
        'ssm_d': 1.0 + nrm((SSM_HEADS,), 0.1),
        'ssm_norm': 1.0 + nrm((SSM_INNER,), 0.05),
        'mla_w_dq': nrm((d, MLA_Q_RANK), d ** -0.5),
        'mla_g_q': 1.0 + nrm((MLA_Q_RANK,), 0.05),
        'mla_w_uq': nrm((MLA_Q_RANK, MLA_HEADS * (MLA_NOPE + MLA_ROPE)), MLA_Q_RANK ** -0.5),
        'mla_w_dkv': nrm((d, MLA_KV_RANK + MLA_ROPE), d ** -0.5),
        'mla_g_kv': 1.0 + nrm((MLA_KV_RANK,), 0.05),
        'mla_w_uk': nrm((MLA_KV_RANK, MLA_HEADS, MLA_NOPE), MLA_KV_RANK ** -0.5),
        'mla_w_uv': nrm((MLA_KV_RANK, MLA_HEADS, MLA_V), MLA_KV_RANK ** -0.5),
        'mla_w_o': nrm((MLA_HEADS * MLA_V, d), (MLA_HEADS * MLA_V) ** -0.5),
    }

def reference(x_prompt, x_sample, c_prompt, c_sample, state_hgrn, state_ssm, state_conv,
              cache_ckv, cache_kpe, page_table, ada_w, ada_b, norm_pre, norm_post,
              ffn_wg, ffn_wu, ffn_wd, w_in_ab, w_out_ab, hg_lb_logits, hg_norm,
              ssm_conv_w, ssm_conv_b, ssm_dt_bias, ssm_a_log, ssm_d, ssm_norm,
              mla_w_dq, mla_g_q, mla_w_uq, mla_w_dkv, mla_g_kv, mla_w_uk, mla_w_uv, mla_w_o):
    P = dict(ada_w=ada_w, ada_b=ada_b, norm_pre=norm_pre, norm_post=norm_post,
             ffn_wg=ffn_wg, ffn_wu=ffn_wu, ffn_wd=ffn_wd, w_in_ab=w_in_ab, w_out_ab=w_out_ab,
             hg_lb_logits=hg_lb_logits, hg_norm=hg_norm, ssm_conv_w=ssm_conv_w, ssm_conv_b=ssm_conv_b,
             ssm_dt_bias=ssm_dt_bias, ssm_a_log=ssm_a_log, ssm_d=ssm_d, ssm_norm=ssm_norm,
             mla_w_dq=mla_w_dq, mla_g_q=mla_g_q, mla_w_uq=mla_w_uq, mla_w_dkv=mla_w_dkv,
             mla_g_kv=mla_g_kv, mla_w_uk=mla_w_uk, mla_w_uv=mla_w_uv, mla_w_o=mla_w_o)
    bp = x_prompt.shape[0]
    hg0 = jnp.zeros((bp, HG_HEADS, HG_KEY, HG_VAL), state_hgrn.dtype)
    ssm0 = jnp.zeros((bp, SSM_HEADS, SSM_STATE, SSM_HEAD_DIM), state_ssm.dtype)
    conv0 = jnp.zeros((bp, SSM_CONV - 1, SSM_CONV_CH), x_prompt.dtype)
    y_prompt, hg_p, ssm_p, conv_p, ckv_p, kpe_p = trunk(x_prompt, c_prompt, 0, hg0, ssm0, conv0, None, None, P)
    db = x_sample.shape[0]
    past_ckv = cache_ckv[page_table].reshape(db, -1, MLA_KV_RANK)
    past_kpe = cache_kpe[page_table].reshape(db, -1, MLA_ROPE)
    y_sample, hg_s, ssm_s, conv_s, ckv_s, kpe_s = trunk(x_sample, c_sample, past_ckv.shape[1], state_hgrn,
                                                        state_ssm, state_conv, past_ckv, past_kpe, P)
    return (y_prompt, y_sample, hg_p, hg_s, ssm_p, ssm_s, conv_p, conv_s, ckv_p, ckv_s, kpe_p, kpe_s)


_drawn_inputs = setup_inputs


def setup_inputs(seed=0):
    import zlib

    import numpy as np

    out = dict(_drawn_inputs(seed))
    spreads = {}
    factors = {'hg_norm': 6.598, 'ssm_conv_b': 3.439, 'ssm_d': 3.033, 'ssm_norm': 4.385, 'mla_g_q': 4.029}
    for name, (base, spread) in spreads.items():
        noise = np.random.default_rng([zlib.crc32(name.encode()), seed]).standard_normal(out[name].shape)
        drawn = base * np.exp(spread * noise) if base else spread * noise
        out[name] = __import__('jax').numpy.asarray(drawn.astype(out[name].dtype))
    for name, factor in factors.items():
        out[name] = (out[name] * factor).astype(out[name].dtype)
    return out
```

```python
from contextlib import ExitStack

import numpy as np

import concourse.bass as bass
from concourse import mybir

F32 = mybir.dt.float32
I32 = mybir.dt.int32
ALU = mybir.AluOpType
ACT = mybir.ActivationFunctionType
AX_X = mybir.AxisListType.X

P = 128
D = 1024
DC = D // P
NP_ = 512
NB = 8
T = NP_ + NB
HT = T // 2
FC = 2816 // P
NSEQ = 1 + NB
NMOD = 3 * DC
EPS = 1e-6
CH = 128
NCH = NP_ // CH
LEVELS = (64, 32, 16, 8, 4, 2, 1)
HG = 8
SG_ = 4
GH = 4
HD = 64
MH = 16
RC = 2
ROPE = 64
PAGE = 128
NPAGE = 16
PAST = PAGE * NPAGE
SCALE = float((128 + 64) ** -0.5)
NEG = -1e30

_COLS = {}
_at = 0
for _name, _n in (("ident", P), ("ones", P), ("reset", NP_), ("sel", NB * P), ("sel16", 16 * P), ("causal", P),
                  ("neg", P), ("cos", T), ("sin", T), ("perm", P), ("own", NB * NB)):
    _COLS[_name] = (_at, _at + _n)
    _at += _n
N_CONST = _at


def constants():
    t = np.zeros((P, N_CONST), np.float32)

    def put(name, a):
        a0, a1 = _COLS[name]
        t[:a.shape[0], a0:a1] = a.reshape(a.shape[0], a1 - a0)

    r = np.arange(P)
    put("ident", np.eye(P))
    put("ones", np.ones((P, P)))
    put("reset", np.tile((np.arange(NP_) % CH != 0), (P, 1)))
    sel = np.zeros((NB, NB, P))
    sel[np.arange(NB), np.arange(NB)] = 1
    put("sel", sel)
    sel16 = np.zeros((16, 16, P))
    sel16[np.arange(16), np.arange(16)] = 1
    put("sel16", sel16)
    put("causal", (r[:, None] <= r[None, :]).astype(np.float32))
    put("neg", np.where(r[None, :] <= r[:, None], 0.0, NEG))
    half = ROPE // 2
    inv = (10000.0 ** (-np.arange(half, dtype=np.float32) / half)).astype(np.float32)
    pos = np.concatenate([np.arange(NP_), np.full(NB, PAST)]).astype(np.float32)
    ang = (inv[:, None] * pos[None]).astype(np.float32)
    put("cos", np.tile(np.cos(ang), (4, 1)))
    put("sin", np.concatenate([-np.sin(ang), np.sin(ang)] * 2))
    perm = np.zeros((P, P))
    perm[(r // ROPE) * ROPE + (r + half) % ROPE, r] = 1
    put("perm", perm)
    own = np.full((16, NB, NB), NEG)
    own[:, np.arange(NB), np.arange(NB)] = 0
    put("own", own)
    masks = np.zeros((P, len(LEVELS), P), np.int32)
    s, u = r[:, None], r[None, :]
    for n, m in enumerate(LEVELS):
        masks[:, n] = (s // (2 * m) == u // (2 * m)) & ((s // m) % 2 == 0) & ((u // m) % 2 == 1)
    return t, masks


WS = 24
LOADS = {}


def _plan():
    n = 0
    for layer in range(2):
        for sub in range(3):
            s = layer * 3 + sub
            if sub != 1:
                LOADS["up", s] = n
                n += FC
            elif layer == 0:
                LOADS["hgrn"] = n
                n += 2 * HG
                LOADS["ssm"] = n
                n += 2 * SG_
            else:
                LOADS["latent"] = n
                n += 3
                LOADS["pairs"] = n
                n += MH // 2
                LOADS["uv"] = n
                n += 2
            LOADS["down", s] = n
            n += DC
    return n


_plan()


def build_program(nc, A, O):
    ctx = ExitStack()
    with ctx:
        def sb(name, shape, dt=F32):
            return ctx.enter_context(nc.sbuf_tensor(name, shape, dt))

        def sem(name):
            return ctx.enter_context(nc.semaphore(name))

        PS = ctx.enter_context(nc.psum_tensor("PS", [P, 8, 512], F32))

        CT = sb("consts", [P, N_CONST])
        MSK = sb("level_masks", [P, len(LEVELS), P], I32)
        X = sb("residual", [P, DC, T])
        H = sb("hidden", [P, DC, T])
        Y = sb("sub_out", [P, DC, T])
        R = sb("inv_rms", [P, T])
        MOD = sb("modulation", [P, NMOD, NSEQ])
        AM = sb("pre_scale", [P, DC, NSEQ])
        GM = sb("post_scale", [P, DC, NSEQ])
        CS = sb("silu_c", [P, DC, NSEQ])
        CE = sb("exp_c", [P, DC, NSEQ])
        W = sb("weight_ring", [P, 2, WS * P])
        AD = sb("ada_ring", [P, 4, DC * P])
        ADB = sb("ada_bias", [P, 6, NMOD])
        NPRE = sb("norm_pre", [P, 6, DC])
        NPOST = sb("norm_post", [P, 6, DC])
        BIG = sb("arena", [P, 22400])

        def const(name, rows=P):
            a0, a1 = _COLS[name]
            return CT[0:rows, a0:a1]

        IDENT, ONES = const("ident"), const("ones")

        class Arena:
            def __init__(self, t, start=0):
                self.t, self.at = t, start

            def take(self, *shape, rows=P):
                n = int(np.prod(shape))
                ap = self.t[0:rows, self.at:self.at + n]
                self.at += n
                assert self.at <= self.t.shape[1], self.at
                if len(shape) == 1:
                    return ap
                names = "abcd"[:len(shape)]
                return ap.rearrange(f"p ({' '.join(names)}) -> p {' '.join(names)}",
                                    **{k: v for k, v in zip(names, shape)})

        ar = Arena(BIG)
        GU = ar.take(FC, T)
        SILU = ar.take(2, T)
        ar = Arena(BIG)
        OC = ar.take(16, T)
        mix0 = ar.at
        LB = ar.take(3, HG)
        LMX = ar.take(HG)
        HVEC = ar.take(3, HG)
        HP = ar.take(3)
        E1, E2, E3 = ar.take(T), ar.take(T), ar.take(T)
        QS, KK, FG, GS = ar.take(T), ar.take(T), ar.take(T), ar.take(T)
        E2R = ar.take(T)
        BB = ar.take(NP_)
        KD = ar.take(NP_)
        KDT = ar.take(NCH, P)
        EB = ar.take(NP_)
        QI = ar.take(NP_)
        VV = ar.take(NCH, P)
        VS = ar.take(P, rows=NB)
        AT = ar.take(NCH, P)
        ST = ar.take(NCH, P)
        SQO = ar.take(T)
        RH = ar.take(T)
        yar = Arena(Y[:].rearrange("p a b -> p (a b)"))
        DL = yar.take(len(LEVELS), NP_)
        S0 = ar.take(NB, P)
        VK = ar.take(NB, P)
        ar = Arena(BIG, mix0)
        CW = ar.take(SG_, 4, 5)
        CWG = ar.take(4, 5)
        DSK = ar.take(SG_, 2)
        SNW = ar.take(SG_, 2)
        DSN = ar.take(4)
        DTW = ar.take(DC, 16)
        SMS = ar.take(4, rows=16)
        DT = ar.take(T, rows=16)
        LA = ar.take(T, rows=16)
        DTT = ar.take(NCH, 16)
        BT = ar.take(NCH, 16)
        DTS = ar.take(16, rows=NB)
        DTG = ar.take(NCH, GH)
        BTG = ar.take(NCH, GH)
        DTSG = ar.take(GH, rows=NB)
        SELG = ar.take(GH, P, rows=16)
        XR = ar.take(4, T)
        DTV, DTE = XR[0:16, 0, :], XR[0:16, 1, :]
        CV = ar.take(4, T)
        STC = ar.take(4, 3, NB)
        GZ = ar.take(2, T)
        XD = ar.take(NCH, GH, HD)
        XW = ar.take(NCH, GH, HD)
        XDS = ar.take(GH * HD, rows=NB)
        BTK = ar.take(NCH, P)
        CBM = ar.take(NCH, P)
        WL = ar.take(GH, NCH)
        EL = ar.take(GH, NCH)
        EA = ar.take(GH, NB)
        SS = ar.take(NCH, GH, HD)
        ssm_e = ar.at
        EV = ar.take(4, T)
        SEG = EV[:, :, 0:NP_]
        yar = Arena(Y[:].rearrange("p a b -> p (a b)"))
        SM0 = yar.take(NB, GH, HD)
        CEX = yar.take(GH, NP_)
        YV = GZ
        SUU = CV[:, 0:2, :]
        ar = Arena(BIG, mix0)
        GQ = ar.take(4)
        GKV = ar.take(RC)
        CKV = ar.take(RC, T)
        KPE = ar.take(T)
        QL = ar.take(RC, MH, NB)
        QPS = ar.take(MH, NB, rows=ROPE)
        OL = ar.take(RC, MH, NB)
        CKVS = ar.take(RC, P, rows=NB)
        mla0 = ar.at
        CQ = Y[:, 0:4, :]
        TMP = ar.take(T)
        QR = ar.take(T)
        QP = ar.take(T)
        QN = ar.take(2, T)
        KN = ar.take(2, NP_)
        VT = ar.take(NCH, 2, P)
        PR = ar.take(2, 4, NP_)
        PTR = ar.take(4, NP_)
        SMX = ar.take(2, 4)
        SNB = ar.take(2, 4)
        SRS = ar.take(2, 4)
        SRI = ar.take(2, 4)
        ar = Arena(BIG, mla0)
        KT = ar.take(RC, PAST)
        KN_ = ar.take(NPAGE, RC * P)
        QLB = ar.take(RC, MH)
        QPB = ar.take(MH, rows=ROPE)
        PTD = ar.take(NPAGE + 1, MH)
        DST = ar.take(8, rows=MH)
        har = Arena(H[:].rearrange("p a b -> p (a b)"))
        KPT = har.take(PAST, rows=ROPE)
        PD = har.take(PAST + NB, rows=MH)
        TABLE = sb("page_table", [1, NB * NPAGE], I32)

        stage_done = sem("stage_done")
        const_in = sem("const_in")
        wait_passed = sem("wait_passed")
        w_arrived = [sem("w_arrived0"), sem("w_arrived1")]
        w_free = sem("w_free")
        ada_arrived = [sem(f"ada_arrived{c}") for c in range(4)]
        mod_ready = sem("mod_ready")
        mod_taken = sem("mod_taken")
        pre_sq = sem("pre_sq")
        sums_ready = sem("sums_ready")
        var_ready = sem("var_ready")
        root_ready = sem("root_ready")
        xr_ready = sem("xr_ready")
        hid_ready = sem("hid_ready")
        gu_ready = sem("gu_ready")
        silu_ready = sem("silu_ready")
        gu_taken = sem("gu_taken")
        y_ready = sem("y_ready")
        y_taken = sem("y_taken")
        out_stored = sem("out_stored")
        c_exp = sem("c_exp")
        N_FENCES = 37
        vec_in = sem("vec_in")
        lb_exp = sem("lb_exp")
        h_proj = sem("h_proj")
        h_exp = sem("h_exp")
        h_v = sem("h_v")
        h_f = sem("h_f")
        h_lf = sem("h_lf")
        h_d = sem("h_d")
        h_ex = sem("h_ex")
        h_qk = sem("h_qk")
        h_kd = sem("h_kd")
        h_kt = sem("h_kt")
        h_kdt = sem("h_kdt")
        h_vb = sem("h_vb")
        h_vk = sem("h_vk")
        h_u = sem("h_u")
        h_s = sem("h_s")
        h_p = sem("h_p")
        h_ptk = sem("h_ptk")
        h_att = sem("h_att")
        h_o = sem("h_o")
        h_os = sem("h_os")
        h_sq = sem("h_sq")
        h_ss = sem("h_ss")
        h_var = sem("h_var")
        h_r = sem("h_r")
        h_done = sem("h_done")
        s_loaded = sem("s_loaded")
        s_new = sem("s_new")
        s_stored = sem("s_stored")
        g_in = sem("g_in")
        d_step = sem("d_step")
        d_act = sem("d_act")
        d_pe = sem("d_pe")
        g_proj = sem("g_proj")
        g_raw = sem("g_raw")
        g_conv = sem("g_conv")
        g_cexp = sem("g_cexp")
        g_zexp = sem("g_zexp")
        g_x = sem("g_x")
        g_z = sem("g_z")
        g_sel = sem("g_sel")
        g_tr = sem("g_tr")
        g_btk = sem("g_btk")
        g_xt = sem("g_xt")
        g_bc = sem("g_bc")
        g_cb = sem("g_cb")
        g_cbm = sem("g_cbm")
        g_wl = sem("g_wl")
        g_wle = sem("g_wle")
        g_seg = sem("g_seg")
        g_sege = sem("g_sege")
        g_bcx = sem("g_bcx")
        g_m = sem("g_m")
        g_xw = sem("g_xw")
        g_u = sem("g_u")
        g_s = sem("g_s")
        g_bcfree = sem("g_bcfree")
        g_xb = sem("g_xb")
        g_uu = sem("g_uu")
        g_y = sem("g_y")
        g_ys = sem("g_ys")
        g_yv = sem("g_yv")
        g_sq = sem("g_sq")
        g_ss = sem("g_ss")
        g_var = sem("g_var")
        g_r = sem("g_r")
        g_done = sem("g_done")
        st_in = sem("st_in")
        st_out = sem("st_out")
        st_ok = sem("st_ok")
        m_proj = sem("m_proj")
        m_copy = sem("m_copy")
        m_ss = sem("m_ss")
        m_var = sem("m_var")
        m_root = sem("m_root")
        m_norm = sem("m_norm")
        m_perm = sem("m_perm")
        m_cks = sem("m_cks")
        p_q = sem("p_q")
        p_qc = sem("p_qc")
        p_perm = sem("p_perm")
        p_qp = sem("p_qp")
        p_ql = sem("p_ql")
        p_qlt = sem("p_qlt")
        p_v = sem("p_v")
        p_vc = sem("p_vc")
        p_k = sem("p_k")
        p_kc = sem("p_kc")
        p_sc = sem("p_sc")
        p_mx = sem("p_mx")
        p_pr = sem("p_pr")
        p_pn = sem("p_pn")
        p_pt = sem("p_pt")
        p_ptc = sem("p_ptc")
        p_o = sem("p_o")
        p_oc = sem("p_oc")
        k_in = sem("k_in")
        k_free = sem("k_free")
        b_q = sem("b_q")
        b_sc = sem("b_sc")
        b_mx = sem("b_mx")
        b_ex = sem("b_ex")
        b_pn = sem("b_pn")
        b_pt = sem("b_pt")
        b_ptc = sem("b_ptc")
        b_o = sem("b_o")
        b_oc = sem("b_oc")
        u_o = sem("u_o")

        block = ctx.enter_context(nc.Block())

        def fencer(eng):
            state = [0]

            def fence():
                state[0] += 1
                eng.drain().then_inc(stage_done, 1)
                eng.wait_ge(stage_done, 3 * state[0])
            return fence

        def pair(bank, cols=HT, rows=P):
            return PS[0:rows, bank:bank + 2, 0:cols]

        def two(ap):
            return ap.rearrange("p (a b) -> p a b", a=2)

        def apart(eng):
            eng.sem_inc(wait_passed, 1)

        def w_ready(pe, base, i, jj):
            slot = (base + jj) % 2
            pe.wait_ge(w_arrived[slot], i * 16 + 16 * ((base + jj) // 2 + 1))
            return slot

        @block.sync
        def _(sp):
            sp.dma_start(CT[:, :], A["const"]).then_inc(const_in, 16)
            sp.dma_start(MSK[:, :, :], A["masks"]).then_inc(const_in, 16)
            sp.dma_start(X[:, :, :], A["x"]).then_inc(const_in, 16)
            sp.dma_start(CS[:, :, :], A["c"]).then_inc(const_in, 16)
            sp.dma_start(ADB[:, :, :], A["ada_b"]).then_inc(const_in, 16)
            sp.dma_start(NPRE[:, :, :], A["norm_pre"]).then_inc(const_in, 16)
            sp.dma_start(NPOST[:, :, :], A["norm_post"]).then_inc(const_in, 16)
            sp.dma_start(TABLE[:, :], A["page_table"]).then_inc(const_in, 16)

            def load(base, i, jj, tiles, src):
                slot = (base + jj) % 2
                sp.wait_ge(w_free, i * 2 + (base + jj + 1))
                sp.dma_start(W[:, slot, 0:tiles * P], src).then_inc(w_arrived[slot], 16)

            def ffn_up(s, f):
                base = LOADS["up", s]
                with sp.Fori(0, FC // 2) as i:
                    for jj in range(2):
                        load(base, i, jj, 2 * DC, A["ffn_gu"][i * 2 + (f * FC + jj)])

            def down(s, src, tiles, first):
                base = LOADS["down", s]
                with sp.Fori(0, DC // 2) as i:
                    for jj in range(2):
                        load(base, i, jj, tiles, src[i * 2 + (first + jj)])

            for layer in range(2):
                ffn_up(layer * 3, layer * 2)
                down(layer * 3, A["ffn_wd"], FC, layer * 2 * DC)
                if layer == 0:
                    with sp.Fori(0, HG) as h:
                        for jj in range(2):
                            load(LOADS["hgrn"], h, jj, 16, A["w_hgrn"][h * 2 + jj])
                    with sp.Fori(0, SG_) as g:
                        for jj in range(2):
                            load(LOADS["ssm"], g, jj, 24, A["w_ssm"][g * 2 + jj])
                    down(1, A["w_out_ab"], 16, 0)
                else:
                    base = LOADS["latent"]
                    load(base, 0, 0, 16, A["mla_dq"][0])
                    load(base, 0, 1, 16, A["mla_dq"][1])
                    load(base, 0, 2, 24, A["mla_dkv"])
                    with sp.Fori(0, MH // 4) as i:
                        for jj in range(2):
                            load(LOADS["pairs"], i, jj, 24, A["mla_pairs"][i * 2 + jj])
                    with sp.Fori(0, NB) as b:
                        sp.wait_ge(k_free, b + 1)
                        for pg in range(NPAGE):
                            page = sp.value_load(TABLE[0:1, bass.ds(b * NPAGE + pg, 1)], min_val=0,
                                                 max_val=A["ckvT"].shape[0] - 1)
                            sp.dma_start(KT[:, :, pg * PAGE:(pg + 1) * PAGE], A["ckvT"][page]).then_inc(k_in, 16)
                            sp.dma_start(KN_[:, pg, :], A["ckv"][page]).then_inc(k_in, 16)
                            sp.dma_start(KPT[:, pg * PAGE:(pg + 1) * PAGE], A["kpeT"][page]).then_inc(k_in, 16)
                    load(LOADS["uv"], 0, 0, 16, A["mla_uv"][0])
                    load(LOADS["uv"], 0, 1, 16, A["mla_uv"][1])
                    down(4, A["mla_wo"], 16, 0)
                ffn_up(layer * 3 + 2, layer * 2 + 1)
                down(layer * 3 + 2, A["ffn_wd"], FC, (layer * 2 + 1) * DC)

        @block.gpsimd
        def _(pool):
            pool.sem_inc(s_stored, 1)
            pool.sem_inc(st_ok, 1)

            def ada(s):
                with pool.Fori(0, NMOD // 4) as i:
                    for c in range(4):
                        pool.wait_ge(mod_taken, i * 4 + (s * NMOD + c + 1))
                        apart(pool)
                        pool.dma_start(AD[:, c, :], A["ada_w"][i * 4 + (s * NMOD + c)]).then_inc(ada_arrived[c], 16)

            ada(0)
            ada(1)
            pool.wait_ge(stage_done, 3 * 5)
            pool.dma_start(LB, A["lb_logits"]).then_inc(vec_in, 16)
            pool.dma_start(HVEC[:, 2, :], A["hg_norm"]).then_inc(vec_in, 16)
            with pool.Fori(0, HG) as h:
                pool.wait_ge(h_done, h + 1)
                apart(pool)
                pool.dma_start(S0, A["state_hgrn"][h]).then_inc(s_loaded, 16)
                pool.wait_ge(h_s, h + 1)
                apart(pool)
                pool.dma_start(O["hgrn_prompt"][h], ST[:, NCH - 1, :]).then_inc(out_stored, 16)
                pool.wait_ge(s_new, h + 1)
                apart(pool)
                pool.dma_start(O["hgrn_sample"][h], S0).then_inc(out_stored, 16)
                pool.wait_ge(out_stored, h * 32 + 32)
                pool.sem_inc(s_stored, 1)
            pool.wait_ge(stage_done, 3 * 9)
            for dst, name in ((CW, "conv_w"), (DSK, "ssm_d"), (SNW, "ssm_norm"), (DTW, "w_dt"), (SMS[:, 0:2], "ssm_small")):
                pool.dma_start(dst, A[name]).then_inc(g_in, 16)
            with pool.Fori(0, SG_) as g:
                pool.wait_ge(g_done, g + 1)
                apart(pool)
                pool.dma_start(STC, A["state_conv"][g]).then_inc(st_in, 16)
                pool.dma_start(SM0, A["state_ssm"][g]).then_inc(st_in, 16)
                pool.wait_ge(st_in, g * 32 + 32)
                pool.wait_ge(g_raw, g * 4 + 4)
                apart(pool)
                pool.dma_start(O["conv_prompt"][g], XR[:, :, NP_ - 3:NP_]).then_inc(st_out, 16)
                pool.dma_start(O["conv_sample"][g, :, :, 0:2, :], STC[:, :, 1:3, :]).then_inc(st_out, 16)
                pool.dma_start(O["conv_sample"][g, :, :, 2, :], XR[:, :, NP_:T]).then_inc(st_out, 16)
                pool.wait_ge(g_s, g + 1)
                apart(pool)
                pool.dma_start(O["ssm_prompt"][g], SS[:, NCH - 1]).then_inc(st_out, 16)
                pool.wait_ge(g_uu, g * 2 + 2)
                apart(pool)
                pool.dma_start(O["ssm_sample"][g], SM0).then_inc(st_out, 16)
                pool.wait_ge(st_out, g * 80 + 80)
                pool.sem_inc(st_ok, 1)
            ada(2)
            ada(3)
            pool.wait_ge(stage_done, 3 * 24)
            pool.dma_start(GQ, A["mla_gq"]).then_inc(m_cks, 16)
            pool.dma_start(GKV, A["mla_gkv"]).then_inc(m_cks, 16)
            ada(4)
            pool.wait_ge(m_norm, 3)
            pool.dma_start(O["ckv"], CKV).then_inc(out_stored, 16)
            pool.dma_start(O["kpe"], KPE[0:ROPE, :]).then_inc(out_stored, 16)
            pool.wait_ge(out_stored, 32 * HG + 32)
            ada(5)
            pool.wait_ge(stage_done, 3 * N_FENCES)
            pool.dma_start(O["y"], X[:, :, :]).then_inc(out_stored, 16)
            pool.wait_ge(out_stored, 32 * HG + 48)

        @block.tensor
        def _(pe):
            fence = fencer(pe)
            pe.sem_inc(w_free, 2)

            def product(bank, weights, moving, rows=P):
                n = len(weights)
                for k in range(n):
                    for hf in range(2):
                        last = pe.matmul(PS[0:rows, bank + hf, 0:HT], weights[k], moving[k][:, hf * HT:(hf + 1) * HT],
                                         start=(k == 0), stop=(k == n - 1))
                return last

            def tiles(slot, first, n):
                return [W[:, slot, (first + k) * P:(first + k + 1) * P] for k in range(n)]

            def rows_of(buf, n):
                return [buf[:, k, :] for k in range(n)]

            def modulation(s):
                with pe.Fori(0, NMOD // 4) as i:
                    for c in range(4):
                        pe.wait_ge(ada_arrived[c], i * 16 + (16 * 6 * s + 16))
                        pe.wait_ge(mod_taken, i * 4 + (s * NMOD + c + 1))
                        for k in range(DC):
                            last = pe.matmul(PS[:, 4 + c, 0:NSEQ], AD[:, c, k * P:(k + 1) * P],
                                             CS[:, k, :], start=(k == 0), stop=(k == DC - 1))
                        last.then_inc(mod_ready, 1)
                fence()

            def pre_norm(s):
                pe.wait_ge(pre_sq, DC * (s + 1))
                product(0, [ONES] * DC, rows_of(Y, DC)).then_inc(sums_ready, 1)
                fence()

            def post_norm(s):
                product(0, [ONES] * DC, rows_of(H, DC)).then_inc(sums_ready, 1)
                fence()

            def ffn_up(s, n):
                base = LOADS["up", s]
                with pe.Fori(0, FC // 2) as i:
                    for jj in range(2):
                        slot = w_ready(pe, base, i, jj)
                        pe.wait_ge(gu_taken, i * 2 + (n * FC + jj + 1))
                        product(4 * jj, tiles(slot, 0, DC), rows_of(H, DC))
                        last = product(4 * jj + 2, tiles(slot, DC, DC), rows_of(H, DC))
                        last.then_inc(gu_ready, 1)
                        pe.wait_ge(gu_ready, i * 2 + (n * FC + jj + 1))
                        pe.sem_inc(w_free, 1)
                fence()

            def down(s, src, nk):
                base = LOADS["down", s]
                with pe.Fori(0, DC // 2) as i:
                    for jj in range(2):
                        slot = w_ready(pe, base, i, jj)
                        pe.wait_ge(y_taken, i * 2 + (s * DC + jj + 1))
                        product(2 * jj, tiles(slot, 0, nk), rows_of(src, nk)).then_inc(y_ready, 1)
                        pe.wait_ge(y_ready, i * 2 + (s * DC + jj + 1))
                        pe.sem_inc(w_free, 1)
                fence()

            def hgrn():
                fence()
                with pe.Fori(0, HG) as h:
                    pe.wait_ge(h_done, h + 1)
                    slot = w_ready(pe, LOADS["hgrn"], h, 0)
                    product(0, tiles(slot, 0, DC), rows_of(H, DC)).then_inc(h_proj, 1)
                    product(2, tiles(slot, DC, DC), rows_of(H, DC)).then_inc(h_proj, 1)
                    pe.wait_ge(h_proj, h * 4 + 2)
                    pe.sem_inc(w_free, 1)
                    slot = w_ready(pe, LOADS["hgrn"], h, 1)
                    product(4, tiles(slot, DC, DC), rows_of(H, DC)).then_inc(h_proj, 1)
                    wi = tiles(slot, 0, DC)
                    for c in range(NCH):
                        for k in range(DC):
                            pe.matmul(PS[:, 6, c * P:(c + 1) * P], H[:, k, c * CH:(c + 1) * CH], wi[k],
                                      start=(k == 0), stop=(k == DC - 1))
                    for k in range(DC):
                        last = pe.matmul(PS[0:NB, 7, 0:P], H[:, k, NP_:T], wi[k], start=(k == 0), stop=(k == DC - 1))
                    last.then_inc(h_proj, 1)
                    pe.wait_ge(h_proj, h * 4 + 4)
                    pe.sem_inc(w_free, 1)
                    pe.wait_ge(h_v, h + 1)
                    for b in range(NB):
                        last = pe.matmul(PS[:, 6 + b // 4, (b % 4) * P:(b % 4 + 1) * P],
                                         const("sel", NB)[:, b * P:(b + 1) * P], VS, start=True, stop=True)
                    last.then_inc(h_vb, 1)
                    pe.wait_ge(h_kd, h + 1)
                    for c in range(NCH):
                        last = pe.transpose(PS[:, 4, c * P:(c + 1) * P], KD[:, c * CH:(c + 1) * CH], IDENT)
                    last.then_inc(h_kt, 1)
                    for n in range(1 + len(LEVELS)):
                        if n >= 1:
                            pe.wait_ge(h_qk, h * 7 + n)
                        pe.wait_ge(h_ptk, h * 8 + (n + 1))
                        for c in range(NCH):
                            cc = slice(c * CH, (c + 1) * CH)
                            lhs, rhs = (KK[:, cc], QS[:, cc]) if n == 0 else (DL[:, n - 1, cc], DL[:, n - 1, cc])
                            last = pe.matmul(PS[:, n % 4, cc], lhs, rhs, start=True, stop=True)
                        last.then_inc(h_p, 1)
                        if n == 0:
                            pe.wait_ge(h_kdt, h + 1)
                            for c in range(NCH):
                                last = pe.matmul(PS[:, 5, c * P:(c + 1) * P], KDT[:, c, :], VV[:, c, :],
                                                 start=True, stop=True)
                            last.then_inc(h_u, 1)
                    pe.wait_ge(h_vk, h + 1)
                    pe.wait_ge(h_att, h + 1)
                    pe.wait_ge(h_s, h + 1)
                    for c in range(NCH):
                        cc = slice(c * CH, (c + 1) * CH)
                        last = pe.matmul(PS[:, 6, cc], VV[:, c, :], AT[:, c, :], start=True, stop=(c == 0))
                        if c:
                            last = pe.matmul(PS[:, 6, cc], ST[:, c - 1, :], QI[:, cc], start=False, stop=True)
                    last.then_inc(h_o, 1)
                    pe.wait_ge(s_new, h + 1)
                    for b in range(NB):
                        last = pe.matmul(PS[:, 7, b:b + 1], S0[:, b, :], QS[:, NP_ + b:NP_ + b + 1],
                                         start=True, stop=True)
                    last.then_inc(h_o, 1)
                    pe.wait_ge(h_sq, h + 1)
                    product(0, [ONES], [SQO]).then_inc(h_ss, 1)
                fence()

            def ssm():
                fence()
                pe.wait_ge(g_in, 80)
                product(0, [DTW[:, k, :] for k in range(DC)], rows_of(H, DC), rows=16).then_inc(d_pe, 1)
                pe.wait_ge(d_step, 4)
                for c in range(NCH):
                    pe.transpose(PS[:, 2, c * 16:(c + 1) * 16], DT[:, c * CH:(c + 1) * CH], IDENT[0:16, 0:16])
                    pe.transpose(PS[:, 4, c * 16:(c + 1) * 16], LA[:, c * CH:(c + 1) * CH], IDENT[0:16, 0:16])
                pe.transpose(PS[0:NB, 3, 0:16], DT[:, NP_:T], IDENT[0:16, 0:16]).then_inc(d_pe, 1)
                fence()
                with pe.Fori(0, SG_) as g:
                    pe.wait_ge(g_done, g + 1)
                    slot = w_ready(pe, LOADS["ssm"], g, 0)
                    for c in range(3):
                        product(2 * c, tiles(slot, c * DC, DC), rows_of(H, DC)).then_inc(g_proj, 1)
                    pe.wait_ge(g_proj, g * 6 + 3)
                    pe.sem_inc(w_free, 1)
                    slot = w_ready(pe, LOADS["ssm"], g, 1)
                    product(6, tiles(slot, 0, DC), rows_of(H, DC)).then_inc(g_proj, 1)
                    for c in range(2):
                        pe.wait_ge(g_raw, g * 4 + (c + 1))
                        product(2 * c, tiles(slot, (c + 1) * DC, DC), rows_of(H, DC)).then_inc(g_proj, 1)
                    pe.wait_ge(g_proj, g * 6 + 6)
                    pe.sem_inc(w_free, 1)
                    pe.wait_ge(g_x, g + 1)
                    pe.wait_ge(g_raw, g * 4 + 4)
                    for c in range(NCH):
                        for x in range(2):
                            pe.transpose(PS[:, 4 + c // 2, (c % 2) * 256 + x * P:(c % 2) * 256 + (x + 1) * P],
                                         CV[:, x, c * CH:(c + 1) * CH], IDENT)
                        pe.transpose(PS[:, 6, c * P:(c + 1) * P], CV[:, 2, c * CH:(c + 1) * CH], IDENT)
                    for x in range(2):
                        pe.transpose(PS[0:NB, 7, x * P:(x + 1) * P], CV[:, x, NP_:T], IDENT)
                    pe.wait_ge(g_sel, g + 1)
                    for j in range(GH):
                        last = pe.matmul(PS[:, 7, 256 + j * NB:256 + (j + 1) * NB], SELG[:, j, :], LA[:, NP_:T],
                                         start=True, stop=True)
                    last.then_inc(g_tr, 1)
                    pe.wait_ge(g_z, g + 1)
                    for j in range(GH):
                        last = pe.matmul(PS[:, j, :], SELG[:, j, :], LA[:, 0:NP_], start=True, stop=True)
                    last.then_inc(g_bc, 1)
                    pe.wait_ge(g_btk, g + 1)
                    for c in range(NCH):
                        cc = slice(c * CH, (c + 1) * CH)
                        last = pe.matmul(PS[:, 6, cc], CV[:, 2, cc], CV[:, 3, cc], start=True, stop=True)
                    last.then_inc(g_cb, 1)
                    pe.wait_ge(g_xw, g + 1)
                    for c in range(NCH):
                        last = pe.matmul(PS[:, 4 + c // 2, (c % 2) * 256:(c % 2 + 1) * 256], BTK[:, c, :],
                                         XW[:, c].rearrange("p a b -> p (a b)"), start=True, stop=True)
                    last.then_inc(g_u, 1)
                    pe.wait_ge(g_bcfree, g + 1)
                    for b in range(NB):
                        last = pe.matmul(PS[:, b // 2, (b % 2) * 256:(b % 2 + 1) * 256],
                                         const("sel", NB)[:, b * P:(b + 1) * P], XDS, start=True, stop=True)
                    last.then_inc(g_xb, 1)
                    pe.wait_ge(g_m, g * 4 + 4)
                    pe.wait_ge(g_s, g + 1)
                    for j in range(GH):
                        lo = (j % 2) * HD
                        for c in range(NCH):
                            cc = slice(c * CH, (c + 1) * CH)
                            out = PS[lo:lo + HD, 6 + j // 2, cc]
                            last = pe.matmul(out, XD[:, c, j, :], SEG[:, j, cc], start=True, stop=(c == 0))
                            if c:
                                last = pe.matmul(out, SS[:, c - 1, j, :], CEX[:, j, cc], start=False, stop=True)
                    last.then_inc(g_y, 1)
                    pe.wait_ge(g_uu, g * 2 + 2)
                    for x in range(2):
                        for b in range(NB):
                            last = pe.matmul(PS[:, 4, x * NB + b:x * NB + b + 1],
                                             SM0[:, b, 2 * x:2 * x + 2, :].rearrange("p a b -> p (a b)"),
                                             CV[:, 3, NP_ + b:NP_ + b + 1], start=True, stop=True)
                    last.then_inc(g_y, 1)
                    pe.wait_ge(g_sq, g + 1)
                    product(0, [ONES] * 2, rows_of(SUU, 2)).then_inc(g_ss, 1)
                fence()

            def mla():
                base = LOADS["latent"]
                for c in range(4):
                    if c % 2 == 0:
                        slot = w_ready(pe, base, 0, c // 2)
                    product(2 * c, tiles(slot, (c % 2) * DC, DC), rows_of(H, DC)).then_inc(m_proj, 1)
                pe.wait_ge(m_proj, 4)
                pe.sem_inc(w_free, 2)
                slot = w_ready(pe, base, 0, 2)
                for c in range(3):
                    pe.wait_ge(m_copy, c + 2)
                    product(2 * (c + 1), tiles(slot, c * DC, DC), rows_of(H, DC)).then_inc(m_proj, 1)
                pe.wait_ge(m_proj, 7)
                pe.sem_inc(w_free, 1)
                product(0, [ONES] * 4, rows_of(Y[:, 4:8, :], 4)).then_inc(m_ss, 1)
                pe.wait_ge(m_copy, 7)
                pe.wait_ge(m_var, 1)
                product(0, [ONES] * 2, rows_of(QN, 2)).then_inc(m_ss, 1)
                product(2, [const("perm")], [QR]).then_inc(m_perm, 1)
                pe.wait_ge(m_norm, 2)
                for r in range(RC):
                    last = pe.transpose(PS[0:NB, 4, r * P:(r + 1) * P], CKV[:, r, NP_:T], IDENT)
                last.then_inc(m_perm, 1)
                fence()

                def head_pair(i, jj):
                    n = i * 2 + jj
                    slot = w_ready(pe, LOADS["pairs"], i, jj)
                    pe.wait_ge(p_oc, n * 2 + 2)
                    for c in range(3):
                        product(2 * c, tiles(slot, 4 * ((c + 2) % 3), 4), rows_of(CQ, 4)).then_inc(p_q, 1)
                    pe.wait_ge(p_qc, n * 3 + 3)
                    product(0, [const("perm")], [QR]).then_inc(p_perm, 1)
                    ukt = W[:, slot, 20 * P:24 * P].rearrange("p (a b) -> p a b", a=2)
                    for hh in range(2):
                        for r in range(RC):
                            last = pe.matmul(PS[:, 2, (hh * 2 + r) * NB:(hh * 2 + r + 1) * NB],
                                             ukt[:, hh, r * P:(r + 1) * P], QN[:, hh, NP_:T], start=True, stop=True)
                    last.then_inc(p_ql, 1)
                    uv = W[:, slot, 16 * P:20 * P].rearrange("p (a b) -> p a b", a=2)
                    for c in range(NCH):
                        for k in range(RC):
                            last = pe.matmul(PS[:, 6 + c // 2, (c % 2) * 256:(c % 2 + 1) * 256],
                                             CKV[:, k, c * CH:(c + 1) * CH], uv[:, k, :],
                                             start=(k == 0), stop=(k == RC - 1))
                    last.then_inc(p_v, 1)
                    uk = tiles(slot, 12, 4)
                    for hh in range(2):
                        for k in range(RC):
                            last = pe.matmul(PS[:, 4 + hh, :], uk[hh * 2 + k], CKV[:, k, 0:NP_],
                                             start=(k == 0), stop=(k == RC - 1))
                    last.then_inc(p_k, 1)
                    pe.wait_ge(p_k, n + 1)
                    pe.sem_inc(w_free, 1)
                    pe.wait_ge(p_kc, n + 1)
                    pe.wait_ge(p_qp, n + 1)
                    pe.wait_ge(p_qlt, n + 1)
                    pe.wait_ge(p_vc, n + 1)
                    for hh in range(2):
                        lo = hh * ROPE
                        for qb in range(4):
                            nk = (qb + 1) * P
                            out = PS[:, 4 * hh + qb, 0:nk]
                            pe.matmul(out, QN[:, hh, qb * P:(qb + 1) * P], KN[:, hh, 0:nk], start=True, stop=False)
                            pe.matmul(out, QP[lo:lo + ROPE, qb * P:(qb + 1) * P], KPE[lo:lo + ROPE, 0:nk],
                                      start=False, stop=True).then_inc(p_sc, 1)
                    for hh in range(2):
                        pe.wait_ge(p_pn, n * 8 + (hh * 4 + 4))
                        for kb in range(4):
                            for qb in range(kb, 4):
                                last = pe.transpose(PS[:, 4 * hh + kb, (qb - kb) * P:(qb - kb + 1) * P],
                                                    PR[:, hh, qb, kb * P:(kb + 1) * P], IDENT)
                        last.then_inc(p_pt, 1)
                        pe.wait_ge(p_ptc, n * 2 + (hh + 1))
                        for kb in range(4):
                            last = pe.matmul(PS[:, 4 * hh, kb * P:NP_], VT[:, kb, hh, :], PTR[:, kb, 0:NP_ - kb * P],
                                             start=(kb == 0), stop=(kb == 3))
                        last.then_inc(p_o, 1)

                with pe.Fori(0, MH // 4) as i:
                    for jj in range(2):
                        head_pair(i, jj)
                fence()
                pe.sem_inc(k_free, 1)
                with pe.Fori(0, NB) as b:
                    pe.wait_ge(b_q, b + 1)
                    pe.wait_ge(k_in, b * (48 * NPAGE) + 48 * NPAGE)
                    for kb in range(4):
                        cc = slice(kb * 512, (kb + 1) * 512)
                        for r in range(RC):
                            pe.matmul(PS[0:MH, kb, :], QLB[:, r, :], KT[:, r, cc], start=(r == 0), stop=False)
                        last = pe.matmul(PS[0:MH, kb, :], QPB, KPT[:, cc], start=False, stop=True)
                    for r in range(RC):
                        pe.matmul(PS[0:MH, 4, 0:NB], QLB[:, r, :], CKV[:, r, NP_:T], start=(r == 0), stop=False)
                    pe.matmul(PS[0:MH, 4, 0:NB], QPB, KPE[0:ROPE, NP_:T], start=False, stop=True).then_inc(b_sc, 1)
                    pe.wait_ge(b_pn, b + 1)
                    apart(pe)
                    for pg in range(NPAGE):
                        pe.transpose(PS[:, 5, pg * MH:(pg + 1) * MH], PD[:, pg * PAGE:(pg + 1) * PAGE],
                                     IDENT[0:MH, 0:MH])
                    pe.transpose(PS[0:NB, 6, 0:MH], PD[:, PAST:PAST + NB], IDENT[0:MH, 0:MH]).then_inc(b_pt, 1)
                    pe.wait_ge(b_ptc, b + 1)
                    for r in range(RC):
                        for pg in range(NPAGE):
                            pe.matmul(PS[:, 7, r * MH:(r + 1) * MH], KN_[:, pg, r * P:(r + 1) * P], PTD[:, pg, :],
                                      start=(pg == 0), stop=False)
                        last = pe.matmul(PS[:, 7, r * MH:(r + 1) * MH], CKVS[:, r, :], PTD[0:NB, NPAGE, :],
                                         start=False, stop=True)
                    last.then_inc(b_o, 1)
                    pe.wait_ge(b_o, b + 1)
                    pe.sem_inc(k_free, 1)
                fence()
                slot = w_ready(pe, LOADS["uv"], 0, 0)
                for hh in range(8):
                    for k in range(RC):
                        last = pe.matmul(PS[:, 0, hh * NB:(hh + 1) * NB], W[:, slot, (k * 8 + hh) * P:(k * 8 + hh + 1) * P],
                                         OL[:, k, hh, :], start=(k == 0), stop=(k == RC - 1))
                last.then_inc(u_o, 1)
                pe.wait_ge(u_o, 1)
                pe.sem_inc(w_free, 1)
                slot = w_ready(pe, LOADS["uv"], 0, 1)
                for hh in range(8):
                    for k in range(RC):
                        last = pe.matmul(PS[:, 1, hh * NB:(hh + 1) * NB], W[:, slot, (k * 8 + hh) * P:(k * 8 + hh + 1) * P],
                                         OL[:, k, 8 + hh, :], start=(k == 0), stop=(k == RC - 1))
                last.then_inc(u_o, 1)
                pe.wait_ge(u_o, 2)
                pe.sem_inc(w_free, 1)
                fence()

            pe.wait_ge(const_in, 128)
            pe.wait_ge(c_exp, 2)
            for s in range(6):
                modulation(s)
                pre_norm(s)
                if s == 1:
                    hgrn()
                    ssm()
                    down(s, OC, 16)
                elif s == 4:
                    mla()
                    down(s, OC, 16)
                else:
                    ffn_up(s, (0, None, 1, 2, None, 3)[s])
                    down(s, GU, FC)
                post_norm(s)

        @block.scalar
        def _(act):
            fence = fencer(act)

            def root(q):
                act.wait_ge(var_ready, q)
                act.activation(R[:, :], R[:, :], ACT.Sqrt).then_inc(root_ready, 1)

            def pre_norm(s):
                for c in range(DC):
                    act.activation(Y[:, c, :], X[:, c, :], ACT.Square).then_inc(pre_sq, 1)
                root(2 * s + 1)
                for c in range(DC):
                    act.wait_ge(xr_ready, s * DC + c + 1)
                    act.activation(H[:, c, 0:NP_], H[:, c, 0:NP_], ACT.Identity, bias=MOD[:, c, 0:1],
                                   scale=AM[:, c, 0:1])
                fence()

            def post_norm(s):
                root(2 * s + 2)
                fence()

            def ffn_up(n):
                with act.Fori(0, FC // 2) as i:
                    for jj in range(2):
                        act.wait_ge(gu_ready, i * 2 + (n * FC + jj + 1))
                        act.activation(two(SILU[:, jj, :]), pair(4 * jj), ACT.Silu).then_inc(silu_ready, 1)
                fence()

            def down(s):
                with act.Fori(0, DC // 2) as i:
                    for jj in range(2):
                        act.wait_ge(y_ready, i * 2 + (s * DC + jj + 1))
                        act.activation(two(Y[:, i * 2 + jj, :]), pair(2 * jj), ACT.Copy)
                        act.activation(two(H[:, i * 2 + jj, :]), pair(2 * jj), ACT.Square).then_inc(y_taken, 1)
                fence()

            def hgrn():
                act.wait_ge(lb_exp, 1)
                act.activation(LB, LB, ACT.Exp).then_inc(lb_exp, 1)
                fence()
                with act.Fori(0, HG) as h:
                    for n, dst in enumerate((E1, E2, E3)):
                        act.wait_ge(h_proj, h * 4 + (n + 1))
                        act.activation(two(dst), pair(2 * n), ACT.Exp, scale=-1.0).then_inc(h_exp, 1)
                    act.wait_ge(h_proj, h * 4 + 4)
                    act.activation(VV.rearrange("p a b -> p (a b)"), PS[:, 6, :], ACT.Copy)
                    act.activation(VS, PS[0:NB, 7, 0:P], ACT.Copy).then_inc(h_v, 1)
                    act.wait_ge(h_f, h + 1)
                    act.activation(BB, FG[:, 0:NP_], ACT.Ln).then_inc(h_lf, 1)
                    act.wait_ge(h_d, h * 9 + 1)
                    act.activation(EB, BB, ACT.Exp).then_inc(h_ex, 1)
                    act.wait_ge(h_d, h * 9 + 2)
                    act.activation(KD, KD, ACT.Exp).then_inc(h_ex, 1)
                    for n in range(len(LEVELS)):
                        act.wait_ge(h_d, h * 9 + (3 + n))
                        act.activation(DL[:, n, :], DL[:, n, :], ACT.Exp).then_inc(h_ex, 1)
                    act.wait_ge(h_kt, h + 1)
                    act.activation(KDT.rearrange("p a b -> p (a b)"), PS[:, 4, :], ACT.Copy).then_inc(h_kdt, 1)
                    act.wait_ge(h_o, h * 2 + 2)
                    act.activation(SQO[:, 0:NP_], PS[:, 6, :], ACT.Square)
                    act.activation(SQO[:, NP_:T], PS[:, 7, 0:NB], ACT.Square).then_inc(h_sq, 1)
                    act.wait_ge(h_var, h + 1)
                    act.activation(R[:, :], R[:, :], ACT.Ln)
                    act.drain()
                    act.activation(R[:, :], R[:, :], ACT.Exp, scale=-0.5).then_inc(h_r, 1)
                fence()

            def ssm():
                fence()
                act.wait_ge(d_step, 1)
                act.activation(DTE, DTE, ACT.Exp, scale=-1.0)
                act.activation(SMS[:, 2:3], SMS[:, 1:2], ACT.Exp).then_inc(d_act, 1)
                act.wait_ge(d_step, 2)
                act.activation(DTE, DTE, ACT.Ln).then_inc(d_act, 1)
                act.wait_ge(d_pe, 2)
                act.activation(DTT.rearrange("p a b -> p (a b)"), PS[:, 2, 0:NCH * 16], ACT.Copy)
                act.activation(BT.rearrange("p a b -> p (a b)"), PS[:, 4, 0:NCH * 16], ACT.Copy)
                act.activation(DTS, PS[0:NB, 3, 0:16], ACT.Copy)
                fence()
                with act.Fori(0, SG_) as g:
                    act.wait_ge(st_ok, g + 1)
                    for c in range(4):
                        act.wait_ge(g_proj, g * 6 + (c + 1))
                        act.activation(two(XR[:, c, :]), pair(2 * c), ACT.Copy).then_inc(g_raw, 1)
                    act.wait_ge(g_conv, g + 1)
                    act.activation(EV.rearrange("p a b -> p (a b)"), CV.rearrange("p a b -> p (a b)"), ACT.Exp,
                                   scale=-1.0).then_inc(g_cexp, 1)
                    for z in range(2):
                        act.wait_ge(g_proj, g * 6 + (5 + z))
                        act.activation(two(GZ[:, z, :]), pair(2 * z), ACT.Exp, scale=-1.0).then_inc(g_zexp, 1)
                    act.wait_ge(g_tr, g + 1)
                    act.activation(BTK.rearrange("p a b -> p (a b)"), PS[:, 6, :], ACT.Copy).then_inc(g_btk, 1)
                    act.wait_ge(g_xt, g + 1)
                    act.activation(EA.rearrange("p a b -> p (a b)"), PS[:, 7, 256:256 + GH * NB], ACT.Exp)
                    act.wait_ge(g_bc, g + 1)
                    for j in range(GH):
                        act.activation(CEX[:, j, :], PS[:, j, :], ACT.Exp).then_inc(g_bcx, 1)
                    act.wait_ge(g_wl, g + 1)
                    act.activation(WL.rearrange("p a b -> p (a b)"), WL.rearrange("p a b -> p (a b)"), ACT.Exp)
                    act.activation(EL.rearrange("p a b -> p (a b)"), EL.rearrange("p a b -> p (a b)"),
                                   ACT.Exp).then_inc(g_wle, 1)
                    for j in range(GH):
                        act.wait_ge(g_seg, g * 4 + (j + 1))
                        act.activation(SEG[:, j, :], SEG[:, j, :], ACT.Exp).then_inc(g_sege, 1)
                    act.wait_ge(g_yv, g + 1)
                    for x in range(2):
                        act.activation(SUU[:, x, :], EV[:, x, :], ACT.Square)
                    act.drain().then_inc(g_sq, 1)
                    act.wait_ge(g_var, g + 1)
                    act.activation(R[:, :], R[:, :], ACT.Ln)
                    act.drain()
                    act.activation(R[:, :], R[:, :], ACT.Exp, scale=-0.5).then_inc(g_r, 1)
                fence()

            def mla():
                for c in range(4):
                    act.wait_ge(m_proj, c + 1)
                    act.activation(two(CQ[:, c, :]), pair(2 * c), ACT.Copy)
                    act.activation(two(Y[:, 4 + c, :]), pair(2 * c), ACT.Square).then_inc(m_copy, 1)
                for c in range(RC):
                    act.wait_ge(m_proj, 5 + c)
                    act.activation(two(CKV[:, c, :]), pair(2 * c + 2), ACT.Copy)
                    act.activation(two(QN[:, c, :]), pair(2 * c + 2), ACT.Square).then_inc(m_copy, 1)
                act.wait_ge(m_proj, 7)
                act.activation(two(QR), pair(6), ACT.Copy).then_inc(m_copy, 1)
                for n in range(2):
                    act.wait_ge(m_var, n + 1)
                    act.activation(R[:, :], R[:, :], ACT.Sqrt).then_inc(m_root, 1)
                act.wait_ge(m_perm, 2)
                act.activation(CKVS.rearrange("p a b -> p (a b)"), PS[0:NB, 4, 0:RC * P], ACT.Copy)
                fence()
                with act.Fori(0, MH // 4) as i:
                    for jj in range(2):
                        n = i * 2 + jj
                        for c in range(3):
                            act.wait_ge(p_q, n * 3 + (c + 1))
                            dst = QR if c == 0 else QN[:, c - 1, :]
                            act.activation(two(dst), pair(2 * c), ACT.Copy).then_inc(p_qc, 1)
                        act.wait_ge(p_v, n + 1)
                        act.activation(VT.rearrange("p a b c -> p (a b c)").rearrange("p (a b) -> p a b", a=2),
                                       PS[:, 6:8, :], ACT.Copy).then_inc(p_vc, 1)
                        act.wait_ge(p_k, n + 1)
                        act.activation(KN, PS[:, 4:6, :], ACT.Copy).then_inc(p_kc, 1)
                        for hh in range(2):
                            for qb in range(4):
                                nk = (qb + 1) * P
                                act.wait_ge(p_mx, n * 8 + (hh * 4 + qb + 1))
                                act.activation(PR[:, hh, qb, 0:nk], PS[:, 4 * hh + qb, 0:nk], ACT.Exp,
                                               bias=SNB[:, hh, qb:qb + 1], scale=SCALE,
                                               accum_out=SRS[:, hh, qb:qb + 1]).then_inc(p_pr, 1)
                        for hh in range(2):
                            act.wait_ge(p_pt, n * 2 + (hh + 1))
                            if hh:
                                act.wait_ge(p_o, n * 2 + 1)
                            for kb in range(4):
                                last = act.activation(PTR[:, kb, 0:NP_ - kb * P], PS[:, 4 * hh + kb, 0:NP_ - kb * P],
                                                      ACT.Copy)
                            last.then_inc(p_ptc, 1)
                            act.wait_ge(p_o, n * 2 + (hh + 1))
                            act.activation(OC[:, n * 2 + hh, 0:NP_], PS[:, 4 * hh, :], ACT.Copy).then_inc(p_oc, 1)
                fence()
                with act.Fori(0, NB) as b:
                    act.wait_ge(b_mx, b + 1)
                    act.activation(PD[:, 0:PAST].rearrange("p (a b) -> p a b", a=4), PS[0:MH, 0:4, :], ACT.Exp,
                                   bias=DST[:, 3:4], scale=SCALE, accum_out=DST[:, 4:5])
                    act.activation(PD[:, PAST:PAST + NB], PS[0:MH, 4, 0:NB], ACT.Exp, bias=DST[:, 3:4], scale=SCALE,
                                   accum_out=DST[:, 5:6])
                    act.drain().then_inc(b_ex, 1)
                    act.wait_ge(b_pt, b + 1)
                    act.activation(PTD[:, 0:NPAGE, :].rearrange("p a b -> p (a b)"), PS[:, 5, 0:NPAGE * MH], ACT.Copy)
                    act.activation(PTD[0:NB, NPAGE, :], PS[0:NB, 6, 0:MH], ACT.Copy).then_inc(b_ptc, 1)
                fence()
                act.wait_ge(u_o, 2)
                for n in range(2):
                    act.activation(OC[:, 8 * n:8 * n + 8, NP_:T],
                                   PS[:, n, 0:8 * NB].rearrange("p (a b) -> p a b", a=8), ACT.Copy)
                fence()

            act.wait_ge(const_in, 128)
            act.activation(CE[:, :, :].rearrange("p a b -> p (a b)"), CS[:, :, :].rearrange("p a b -> p (a b)"),
                           ACT.Exp, scale=-1.0).then_inc(c_exp, 1)
            for s in range(6):
                fence()
                pre_norm(s)
                if s == 1:
                    hgrn()
                    ssm()
                elif s == 4:
                    mla()
                else:
                    ffn_up((0, None, 1, 2, None, 3)[s])
                down(s)
                post_norm(s)

        @block.vector
        def _(dve):
            fence = fencer(dve)
            tt, ts, stt = dve.tensor_tensor, dve.tensor_scalar, dve.scalar_tensor_tensor
            dve.sem_inc(mod_taken, 4)
            dve.sem_inc(gu_taken, 2)
            dve.sem_inc(y_taken, 2)
            dve.sem_inc(p_oc, 2)
            dve.sem_inc(h_done, 1)
            dve.sem_inc(h_ptk, 4)

            def bcast(ap, axis, n):
                ap = ap.unsqueeze(axis)
                shape = list(ap.shape)
                shape[axis] = n
                return ap.to_broadcast(shape)

            def modulation(s):
                with dve.Fori(0, NMOD // 4) as i:
                    for c in range(4):
                        dve.wait_ge(mod_ready, i * 4 + (s * NMOD + c + 1))
                        ts(MOD[:, i * 4 + c, :], PS[:, 4 + c, 0:NSEQ], ADB[:, s, bass.ds(i * 4 + c, 1)], None,
                           ALU.add).then_inc(mod_taken, 1)
                fence()

            def inv_rms(q, width):
                dve.wait_ge(sums_ready, q)
                ts(two(R[:, :]), pair(0), 1.0 / width, EPS, ALU.mult, ALU.add).then_inc(var_ready, 1)
                dve.wait_ge(root_ready, q)
                dve.reciprocal(R[:, :], R[:, :])
                dve.drain()

            def pre_norm(s):
                ts(AM[:, :, :], MOD[:, DC:2 * DC, :], 1.0, None, ALU.add)
                ts(GM[:, :, :], MOD[:, 2 * DC:3 * DC, :], 1.0 if s % 3 == 1 else 0.5, None, ALU.mult)
                dve.drain()
                tt(AM[:, :, :], AM[:, :, :], bcast(NPRE[:, s, :], 2, NSEQ), ALU.mult)
                tt(GM[:, :, :], GM[:, :, :], bcast(NPOST[:, s, :], 2, NSEQ), ALU.mult)
                inv_rms(2 * s + 1, D)
                for c in range(DC):
                    tt(H[:, c, :], X[:, c, :], R[:, :], ALU.mult).then_inc(xr_ready, 1)
                dve.drain()
                tt(H[:, :, NP_:T], H[:, :, NP_:T], AM[:, :, 1:NSEQ], ALU.mult)
                dve.drain()
                tt(H[:, :, NP_:T], H[:, :, NP_:T], MOD[:, 0:DC, 1:NSEQ], ALU.add)
                fence()

            def post_norm(s):
                inv_rms(2 * s + 2, D)
                tt(Y[:, :, NP_:T], Y[:, :, NP_:T], GM[:, :, 1:NSEQ], ALU.mult)
                for c in range(DC):
                    stt(Y[:, c, 0:NP_], Y[:, c, 0:NP_], GM[:, c, 0:1], R[:, 0:NP_], ALU.mult, ALU.mult)
                dve.drain()
                tt(Y[:, :, NP_:T], Y[:, :, NP_:T], bcast(R[:, NP_:T], 1, DC), ALU.mult)
                for c in range(DC):
                    tt(X[:, c, 0:NP_], X[:, c, 0:NP_], Y[:, c, 0:NP_], ALU.add)
                dve.drain()
                tt(X[:, :, NP_:T], X[:, :, NP_:T], Y[:, :, NP_:T], ALU.add)
                fence()

            def ffn_up(n):
                with dve.Fori(0, FC // 2) as i:
                    for jj in range(2):
                        dve.wait_ge(silu_ready, i * 2 + (n * FC + jj + 1))
                        tt(two(GU[:, i * 2 + jj, :]), pair(4 * jj + 2), two(SILU[:, jj, :]),
                           ALU.mult).then_inc(gu_taken, 1)
                fence()

            def sigmoid(e):
                ts(e, e, 1.0, None, ALU.add)
                dve.drain()
                dve.reciprocal(e, e)
                dve.drain()

            def hgrn():
                dve.wait_ge(vec_in, 32)
                tt(LMX, LB[:, 0, :], LB[:, 1, :], ALU.max)
                dve.drain()
                tt(LMX, LMX, LB[:, 2, :], ALU.max)
                dve.drain()
                tt(LB, LB, bcast(LMX, 1, 3), ALU.subtract).then_inc(lb_exp, 1)
                dve.wait_ge(lb_exp, 2)
                tt(LMX, LB[:, 0, :], LB[:, 1, :], ALU.add)
                dve.drain()
                tt(LMX, LMX, LB[:, 2, :], ALU.add)
                dve.drain()
                dve.reciprocal(LMX, LMX)
                dve.drain()
                tt(HVEC[:, 0, :], LB[:, 0, :], LMX, ALU.mult)
                dve.drain()
                ts(HVEC[:, 1, :], HVEC[:, 0, :], -1.0, 1.0, ALU.mult, ALU.add)
                fence()
                with dve.Fori(0, HG) as h:
                    dve.tensor_copy(HP, HVEC[:, :, h])
                    dve.wait_ge(h_exp, h * 3 + 1)
                    sigmoid(E1)
                    tt(two(QS), pair(0), two(E1), ALU.mult)
                    dve.wait_ge(h_exp, h * 3 + 2)
                    ts(E2, E2, 1e30, None, ALU.min)
                    dve.drain()
                    dve.tensor_copy(E2R, E2)
                    dve.drain()
                    sigmoid(E2R)
                    ts(FG, E2R, HP[:, 1:2], HP[:, 0:1], ALU.mult, ALU.add).then_inc(h_f, 1)
                    stt(KK, E2, HP[:, 1:2], E2R, ALU.mult, ALU.mult)
                    dve.wait_ge(h_exp, h * 3 + 3)
                    sigmoid(E3)
                    tt(two(GS), pair(4), two(E3), ALU.mult)
                    dve.wait_ge(h_lf, h + 1)
                    dve.tensor_copy(EB, BB)
                    dve.drain()
                    dve.tensor_tensor_scan(BB, const("reset"), EB, 0.0, ALU.mult, ALU.add)
                    dve.drain().then_inc(h_d, 1)
                    B4 = BB.rearrange("p (a b) -> p a b", b=CH)
                    tt(KD.rearrange("p (a b) -> p a b", b=CH), B4[:, :, CH - 1:CH].to_broadcast([P, NCH, CH]), B4,
                       ALU.subtract).then_inc(h_d, 1)
                    for n, m in enumerate(LEVELS):
                        b = BB.rearrange("p (a c b) -> p a c b", c=2, b=m)
                        d = DL[:, n, :].rearrange("p (a c b) -> p a c b", c=2, b=m)
                        ref = b[:, :, 0, m - 1:m].to_broadcast([P, NP_ // (2 * m), m])
                        tt(d[:, :, 1, :], b[:, :, 1, :], ref, ALU.subtract)
                        tt(d[:, :, 0, :], ref, b[:, :, 0, :], ALU.subtract).then_inc(h_d, 1)
                    dve.wait_ge(h_ex, h * 9 + 1)
                    tt(QI, QS[:, 0:NP_], EB, ALU.mult)
                    dve.wait_ge(h_ex, h * 9 + 2)
                    tt(KD, KD, KK[:, 0:NP_], ALU.mult).then_inc(h_kd, 1)
                    for n, m in enumerate(LEVELS):
                        dve.wait_ge(h_ex, h * 9 + (3 + n))
                        d = DL[:, n, :].rearrange("p (a c b) -> p a c b", c=2, b=m)
                        q = QS[:, 0:NP_].rearrange("p (a c b) -> p a c b", c=2, b=m)
                        k = KK[:, 0:NP_].rearrange("p (a c b) -> p a c b", c=2, b=m)
                        tt(d[:, :, 1, :], d[:, :, 1, :], q[:, :, 1, :], ALU.mult)
                        tt(d[:, :, 0, :], d[:, :, 0, :], k[:, :, 0, :], ALU.mult).then_inc(h_qk, 1)
                    dve.wait_ge(s_loaded, h * 16 + 16)
                    dve.wait_ge(h_vb, h + 1)
                    tt(S0, S0, bcast(FG[:, NP_:T], 2, P), ALU.mult)
                    for b in range(2):
                        tt(VK[:, 4 * b:4 * b + 4, :], PS[:, 6 + b, :].rearrange("p (a b) -> p a b", a=4),
                           bcast(KK[:, NP_ + 4 * b:NP_ + 4 * b + 4], 2, P), ALU.mult)
                    dve.drain().then_inc(h_vk, 1)
                    tt(S0, S0, VK, ALU.add).then_inc(s_new, 1)
                    ident = bcast(IDENT, 1, NCH)
                    for n in range(1 + len(LEVELS)):
                        dve.wait_ge(h_p, h * 8 + (n + 1))
                        src = PS[:, n % 4, :].rearrange("p (a b) -> p a b", a=NCH)
                        if n == 0:
                            tt(AT, src, ident, ALU.mult).then_inc(h_ptk, 1)
                            dve.drain()
                        else:
                            apart(dve)
                            dve.copy_predicated(AT, bcast(MSK[:, n - 1, :], 1, NCH), src).then_inc(h_ptk, 1)
                            dve.drain()
                    dve.sem_inc(h_att, 1)
                    dve.wait_ge(h_u, h + 1)
                    dve.wait_ge(s_stored, h + 1)
                    dve.tensor_copy(ST[:, 0, :], PS[:, 5, 0:P])
                    for c in range(1, NCH):
                        dve.drain()
                        stt(ST[:, c, :], ST[:, c - 1, :], EB[:, (c + 1) * CH - 1:(c + 1) * CH],
                            PS[:, 5, c * P:(c + 1) * P], ALU.mult, ALU.add)
                    dve.drain().then_inc(h_s, 1)
                    dve.wait_ge(h_ss, h + 1)
                    ts(two(R[:, :]), pair(0), 1.0 / P, EPS, ALU.mult, ALU.add).then_inc(h_var, 1)
                    dve.wait_ge(h_r, h + 1)
                    tt(R[:, 0:NP_], R[:, 0:NP_], PS[:, 6, :], ALU.mult)
                    tt(R[:, NP_:T], R[:, NP_:T], PS[:, 7, 0:NB], ALU.mult)
                    dve.drain()
                    stt(OC[:, h, :], R[:, :], HP[:, 2:3], GS, ALU.mult, ALU.mult)
                    dve.drain().then_inc(h_done, 1)
                dve.wait_ge(s_stored, HG + 1)
                fence()

            def ssm():
                fence()
                dve.wait_ge(g_in, 80)
                dve.wait_ge(d_pe, 1)
                ts(two(DTV), pair(0, rows=16), SMS[:, 0:1], None, ALU.add)
                dve.drain()
                ts(DTE, DTV, -1.0, None, ALU.mult)
                dve.drain()
                tt(DTE, DTE, DTV, ALU.max).then_inc(d_step, 1)
                dve.wait_ge(d_act, 1)
                ts(SMS[:, 2:3], SMS[:, 2:3], -1.0, None, ALU.mult)
                ts(DTE, DTE, 1.0, None, ALU.add).then_inc(d_step, 1)
                dve.wait_ge(d_act, 2)
                stt(DT, DTV, 0.0, DTE, ALU.max, ALU.add)
                dve.drain()
                ts(DTV, DT, SMS[:, 2:3], None, ALU.mult)
                dve.drain().then_inc(d_step, 1)
                dve.tensor_tensor_scan(LA[:, 0:NP_], const("reset", 16), DTV[:, 0:NP_], 0.0, ALU.mult, ALU.add)
                dve.tensor_copy(LA[:, NP_:T], DTV[:, NP_:T])
                dve.drain().then_inc(d_step, 1)
                fence()
                dve.sem_inc(g_done, 1)
                with dve.Fori(0, SG_) as g:
                    dve.tensor_copy(CWG, CW[:, g])
                    dve.tensor_copy(DSN[:, 0:2], DSK[:, g])
                    dve.tensor_copy(DSN[:, 2:4], SNW[:, g])
                    dve.tensor_copy(DTG, DTT[:, :, bass.ds(g * GH, GH)])
                    dve.tensor_copy(BTG, BT[:, :, bass.ds(g * GH, GH)])
                    dve.tensor_copy(DTSG, DTS[:, bass.ds(g * GH, GH)])
                    dve.tensor_copy(SELG.rearrange("p a b -> p (a b)"), const("sel16", 16)[:, bass.ds(g * (GH * P), GH * P)])
                    dve.drain().then_inc(g_sel, 1)
                    dve.wait_ge(g_raw, g * 4 + 4)
                    dve.wait_ge(st_in, g * 32 + 32)
                    for c in range(4):
                        ts(CV[:, c, :], XR[:, c, :], CWG[:, c, 3:4], CWG[:, c, 4:5], ALU.mult, ALU.add)
                    for tap in range(3):
                        dve.drain()
                        d = 3 - tap
                        for c in range(4):
                            stt(CV[:, c, d:NP_], XR[:, c, 0:NP_ - d], CWG[:, c, tap:tap + 1], CV[:, c, d:NP_],
                                ALU.mult, ALU.add)
                            stt(CV[:, c, NP_:T], STC[:, c, tap, :], CWG[:, c, tap:tap + 1], CV[:, c, NP_:T],
                                ALU.mult, ALU.add)
                    dve.drain().then_inc(g_conv, 1)
                    dve.wait_ge(g_cexp, g + 1)
                    sigmoid(EV)
                    tt(CV, CV, EV, ALU.mult)
                    dve.drain().then_inc(g_x, 1)
                    dve.wait_ge(g_zexp, g * 2 + 2)
                    sigmoid(GZ)
                    for z in range(2):
                        tt(two(GZ[:, z, :]), two(GZ[:, z, :]), pair(2 * z), ALU.mult)
                    dve.drain().then_inc(g_z, 1)
                    dve.wait_ge(g_tr, g + 1)
                    for x in range(2):
                        tt(XD[:, 2 * x:2 * x + 2], PS[:, 4 + x, :].rearrange("p (a b c) -> p a b c", a=2, b=GH),
                           bcast(DTG[:, 2 * x:2 * x + 2, :], 3, HD), ALU.mult)
                    tt(XDS.rearrange("p (a b) -> p a b", a=GH), PS[0:NB, 7, 0:GH * HD].rearrange("p (a b) -> p a b", a=GH),
                       bcast(DTSG, 2, HD), ALU.mult)
                    dve.drain().then_inc(g_xt, 1)
                    dve.wait_ge(g_cb, g + 1)
                    tt(CBM, PS[:, 6, :].rearrange("p (a b) -> p a b", a=NCH), bcast(const("causal"), 1, NCH), ALU.mult)
                    dve.wait_ge(g_bcx, g * 4 + 4)
                    last_b = PS[:, 0:GH, CH - 1:NP_:CH]
                    dve.tensor_copy(EL, last_b)
                    tt(WL, last_b, BTG.rearrange("p a b -> p b a"), ALU.subtract)
                    dve.drain().then_inc(g_wl, 1)
                    for j in range(GH):
                        for c in range(NCH):
                            cc = slice(c * CH, (c + 1) * CH)
                            last = ts(SEG[:, j, cc], PS[:, j, cc], BTG[:, c, j:j + 1], 0.0, ALU.subtract, ALU.min)
                        last.then_inc(g_seg, 1)
                    dve.drain().then_inc(g_bcfree, 1)
                    dve.wait_ge(g_wle, g + 1)
                    for c in range(NCH):
                        tt(XW[:, c], XD[:, c], bcast(WL[:, :, c], 2, HD), ALU.mult)
                    dve.drain().then_inc(g_xw, 1)
                    for j in range(GH):
                        tt(CEX[:, j, :], CEX[:, j, :], CV[:, 3, 0:NP_], ALU.mult)
                        dve.wait_ge(g_sege, g * 4 + (j + 1))
                        tt(SEG[:, j, :], SEG[:, j, :], CBM.rearrange("p a b -> p (a b)"), ALU.mult).then_inc(g_m, 1)
                    dve.wait_ge(g_u, g + 1)
                    u = [PS[:, 4 + c // 2, (c % 2) * 256:(c % 2 + 1) * 256].rearrange("p (a b) -> p a b", a=GH)
                         for c in range(NCH)]
                    dve.tensor_copy(SS[:, 0], u[0])
                    for c in range(1, NCH):
                        dve.drain()
                        tt(SS[:, c], SS[:, c - 1], bcast(EL[:, :, c], 2, HD), ALU.mult)
                        dve.drain()
                        tt(SS[:, c], SS[:, c], u[c], ALU.add)
                    dve.drain().then_inc(g_s, 1)
                    for j in range(GH):
                        tt(SM0[:, :, j, :], SM0[:, :, j, :], bcast(EA[:, j, :], 2, HD), ALU.mult)
                    dve.drain().then_inc(g_uu, 1)
                    dve.wait_ge(g_xb, g + 1)
                    for b in range(NB):
                        stt(SM0[:, b].rearrange("p a b -> p (a b)"), PS[:, b // 2, (b % 2) * 256:(b % 2 + 1) * 256],
                            CV[:, 2, NP_ + b:NP_ + b + 1], SM0[:, b].rearrange("p a b -> p (a b)"), ALU.mult, ALU.add)
                    dve.drain().then_inc(g_uu, 1)
                    dve.wait_ge(g_y, g * 2 + 2)
                    for x in range(2):
                        stt(EV[:, x, 0:NP_], CV[:, x, 0:NP_], DSN[:, x:x + 1], PS[:, 6 + x, :], ALU.mult, ALU.add)
                        stt(EV[:, x, NP_:T], CV[:, x, NP_:T], DSN[:, x:x + 1], PS[:, 4, x * NB:(x + 1) * NB],
                            ALU.mult, ALU.add)
                    dve.drain()
                    tt(EV[:, 0:2, :], EV[:, 0:2, :], GZ, ALU.mult)
                    dve.drain().then_inc(g_yv, 1)
                    dve.wait_ge(g_ss, g + 1)
                    ts(two(R[:, :]), pair(0), 1.0 / (2 * P), EPS, ALU.mult, ALU.add).then_inc(g_var, 1)
                    dve.wait_ge(g_r, g + 1)
                    for x in range(2):
                        stt(OC[:, g * 2 + (HG + x), :], EV[:, x, :], DSN[:, 2 + x:3 + x], R[:, :], ALU.mult, ALU.mult)
                    dve.drain().then_inc(g_done, 1)
                dve.wait_ge(st_ok, SG_ + 1)
                fence()

            def mla():
                dve.wait_ge(m_ss, 1)
                ts(two(R[:, :]), pair(0), 1.0 / (4 * P), EPS, ALU.mult, ALU.add).then_inc(m_var, 1)
                dve.wait_ge(m_root, 1)
                dve.reciprocal(R[:, :], R[:, :])
                dve.drain()
                dve.wait_ge(m_cks, 32)
                for c in range(4):
                    stt(CQ[:, c, :], CQ[:, c, :], GQ[:, c:c + 1], R[:, :], ALU.mult, ALU.mult)
                dve.drain().then_inc(m_norm, 1)
                dve.wait_ge(m_ss, 2)
                ts(two(R[:, :]), pair(0), 1.0 / (RC * P), EPS, ALU.mult, ALU.add).then_inc(m_var, 1)
                dve.wait_ge(m_root, 2)
                dve.reciprocal(R[:, :], R[:, :])
                dve.drain()
                for c in range(RC):
                    stt(CKV[:, c, :], CKV[:, c, :], GKV[:, c:c + 1], R[:, :], ALU.mult, ALU.mult)
                dve.drain().then_inc(m_norm, 1)
                dve.wait_ge(m_perm, 1)
                rotate(KPE).then_inc(m_norm, 1)
                fence()
                with dve.Fori(0, MH // 4) as i:
                    for jj in range(2):
                        n = i * 2 + jj
                        dve.wait_ge(p_ql, n + 1)
                        dve.tensor_copy(QL[:, :, bass.ds(n * 2, 2), :].rearrange("p r h b -> p h r b"),
                                        PS[:, 2, 0:4 * NB].rearrange("p (h r b) -> p h r b", h=2, r=RC))\
                           .then_inc(p_qlt, 1)
                        rotate(QP).then_inc(p_qp, 1)
                        dve.drain()
                        for hh in range(2):
                            dve.tensor_copy(QPS[:, n * 2 + hh, :], QP[hh * ROPE:(hh + 1) * ROPE, NP_:T])
                        for hh in range(2):
                            for qb in range(4):
                                nk = (qb + 1) * P
                                dve.wait_ge(p_sc, n * 8 + (hh * 4 + qb + 1))
                                s = PS[:, 4 * hh + qb, 0:nk]
                                tt(s[:, qb * P:nk], s[:, qb * P:nk], const("neg"), ALU.add)
                                dve.drain()
                                dve.reduce_max(SMX[:, hh, qb:qb + 1], s, AX_X)
                                dve.drain()
                                ts(SNB[:, hh, qb:qb + 1], SMX[:, hh, qb:qb + 1], -SCALE, None, ALU.mult)\
                                    .then_inc(p_mx, 1)
                        for hh in range(2):
                            for qb in range(4):
                                nk = (qb + 1) * P
                                dve.wait_ge(p_pr, n * 8 + (hh * 4 + qb + 1))
                                dve.reciprocal(SRI[:, hh, qb:qb + 1], SRS[:, hh, qb:qb + 1])
                                dve.drain()
                                ts(PR[:, hh, qb, 0:nk], PR[:, hh, qb, 0:nk], SRI[:, hh, qb:qb + 1], None, ALU.mult)\
                                    .then_inc(p_pn, 1)
                fence()
                with dve.Fori(0, NB) as b:
                    dve.tensor_copy(QLB, QL[:, :, :, b])
                    dve.tensor_copy(QPB, QPS[:, :, b])
                    dve.drain().then_inc(b_q, 1)
                    dve.wait_ge(b_sc, b + 1)
                    tt(PS[0:MH, 4, 0:NB], PS[0:MH, 4, 0:NB], const("own", MH)[:, bass.ds(b * NB, NB)], ALU.add)
                    dve.tensor_reduce(DST[:, 0:1], PS[0:MH, 0:4, :], mybir.AxisListType.XY, ALU.max)
                    dve.drain()
                    dve.reduce_max(DST[:, 1:2], PS[0:MH, 4, 0:NB], AX_X)
                    dve.drain()
                    tt(DST[:, 2:3], DST[:, 0:1], DST[:, 1:2], ALU.max)
                    dve.drain()
                    ts(DST[:, 3:4], DST[:, 2:3], -SCALE, None, ALU.mult).then_inc(b_mx, 1)
                    dve.wait_ge(b_ex, b + 1)
                    tt(DST[:, 6:7], DST[:, 4:5], DST[:, 5:6], ALU.add)
                    dve.drain()
                    dve.reciprocal(DST[:, 7:8], DST[:, 6:7])
                    dve.drain()
                    ts(PD, PD, DST[:, 7:8], None, ALU.mult)
                    dve.drain().then_inc(b_pn, 1)
                    dve.wait_ge(b_o, b + 1)
                    dve.tensor_copy(OL[:, :, :, b], PS[:, 7, 0:RC * MH].rearrange("p (a b) -> p a b", a=RC))
                    dve.drain().then_inc(b_oc, 1)
                fence()
                fence()

            def rotate(dst):
                bank = 2 if dst is KPE else 0
                tt(two(TMP), pair(bank), two(const("sin")), ALU.mult)
                tt(dst, QR, const("cos"), ALU.mult)
                dve.drain()
                return tt(dst, dst, TMP, ALU.add)

            dve.wait_ge(const_in, 128)
            dve.wait_ge(c_exp, 1)
            sigmoid(CE[:, :, :])
            tt(CS[:, :, :], CS[:, :, :], CE[:, :, :], ALU.mult).then_inc(c_exp, 1)
            for s in range(6):
                modulation(s)
                pre_norm(s)
                if s == 1:
                    hgrn()
                    ssm()
                elif s == 4:
                    mla()
                else:
                    ffn_up((0, None, 1, 2, None, 3)[s])
                fence()
                post_norm(s)


def _tiled(w, k, n):
    return w.reshape(k, P, n, P).transpose(2, 1, 0, 3)


def _lay_out(v):
    cat = np.concatenate
    c = np.ascontiguousarray
    out = {}
    out["const"], out["masks"] = constants()
    x = cat([v["x_prompt"][0], v["x_sample"][:, 0]])
    out["x"] = x.T.reshape(DC, P, T).transpose(1, 0, 2)
    out["c"] = cat([v["c_prompt"], v["c_sample"]]).T.reshape(DC, P, NSEQ).transpose(1, 0, 2)
    out["ada_w"] = v["ada_w"].reshape(2, DC, P, 72, P).transpose(0, 3, 2, 1, 4).reshape(144, P, DC * P)
    out["ada_b"] = v["ada_b"].reshape(6, NMOD, P).transpose(2, 0, 1)
    out["norm_pre"] = v["norm_pre"].reshape(6, DC, P).transpose(2, 0, 1)
    out["norm_post"] = v["norm_post"].reshape(6, DC, P).transpose(2, 0, 1)
    g, u = (v[n].reshape(4, DC, P, FC, P).transpose(0, 3, 2, 1, 4).reshape(4 * FC, P, DC * P)
            for n in ("ffn_wg", "ffn_wu"))
    out["ffn_gu"] = cat([g, u], axis=2)
    out["ffn_wd"] = v["ffn_wd"].reshape(4, FC, P, DC, P).transpose(0, 3, 2, 1, 4).reshape(4 * DC, P, FC * P)
    w = v["w_in_ab"]
    q, f, i, gate = (_tiled(w[:, n * 1024:(n + 1) * 1024], DC, HG) for n in range(4))
    z = _tiled(w[:, 4096:5120], DC, DC)
    xs = _tiled(w[:, 5120:6144], DC, DC)
    b = _tiled(w[:, 6144:6656], DC, SG_)
    cc = _tiled(w[:, 6656:7168], DC, SG_)
    out["w_hgrn"] = np.stack([cat([q, f], axis=2), cat([i, gate], axis=2)], axis=1).reshape(2 * HG, P, 2 * DC * P)
    out["w_ssm"] = np.stack([cat([xs[0::2], xs[1::2], b], axis=2), cat([cc, z[0::2], z[1::2]], axis=2)],
                            axis=1).reshape(2 * SG_, P, 3 * DC * P)
    out["w_dt"] = w[:, 7168:].reshape(DC, P, 16).transpose(1, 0, 2)
    out["w_out_ab"] = _tiled(v["w_out_ab"], 16, DC).reshape(DC, P, 16 * P)
    out["lb_logits"] = v["hg_lb_logits"].reshape(3, HG, P).transpose(2, 0, 1)
    out["hg_norm"] = v["hg_norm"].reshape(HG, P).T
    out["state_hgrn"] = v["state_hgrn"].transpose(1, 2, 0, 3)
    out["ssm_small"] = np.stack([v["ssm_dt_bias"], v["ssm_a_log"]], axis=1)

    def channels(a):
        n = a.shape[0]
        xs = a[:, :1024].reshape(n, SG_, 2, P)
        bc = a[:, 1024:].reshape(n, 2, SG_, P).transpose(0, 2, 1, 3)
        return cat([xs, bc], axis=2).transpose(1, 3, 2, 0)

    out["conv_w"] = cat([channels(v["ssm_conv_w"]), channels(v["ssm_conv_b"][None])], axis=3).transpose(1, 0, 2, 3)
    out["state_conv"] = channels(v["state_conv"].reshape(NB * 3, 2048)).reshape(SG_, P, 4, NB, 3).transpose(0, 1, 2, 4, 3)
    out["state_ssm"] = v["state_ssm"].reshape(NB, SG_, GH, P, HD).transpose(1, 3, 0, 2, 4)
    out["ssm_d"] = np.repeat(v["ssm_d"], HD).reshape(SG_, 2, P).transpose(2, 0, 1)
    out["ssm_norm"] = v["ssm_norm"].reshape(SG_, 2, P).transpose(2, 0, 1)
    out["mla_dq"] = _tiled(v["mla_w_dq"], DC, 4).reshape(2, 2, P, DC * P).transpose(0, 2, 1, 3)
    dkv = v["mla_w_dkv"]
    kpe = dkv[:, 256:].reshape(DC, P, ROPE).transpose(1, 0, 2)
    out["mla_dkv"] = cat([_tiled(dkv[:, :256], DC, RC).transpose(1, 0, 2, 3).reshape(P, 2 * DC, P),
                          cat([kpe, kpe], axis=2)], axis=1)
    uq = v["mla_w_uq"].reshape(4, P, 8, 2, 192)
    nope = uq[..., :128].transpose(2, 1, 3, 0, 4).reshape(8, P, -1)
    rope = uq[..., 128:].transpose(2, 1, 0, 3, 4).reshape(8, P, -1)
    uk = v["mla_w_uk"].reshape(RC, P, 8, 2, P)
    ukn = uk.transpose(2, 1, 3, 0, 4).reshape(8, P, -1)
    ukt = v["mla_w_uk"].reshape(256, 8, 2, P).transpose(1, 3, 2, 0).reshape(8, P, -1)
    uv = v["mla_w_uv"].reshape(RC, P, 8, 2, P).transpose(2, 1, 0, 3, 4).reshape(8, P, -1)
    out["mla_pairs"] = cat([nope, rope, ukn, uv, ukt], axis=2)
    out["mla_uv"] = v["mla_w_uv"].reshape(RC, P, 2, 8 * P).transpose(2, 1, 0, 3).reshape(2, P, 16 * P)
    out["mla_wo"] = _tiled(v["mla_w_o"], 16, DC).reshape(DC, P, 16 * P)
    out["mla_gq"] = v["mla_g_q"].reshape(4, P).T
    out["mla_gkv"] = v["mla_g_kv"].reshape(RC, P).T
    n_phys = v["cache_ckv"].shape[0]
    out["ckv"] = v["cache_ckv"]
    out["ckvT"] = v["cache_ckv"].reshape(n_phys, PAGE, RC, P).transpose(0, 3, 2, 1)
    out["kpeT"] = v["cache_kpe"].transpose(0, 2, 1)
    out["page_table"] = v["page_table"].reshape(1, -1)
    shapes = {"mla_dq": (2, P, 16 * P), "mla_dkv": (P, 24 * P)}
    return {n: c(a).reshape(shapes.get(n, a.shape)) for n, a in out.items()}


_OUTS = {"y": (P, DC, T), "hgrn_prompt": (HG, P, P), "hgrn_sample": (HG, P, NB, P),
         "ssm_prompt": (SG_, P, GH, HD), "ssm_sample": (SG_, P, NB, GH, HD),
         "conv_prompt": (SG_, P, 4, 3), "conv_sample": (SG_, P, 4, 3, NB), "ckv": (P, RC, T), "kpe": (ROPE, T)}


def kernel(**inputs):
    import concourse.bacc as _bacc
    from concourse import mybir as _mybir
    from concourse.bass_utils import run_bass_kernel_spmd as _run

    arrays = _lay_out({n: np.asarray(a) for n, a in inputs.items()})
    nc = _bacc.Bacc("TRN2", target_bir_lowering=False, num_devices=1)
    A = {n: nc.dram_tensor(f"in_{n}", a.shape, _mybir.dt.from_np(a.dtype), kind="ExternalInput").ap()
         for n, a in arrays.items()}
    O = {n: nc.dram_tensor(f"out_{n}", s, F32, kind="ExternalOutput").ap() for n, s in _OUTS.items()}
    build_program(nc, A, O)
    r = _run(nc, [{f"in_{n}": a for n, a in arrays.items()}], core_ids=[0]).results[0]
    o = {n: np.asarray(r[f"out_{n}"]) for n in _OUTS}

    y = o["y"].transpose(2, 1, 0).reshape(T, D)
    ckv = o["ckv"].transpose(2, 1, 0).reshape(T, RC * P)
    kpe = o["kpe"].T

    def rows(a):
        a = a.transpose(3, 0, 2, 1)
        return np.concatenate([a[:, :, 0:2].reshape(a.shape[0], -1), a[:, :, 2].reshape(a.shape[0], -1),
                               a[:, :, 3].reshape(a.shape[0], -1)], axis=1)

    conv_s = rows(o["conv_sample"].reshape(SG_, P, 4, 3 * NB)).reshape(3, NB, 2048).transpose(1, 0, 2)
    return (y[None, :NP_], y[NP_:, None],
            o["hgrn_prompt"][None], o["hgrn_sample"].transpose(2, 0, 1, 3),
            o["ssm_prompt"].transpose(0, 2, 1, 3).reshape(1, 16, P, HD),
            o["ssm_sample"].transpose(2, 0, 3, 1, 4).reshape(NB, 16, P, HD),
            rows(o["conv_prompt"])[None], conv_s,
            ckv[None, :NP_], ckv[NP_:, None], kpe[None, :NP_], kpe[NP_:, None])
```

```python
from contextlib import ExitStack

import numpy as np

import concourse.bass as bass
from concourse import mybir

F32 = mybir.dt.float32
F32R = mybir.dt.float32r
BF16 = mybir.dt.bfloat16
I32 = mybir.dt.int32
ALU = mybir.AluOpType
ACT = mybir.ActivationFunctionType
AX_X = mybir.AxisListType.X

P = 128
D = 1024
DC = D // P
NP_ = 512
NB = 8
T = NP_ + NB
HT = T // 2
FC = 2816 // P
NSEQ = 1 + NB
NMOD = 3 * DC
EPS = 1e-6
CH = 128
NCH = NP_ // CH
LEVELS = (64, 32, 16, 8, 4, 2, 1)
HG = 8
SG_ = 4
GH = 4
HD = 64
MH = 16
RC = 2
ROPE = 64
PAGE = 128
NPAGE = 16
PAST = PAGE * NPAGE
QR_ = 32
QUARTERS = P // QR_
PAGE_W = 4 * PAGE + 64
SCALE = float((128 + 64) ** -0.5)
NEG = -1e30

_COLS = {}
_WIDTH = []
for _table, _entries in enumerate((
        (("ident", P), ("ones", P), ("fold", P), ("eps", 1), ("scratch", 1)),
        (("reset", NP_), ("sel", NB * P), ("sel16", 16 * P), ("causal", P), ("neg", P), ("cos", T), ("sin", T),
         ("perm", P), ("own", NB * NB)))):
    _at = 0
    for _name, _n in _entries:
        _COLS[_name] = (_table, _at, _at + _n)
        _at += _n
    _WIDTH.append(_at)


def constants():
    tables = [np.zeros((P, n), np.float32) for n in _WIDTH]

    def put(name, a):
        t, a0, a1 = _COLS[name]
        tables[t][:a.shape[0], a0:a1] = a.reshape(a.shape[0], a1 - a0)

    r = np.arange(P)
    put("ident", np.eye(P))
    put("ones", np.ones((P, P)))
    put("eps", np.full((P, 1), EPS))
    put("reset", np.tile((np.arange(NP_) % CH != 0), (P, 1)))
    sel = np.zeros((NB, NB, P))
    sel[np.arange(NB), np.arange(NB)] = 1
    put("sel", sel)
    sel16 = np.zeros((16, 16, P))
    sel16[np.arange(16), np.arange(16)] = 1
    put("sel16", sel16)
    put("causal", (r[:, None] <= r[None, :]).astype(np.float32))
    put("neg", np.where(r[None, :] <= r[:, None], 0.0, NEG))
    half = ROPE // 2
    inv = (10000.0 ** (-np.arange(half, dtype=np.float32) / half)).astype(np.float32)
    pos = np.concatenate([np.arange(NP_), np.full(NB, PAST)]).astype(np.float32)
    ang = (inv[:, None] * pos[None]).astype(np.float32)
    put("cos", np.tile(np.cos(ang), (4, 1)))
    put("sin", np.concatenate([-np.sin(ang), np.sin(ang)] * 2))
    perm = np.zeros((P, P))
    perm[(r // ROPE) * ROPE + (r + half) % ROPE, r] = 1
    put("perm", perm)
    put("fold", (r[:, None] % QR_ == r[None, :] % QR_).astype(np.float32))
    own = np.full((QR_, NB, NB), NEG)
    own[:, np.arange(NB), np.arange(NB)] = 0
    put("own", own)
    masks = np.zeros((P, len(LEVELS), P), np.int32)
    s, u = r[:, None], r[None, :]
    for n, m in enumerate(LEVELS):
        masks[:, n] = (s // (2 * m) == u // (2 * m)) & ((s // m) % 2 == 0) & ((u // m) % 2 == 1)
    return tables[0], tables[1], masks


FFN0_DONE, HGRN_DONE, FFN3_DONE, ALL_DONE = 3, 6, 14, 23

WS = 24
LOADS = {}


def _plan():
    LOADS["mod"] = 0
    n = NMOD // 3
    for layer in range(2):
        for sub in range(3):
            s = layer * 3 + sub
            if sub != 1:
                LOADS["up", s] = n
                n += FC
            elif layer == 0:
                LOADS["hgrn"] = n
                n += 2 * HG
                LOADS["ssm"] = n
                n += 2 * SG_
            else:
                LOADS["latent"] = n
                n += 3
                LOADS["pairs"] = n
                n += MH // 2
                LOADS["uv"] = n
                n += 2
            LOADS["down", s] = n
            n += DC
    return n


_plan()


def build_program(nc, A, O):
    ctx = ExitStack()
    with ctx:
        def sb(name, shape, dt=F32):
            return ctx.enter_context(nc.sbuf_tensor(name, shape, dt))

        def shared(name, width, *layouts):
            seen = []
            for layout in layouts:
                with ExitStack() as inner:
                    seen.append([inner.enter_context(nc.sbuf_tensor(n, shape, dt)) for n, shape, dt in layout])
            return [sb(name, [P, width])] + seen

        def sem(name):
            return ctx.enter_context(nc.semaphore(name))

        PS = ctx.enter_context(nc.psum_tensor("PS", [P, 8, 512], F32))

        CT = sb("consts", [P, _WIDTH[0]])
        X = sb("residual", [P, DC, T])
        H, (HB, HL) = shared("hidden", DC * T, [("hid_bf", [P, DC, T], BF16), ("hid_rest", [P, DC, T], BF16)])
        Y, (HH,) = shared("sub_out", DC * T, [("hid_hi", [P, DC, T], F32R)])
        H, Y = (t[:, :].rearrange("p (a b) -> p a b", a=DC) for t in (H, Y))
        R = sb("inv_rms", [P, T])
        MOD = sb("modulation", [P, NMOD, NSEQ])
        AM = sb("pre_scale", [P, DC, NSEQ])
        GM = sb("post_scale", [P, DC, NSEQ])
        CS = sb("silu_c", [P, DC, QR_])
        W = sb("weight_ring", [P, 2, WS * P])
        AD = sb("ada_chunks", [P, 3 * DC * P])
        ADB = sb("ada_bias", [P, 6, NMOD])
        NPRE = sb("norm_pre", [P, 6, DC])
        NPOST = sb("norm_post", [P, 6, DC])
        PARTS, (WH, WB, WL_, SILU), (CT2, MSK) = shared(
            "weight_parts", _WIDTH[1] + len(LEVELS) * P,
            [("w_hi", [P, 2, DC * P], F32R), ("w_bf", [P, 2, DC * P], BF16), ("w_rest", [P, 2, DC * P], BF16),
             ("gate", [P, 2, T], F32)],
            [("mixer_consts", [P, _WIDTH[1]], F32), ("level_masks", [P, len(LEVELS), P], I32)])
        BIG, (GH_, GB, GL, MST) = shared(
            "arena", 23600,
            [("gu_hi", [P, FC, T], F32R), ("gu_bf", [P, FC, T], BF16), ("gu_rest", [P, FC, T], BF16),
             ("mod_space", [P, 3 * P + 2 * DC * NSEQ], F32)])

        def const(name, rows=P):
            table, a0, a1 = _COLS[name]
            return (CT, CT2)[table][0:rows, a0:a1]

        IDENT, ONES = const("ident"), const("ones")

        class Arena:
            def __init__(self, t, start=0):
                self.t, self.at = t, start

            def take(self, *shape, rows=P):
                n = int(np.prod(shape))
                ap = self.t[0:rows, self.at:self.at + n]
                self.at += n
                assert self.at <= self.t.shape[1], self.at
                if len(shape) == 1:
                    return ap
                names = "abcd"[:len(shape)]
                return ap.rearrange(f"p ({' '.join(names)}) -> p {' '.join(names)}",
                                    **{k: v for k, v in zip(names, shape)})

        NORMED = Arena(BIG).take(DC, T)
        ar = Arena(MST)
        MS = ar.take(3 * P)
        CR = ar.take(DC, NSEQ)
        CE = ar.take(DC, NSEQ)
        ar = Arena(BIG)
        OC = ar.take(16, T)
        mix0 = ar.at
        LB = ar.take(3, HG)
        LMX = ar.take(HG)
        HVEC = ar.take(3, HG)
        HP = ar.take(3)
        E2 = ar.take(T)
        QS, KK, FG, GS = ar.take(T), ar.take(T), ar.take(T), ar.take(T)
        E2R = ar.take(T)
        BB = ar.take(NP_)
        KD = ar.take(NP_)
        KDT = ar.take(NCH, P)
        EB = ar.take(NP_)
        QI = ar.take(NP_)
        VV = ar.take(NCH, P)
        VS = ar.take(P, rows=NB)
        AT = ar.take(NCH, P)
        ST = ar.take(NCH, P)
        SQO = ar.take(T)
        RH = ar.take(T)
        yar = Arena(Y.rearrange("p a b -> p (a b)"))
        DL = yar.take(len(LEVELS), NP_)
        S0 = ar.take(NB, P)
        VK = ar.take(NB, P)
        ar = Arena(BIG, mix0)
        CW = ar.take(SG_, 4, 5)
        CWG = ar.take(4, 5)
        DSK = ar.take(SG_, 2)
        SNW = ar.take(SG_, 2)
        DSN = ar.take(4)
        DTW = ar.take(DC, 16)
        SMS = ar.take(4, rows=16)
        DT = ar.take(T, rows=16)
        LA = ar.take(T, rows=16)
        DTT = ar.take(NCH, 16)
        BT = ar.take(NCH, 16)
        DTS = ar.take(16, rows=NB)
        DTG = ar.take(NCH, GH)
        BTG = ar.take(NCH, GH)
        DTSG = ar.take(GH, rows=NB)
        SELG = ar.take(GH, P, rows=16)
        XR = ar.take(4, T)
        DTV, DTE = XR[0:16, 0, :], XR[0:16, 1, :]
        CV = ar.take(4, T)
        STC = ar.take(4, 3, NB)
        GZ = ar.take(2, T)
        XD = ar.take(NCH, GH, HD)
        XW = ar.take(NCH, GH, HD)
        XDS = ar.take(GH * HD, rows=NB)
        BTK = ar.take(NCH, P)
        CBM = ar.take(NCH, P)
        WL = ar.take(GH, NCH)
        EL = ar.take(GH, NCH)
        EA = ar.take(GH, NB)
        SS = ar.take(NCH, GH, HD)
        ssm_e = ar.at
        EV = ar.take(4, T)
        SEG = EV[:, :, 0:NP_]
        yar = Arena(Y.rearrange("p a b -> p (a b)"))
        SM0 = yar.take(NB, GH, HD)
        CEX = yar.take(GH, NP_)
        YV = GZ
        SUU = CV[:, 0:2, :]
        ar = Arena(BIG, mix0)
        GQ = ar.take(4)
        GKV = ar.take(RC)
        CKV = ar.take(RC, T)
        KPE = ar.take(T)
        QL = ar.take(RC, MH, NB)
        QPS = ar.take(MH, NB, rows=ROPE)
        OL = ar.take(RC, MH, NB)
        CKVS = ar.take(RC, P, rows=NB)
        mla0 = ar.at
        CQ = Y[:, 0:4, :]
        TMP = ar.take(T)
        QR = ar.take(T)
        QP = ar.take(T)
        QN = ar.take(2, T)
        KN = ar.take(2, NP_)
        VT = ar.take(NCH, 2, P)
        PR = ar.take(2, 4, NP_)
        PTR = ar.take(4, NP_)
        SMX = ar.take(2, 4)
        SNB = ar.take(2, 4)
        SRS = ar.take(2, 4)
        SRI = ar.take(2, 4)
        ar = Arena(BIG, mla0)
        QLB = ar.take(RC, QR_)
        QPB = ar.take(2, QR_)
        PTD = ar.take(4, P)
        PTO = ar.take(QR_, rows=NB)
        DST = ar.take(8)
        ROW = ar.take(QR_ + P, rows=1)
        PD = ar.take(4, PAGE)
        PDO = ar.take(NB, rows=QR_)
        OP = ar.take(RC * P)
        har = Arena(H.rearrange("p a b -> p (a b)"))
        yar = Arena(Y.rearrange("p a b -> p (a b)"))
        PAGES = [[ar.take(PAGE_W) for _ in range(NPAGE)],
                 [har.take(PAGE_W) for _ in range(7)] + [yar.take(PAGE_W) for _ in range(7)]
                 + [ar.take(PAGE_W) for _ in range(2)]]
        TABLE = sb("page_table", [1, NB * NPAGE], I32)

        stage_done = sem("stage_done")
        const_in = sem("const_in")
        wait_passed = sem("wait_passed")
        w_arrived = [sem("w_arrived0"), sem("w_arrived1")]
        w_free = sem("w_free")
        ada_arrived = sem("ada_arrived")
        mod_ready = sem("mod_ready")
        mod_sums = sem("mod_sums")
        mod_copied = sem("mod_copied")
        pre_sq = sem("pre_sq")
        sums_ready = sem("sums_ready")
        root_ready = sem("root_ready")
        xr_ready = sem("xr_ready")
        hid_ready = sem("hid_ready")
        bf_ready = sem("bf_ready")
        rest_ready = sem("rest_ready")
        acc_ready = sem("acc_ready")
        x_ready = sem("x_ready")
        w_hi_ready = sem("w_hi_ready")
        w_rest_ready = sem("w_rest_ready")
        part_done = sem("part_done")
        silu_ready = sem("silu_ready")
        gu_taken = sem("gu_taken")
        y_ready = sem("y_ready")
        y_taken = sem("y_taken")
        out_stored = sem("out_stored")
        c_exp = sem("c_exp")
        vec_in = sem("vec_in")
        lb_exp = sem("lb_exp")
        h_proj = sem("h_proj")
        h_exp = sem("h_exp")
        h_v = sem("h_v")
        h_f = sem("h_f")
        h_lf = sem("h_lf")
        h_d = sem("h_d")
        h_ex = sem("h_ex")
        h_qk = sem("h_qk")
        h_kd = sem("h_kd")
        h_kt = sem("h_kt")
        h_kdt = sem("h_kdt")
        h_vb = sem("h_vb")
        h_vk = sem("h_vk")
        h_u = sem("h_u")
        h_s = sem("h_s")
        h_p = sem("h_p")
        h_ptk = sem("h_ptk")
        h_att = sem("h_att")
        h_o = sem("h_o")
        h_os = sem("h_os")
        h_sq = sem("h_sq")
        h_ss = sem("h_ss")
        h_r = sem("h_r")
        h_done = sem("h_done")
        s_loaded = sem("s_loaded")
        s_new = sem("s_new")
        s_stored = sem("s_stored")
        g_in = sem("g_in")
        d_step = sem("d_step")
        d_act = sem("d_act")
        d_pe = sem("d_pe")
        g_proj = sem("g_proj")
        g_raw = sem("g_raw")
        g_conv = sem("g_conv")
        g_x = sem("g_x")
        g_z = sem("g_z")
        g_sel = sem("g_sel")
        g_tr = sem("g_tr")
        g_btk = sem("g_btk")
        g_xt = sem("g_xt")
        g_bc = sem("g_bc")
        g_cb = sem("g_cb")
        g_cbm = sem("g_cbm")
        g_wl = sem("g_wl")
        g_wle = sem("g_wle")
        g_seg = sem("g_seg")
        g_sege = sem("g_sege")
        g_bcx = sem("g_bcx")
        g_m = sem("g_m")
        g_xw = sem("g_xw")
        g_u = sem("g_u")
        g_s = sem("g_s")
        g_bcfree = sem("g_bcfree")
        g_xb = sem("g_xb")
        g_uu = sem("g_uu")
        g_y = sem("g_y")
        g_ys = sem("g_ys")
        g_yv = sem("g_yv")
        g_sq = sem("g_sq")
        g_ss = sem("g_ss")
        g_r = sem("g_r")
        g_done = sem("g_done")
        st_in = sem("st_in")
        st_out = sem("st_out")
        st_ok = sem("st_ok")
        m_proj = sem("m_proj")
        m_copy = sem("m_copy")
        m_ss = sem("m_ss")
        m_root = sem("m_root")
        m_norm = sem("m_norm")
        m_perm = sem("m_perm")
        m_cks = sem("m_cks")
        p_q = sem("p_q")
        p_qc = sem("p_qc")
        p_perm = sem("p_perm")
        p_qp = sem("p_qp")
        p_ql = sem("p_ql")
        p_qlt = sem("p_qlt")
        p_v = sem("p_v")
        p_vc = sem("p_vc")
        p_k = sem("p_k")
        p_kc = sem("p_kc")
        p_sc = sem("p_sc")
        p_mx = sem("p_mx")
        p_pr = sem("p_pr")
        p_pn = sem("p_pn")
        p_pt = sem("p_pt")
        p_ptc = sem("p_ptc")
        p_o = sem("p_o")
        p_oc = sem("p_oc")
        k_in = [sem("k_in0"), sem("k_in1")]
        k_free = [sem("k_free0"), sem("k_free1")]
        b_q = sem("b_q")
        b_sc = sem("b_sc")
        b_mx = sem("b_mx")
        b_ex = sem("b_ex")
        b_m = sem("b_m")
        b_mt = sem("b_mt")
        b_sum = sem("b_sum")
        b_tot = sem("b_tot")
        b_on = sem("b_on")
        b_pt = sem("b_pt")
        b_ptc = sem("b_ptc")
        b_o = sem("b_o")
        b_oc = sem("b_oc")
        u_o = sem("u_o")

        block = ctx.enter_context(nc.Block())

        def fencer(eng):
            state = [0]

            def fence():
                state[0] += 1
                eng.drain().then_inc(stage_done, 1)
                eng.wait_ge(stage_done, 3 * state[0])
            return fence

        def pair(bank, cols=HT, rows=P):
            return PS[0:rows, bank:bank + 2, 0:cols]

        def two(ap):
            return ap.rearrange("p (a b) -> p a b", a=2)

        def apart(eng):
            eng.sem_inc(wait_passed, 1)

        def w_ready(pe, base, i, jj):
            slot = (base + jj) % 2
            pe.wait_ge(w_arrived[slot], i * 16 + 16 * ((base + jj) // 2 + 1))
            return slot

        UP_G, DOWN_G = 2, -(-FC // DC)
        FFN_OF = {0: 0, 2: 1, 3: 2, 5: 3}
        FFN_G = FC * UP_G + DC * DOWN_G

        def group(f, down, i, jj, j):
            per = DOWN_G if down else UP_G
            fixed = f * FFN_G + (FC * UP_G if down else 0) + jj * per + j
            return i * (2 * per) + fixed if not isinstance(i, int) else 2 * per * i + fixed, fixed % 2

        def tiles_in(down, j):
            return min(DC, FC - j * DC) if down else DC

        def staggered(eng, down, cut, finish, begin=None, cut_next=None):
            loads, groups = (DC, DOWN_G) if down else (FC, UP_G)

            def step(i, jj, more):
                if begin:
                    begin(i, jj)
                for j in range(2, groups):
                    cut(i, jj, j)
                for j in range(2):
                    if more:
                        cut(i, jj + 1, j)
                    elif cut_next:
                        cut_next(0, 0, j)
                finish(i, jj)

            with eng.Fori(0, loads // 2 - 1) as i:
                for jj in range(2):
                    step(i, jj, True)
            for jj in range(2):
                step(loads // 2 - 1, jj, jj == 0)

        XBANK = (2, 0, 4, 6)

        @block.sync
        def _(sp):
            sp.dma_start(CT[:, :], A["const"]).then_inc(const_in, 16)
            sp.dma_start(X[:, :, :], A["x"]).then_inc(const_in, 16)
            sp.dma_start(CR, A["c"]).then_inc(const_in, 16)
            sp.dma_start(ADB[:, :, :], A["ada_b"]).then_inc(const_in, 16)
            sp.dma_start(NPRE[:, :, :], A["norm_pre"]).then_inc(const_in, 16)
            sp.dma_start(NPOST[:, :, :], A["norm_post"]).then_inc(const_in, 16)
            sp.dma_start(TABLE[:, :], A["page_table"]).then_inc(const_in, 16)

            def load(base, i, jj, tiles, src):
                slot = (base + jj) % 2
                sp.wait_ge(w_free, i * 2 + (base + jj + 1))
                sp.dma_start(W[:, slot, 0:tiles * P], src).then_inc(w_arrived[slot], 16)

            def ffn_up(s, f):
                base = LOADS["up", s]
                with sp.Fori(0, FC // 2) as i:
                    for jj in range(2):
                        load(base, i, jj, 2 * DC, A["ffn_gu"][i * 2 + (f * FC + jj)])

            def down(s, src, tiles, first):
                base = LOADS["down", s]
                with sp.Fori(0, DC // 2) as i:
                    for jj in range(2):
                        load(base, i, jj, tiles, src[i * 2 + (first + jj)])
                        if s < 5:
                            sp.wait_ge(mod_sums, i * 2 + ((s + 1) * 8 + jj + 1))
                            sp.dma_start(AD[:, :], A["ada_w"][i * 2 + ((s + 1) * 8 + jj)]).then_inc(ada_arrived, 16)

            with sp.Fori(0, NMOD // 6) as i:
                for jj in range(2):
                    load(0, i, jj, 24, A["ada_w"][i * 2 + jj])
            for layer in range(2):
                ffn_up(layer * 3, layer * 2)
                down(layer * 3, A["ffn_wd"], FC, layer * 2 * DC)
                if layer == 0:
                    with sp.Fori(0, HG) as h:
                        for jj in range(2):
                            load(LOADS["hgrn"], h, jj, 16, A["w_hgrn"][h * 2 + jj])
                    with sp.Fori(0, SG_) as g:
                        for jj in range(2):
                            load(LOADS["ssm"], g, jj, 24, A["w_ssm"][g * 2 + jj])
                    down(1, A["w_out_ab"], 16, 0)
                else:
                    base = LOADS["latent"]
                    load(base, 0, 0, 16, A["mla_dq"][0])
                    load(base, 0, 1, 16, A["mla_dq"][1])
                    load(base, 0, 2, 24, A["mla_dkv"])
                    with sp.Fori(0, MH // 4) as i:
                        for jj in range(2):
                            load(LOADS["pairs"], i, jj, 24, A["mla_pairs"][i * 2 + jj])
                    with sp.Fori(0, NB // 2) as b:
                        for bb in range(2):
                            sp.wait_ge(k_free[bb], b + 1)
                            for pg in range(NPAGE):
                                page = sp.value_load(TABLE[0:1, bass.ds(b * (2 * NPAGE) + (bb * NPAGE + pg), 1)],
                                                     min_val=0, max_val=A["pages"].shape[0] - 1)
                                sp.dma_start(PAGES[bb][pg], A["pages"][page]).then_inc(k_in[bb], 16)
                    load(LOADS["uv"], 0, 0, 16, A["mla_uv"][0])
                    load(LOADS["uv"], 0, 1, 16, A["mla_uv"][1])
                    down(4, A["mla_wo"], 16, 0)
                ffn_up(layer * 3 + 2, layer * 2 + 1)
                down(layer * 3 + 2, A["ffn_wd"], FC, (layer * 2 + 1) * DC)

        @block.gpsimd
        def _(pool):
            pool.sem_inc(s_stored, 1)
            pool.sem_inc(st_ok, 1)

            pool.wait_ge(stage_done, 3 * FFN0_DONE)
            pool.dma_start(LB, A["lb_logits"]).then_inc(vec_in, 16)
            pool.dma_start(HVEC[:, 2, :], A["hg_norm"]).then_inc(vec_in, 16)
            pool.dma_start(CT2[:, :], A["mixer_const"]).then_inc(vec_in, 16)
            pool.dma_start(MSK[:, :, :], A["masks"]).then_inc(vec_in, 16)
            with pool.Fori(0, HG) as h:
                pool.wait_ge(h_done, h + 1)
                apart(pool)
                pool.dma_start(S0, A["state_hgrn"][h]).then_inc(s_loaded, 16)
                pool.wait_ge(h_s, h + 1)
                apart(pool)
                pool.dma_start(O["hgrn_prompt"][h], ST[:, NCH - 1, :]).then_inc(out_stored, 16)
                pool.wait_ge(s_new, h + 1)
                apart(pool)
                pool.dma_start(O["hgrn_sample"][h], S0).then_inc(out_stored, 16)
                pool.wait_ge(out_stored, h * 32 + 32)
                pool.sem_inc(s_stored, 1)
            pool.wait_ge(stage_done, 3 * HGRN_DONE)
            for dst, name in ((CW, "conv_w"), (DSK, "ssm_d"), (SNW, "ssm_norm"), (DTW, "w_dt"), (SMS[:, 0:2], "ssm_small")):
                pool.dma_start(dst, A[name]).then_inc(g_in, 16)
            with pool.Fori(0, SG_) as g:
                pool.wait_ge(g_done, g + 1)
                apart(pool)
                pool.dma_start(STC, A["state_conv"][g]).then_inc(st_in, 16)
                pool.dma_start(SM0, A["state_ssm"][g]).then_inc(st_in, 16)
                pool.wait_ge(st_in, g * 32 + 32)
                pool.wait_ge(g_raw, g * 4 + 4)
                apart(pool)
                pool.dma_start(O["conv_prompt"][g], XR[:, :, NP_ - 3:NP_]).then_inc(st_out, 16)
                pool.dma_start(O["conv_sample"][g, :, :, 0:2, :], STC[:, :, 1:3, :]).then_inc(st_out, 16)
                pool.dma_start(O["conv_sample"][g, :, :, 2, :], XR[:, :, NP_:T]).then_inc(st_out, 16)
                pool.wait_ge(g_s, g + 1)
                apart(pool)
                pool.dma_start(O["ssm_prompt"][g], SS[:, NCH - 1]).then_inc(st_out, 16)
                pool.wait_ge(g_uu, g * 2 + 2)
                apart(pool)
                pool.dma_start(O["ssm_sample"][g], SM0).then_inc(st_out, 16)
                pool.wait_ge(st_out, g * 80 + 80)
                pool.sem_inc(st_ok, 1)
            pool.wait_ge(stage_done, 3 * FFN3_DONE)
            pool.dma_start(GQ, A["mla_gq"]).then_inc(m_cks, 16)
            pool.dma_start(GKV, A["mla_gkv"]).then_inc(m_cks, 16)
            pool.dma_start(CT2[:, :], A["mixer_const"]).then_inc(m_cks, 16)
            pool.wait_ge(m_norm, 3)
            pool.dma_start(O["ckv"], CKV).then_inc(out_stored, 16)
            pool.dma_start(O["kpe"], KPE[0:ROPE, :]).then_inc(out_stored, 16)
            pool.wait_ge(out_stored, 32 * HG + 32)
            pool.wait_ge(stage_done, 3 * ALL_DONE)
            pool.dma_start(O["y"], X[:, :, :]).then_inc(out_stored, 16)
            pool.wait_ge(out_stored, 32 * HG + 48)

        @block.tensor
        def _(pe):
            fence = fencer(pe)
            pe.sem_inc(w_free, 2)

            def product(bank, weights, moving, rows=P):
                n = len(weights)
                for k in range(n):
                    for hf in range(2):
                        last = pe.matmul(PS[0:rows, bank + hf, 0:HT], weights[k], moving[k][:, hf * HT:(hf + 1) * HT],
                                         start=(k == 0), stop=(k == n - 1))
                return last

            def tiles(slot, first, n):
                return [W[:, slot, (first + k) * P:(first + k + 1) * P] for k in range(n)]

            def product_of_parts(bank, buf, n, first, hi, bf, rest, start, stop, before=None):
                for k in range(n):
                    cols = slice(k * P, (k + 1) * P)
                    if before:
                        before(k)
                    for hf in range(2):
                        out = PS[:, bank + hf, 0:HT]
                        half = slice(hf * HT, (hf + 1) * HT)
                        pe.matmul(out, WH[:, buf, cols], hi[:, first + k, half], start=start and k == 0, stop=False)
                        pe.matmul(out, WB[:, buf, cols], rest[:, first + k, half], start=False, stop=False)
                        last = pe.matmul(out, WL_[:, buf, cols], bf[:, first + k, half], start=False,
                                         stop=stop and k == n - 1)
                return last

            def rows_of(buf, n):
                return [buf[:, k, :] for k in range(n)]

            def mod_sums_of(weights):
                for k in range(DC):
                    q = k % QUARTERS
                    last = pe.matmul(PS[q * QR_:(q + 1) * QR_, 4, 0:3 * P], CS[:, k, :],
                                     weights[:, k * 3 * P:(k + 1) * 3 * P], start=(k < 4), stop=(k >= 4))
                last.then_inc(mod_sums, 1)

            def mod_fold(s, i, jj):
                pe.wait_ge(mod_copied, i * 2 + (s * 8 + jj + 1))
                for c in range(3):
                    last = pe.matmul(PS[:, 5, c * NSEQ:(c + 1) * NSEQ], MS[:, c * P:(c + 1) * P],
                                     const("fold")[:, 0:NSEQ], start=True, stop=True)
                last.then_inc(mod_ready, 1)

            def modulation():
                with pe.Fori(0, NMOD // 6) as i:
                    for jj in range(2):
                        slot = w_ready(pe, LOADS["mod"], i, jj)
                        mod_sums_of(W[:, slot, :])
                        mod_fold(0, i, jj)
                fence()

            def pre_norm(s):
                for c in range(DC):
                    pe.wait_ge(pre_sq, DC * s + c + 1)
                    for hf in range(2):
                        last = pe.matmul(PS[:, hf, 0:HT], ONES, Y[:, c, hf * HT:(hf + 1) * HT],
                                         start=(c == 0), stop=(c == DC - 1))
                last.then_inc(sums_ready, 1)
                if s % 3 == 1:
                    fence()

            def post_norm(s):
                pe.wait_ge(acc_ready, s + 1)
                product(0, [ONES], [R]).then_inc(sums_ready, 1)

            def ffn_up(f):
                def normed(k):
                    pe.wait_ge(bf_ready, f * DC + k + 1)
                    pe.wait_ge(rest_ready, f * DC + k + 1)

                def step(i, jj, before=None):
                    pe.wait_ge(gu_taken, i * 2 + (f * FC + jj + 1))
                    for j in range(UP_G):
                        g, buf = group(f, False, i, jj, j)
                        pe.wait_ge(w_rest_ready, g + 1)
                        product_of_parts(4 * jj + 2 * j, buf, DC, 0, HH, HB, HL, True, True,
                                         before if j == 0 else None).then_inc(part_done, 1)

                step(0, 0, normed)
                step(0, 1)
                with pe.Fori(1, FC // 2) as i:
                    for jj in range(2):
                        step(i, jj)
                fence()

            def ffn_down(s, f):
                with pe.Fori(0, DC // 2) as i:
                    for jj in range(2):
                        if s < 5:
                            pe.wait_ge(ada_arrived, i * 32 + (16 * (8 * s + jj + 1)))
                            mod_sums_of(AD)
                        pe.wait_ge(y_taken, i * 2 + (s * DC + jj + 1))
                        for j in range(DOWN_G):
                            g, buf = group(f, True, i, jj, j)
                            pe.wait_ge(w_rest_ready, g + 1)
                            product_of_parts(2 * jj, buf, tiles_in(True, j), j * DC, GH_, GB, GL, j == 0,
                                             j == DOWN_G - 1).then_inc(part_done, 1)
                        if s < 5:
                            mod_fold(s + 1, i, jj)
                fence()

            def down(s, src, nk):
                base = LOADS["down", s]
                with pe.Fori(0, DC // 2) as i:
                    for jj in range(2):
                        slot = w_ready(pe, base, i, jj)
                        if s < 5:
                            pe.wait_ge(ada_arrived, i * 32 + (16 * (8 * s + jj + 1)))
                            mod_sums_of(AD)
                        pe.wait_ge(y_taken, i * 2 + (s * DC + jj + 1))
                        product(2 * jj, tiles(slot, 0, nk), rows_of(src, nk)).then_inc(y_ready, 1)
                        if s < 5:
                            mod_fold(s + 1, i, jj)
                fence()

            def split_product(bank, weights, between):
                half = DC // 2
                for k in range(DC):
                    if k == half:
                        between()
                    for hf in range(2):
                        last = pe.matmul(PS[:, bank + hf, 0:HT], weights[k], H[:, k, hf * HT:(hf + 1) * HT],
                                         start=(k == 0), stop=(k == DC - 1))
                return last

            def hgrn():
                def head(h, more):
                    slot = LOADS["hgrn"] % 2
                    product(0, tiles(slot, 0, DC), rows_of(H, DC)).then_inc(h_proj, 1)
                    pe.wait_ge(h_done, h + 1)
                    slot = w_ready(pe, LOADS["hgrn"], h, 1)
                    product(4, tiles(slot, DC, DC), rows_of(H, DC)).then_inc(h_proj, 1)
                    wi = tiles(slot, 0, DC)
                    for c in range(NCH):
                        for k in range(DC):
                            pe.matmul(PS[:, 6, c * P:(c + 1) * P], H[:, k, c * CH:(c + 1) * CH], wi[k],
                                      start=(k == 0), stop=(k == DC - 1))
                    for k in range(DC):
                        last = pe.matmul(PS[0:NB, 7, 0:P], H[:, k, NP_:T], wi[k], start=(k == 0), stop=(k == DC - 1))
                    last.then_inc(h_proj, 1)
                    pe.wait_ge(h_v, h + 1)
                    for b in range(NB):
                        last = pe.matmul(PS[:, 6 + b // 4, (b % 4) * P:(b % 4 + 1) * P],
                                         const("sel", NB)[:, b * P:(b + 1) * P], VS, start=True, stop=True)
                    last.then_inc(h_vb, 1)
                    pe.wait_ge(h_kd, h + 1)
                    for c in range(NCH):
                        last = pe.transpose(PS[:, 4, c * P:(c + 1) * P], KD[:, c * CH:(c + 1) * CH], IDENT)
                    last.then_inc(h_kt, 1)
                    for n in range(1 + len(LEVELS)):
                        if n >= 1:
                            pe.wait_ge(h_qk, h * 7 + n)
                        pe.wait_ge(h_ptk, h * 8 + (n + 1))
                        for c in range(NCH):
                            cc = slice(c * CH, (c + 1) * CH)
                            lhs, rhs = (KK[:, cc], QS[:, cc]) if n == 0 else (DL[:, n - 1, cc], DL[:, n - 1, cc])
                            last = pe.matmul(PS[:, n % 4, cc], lhs, rhs, start=True, stop=True)
                        last.then_inc(h_p, 1)
                        if n == 0:
                            pe.wait_ge(h_kdt, h + 1)
                            for c in range(NCH):
                                last = pe.matmul(PS[:, 5, c * P:(c + 1) * P], KDT[:, c, :], VV[:, c, :],
                                                 start=True, stop=True)
                            last.then_inc(h_u, 1)
                    pe.wait_ge(h_vk, h + 1)
                    pe.wait_ge(h_att, h + 1)
                    pe.wait_ge(h_s, h + 1)
                    for c in range(NCH):
                        cc = slice(c * CH, (c + 1) * CH)
                        last = pe.matmul(PS[:, 6, cc], VV[:, c, :], AT[:, c, :], start=True, stop=(c == 0))
                        if c:
                            last = pe.matmul(PS[:, 6, cc], ST[:, c - 1, :], QI[:, cc], start=False, stop=True)
                    last.then_inc(h_o, 1)
                    pe.wait_ge(s_new, h + 1)
                    for b in range(NB):
                        last = pe.matmul(PS[:, 7, b:b + 1], S0[:, b, :], QS[:, NP_ + b:NP_ + b + 1],
                                         start=True, stop=True)
                    last.then_inc(h_o, 1)

                    def sums():
                        pe.wait_ge(h_sq, h + 1)
                        product(0, [ONES], [SQO]).then_inc(h_ss, 1)

                    if more:
                        slot = w_ready(pe, LOADS["hgrn"], h, 2)
                        split_product(2, tiles(slot, DC, DC), sums).then_inc(h_proj, 1)
                    else:
                        sums()
                    pe.wait_ge(h_r, h + 1)

                fence()
                slot = w_ready(pe, LOADS["hgrn"], 0, 0)
                product(2, tiles(slot, DC, DC), rows_of(H, DC)).then_inc(h_proj, 1)
                with pe.Fori(0, HG - 1) as h:
                    head(h, True)
                head(HG - 1, False)
                fence()

            def ssm():
                fence()
                pe.wait_ge(g_in, 80)
                product(0, [DTW[:, k, :] for k in range(DC)], rows_of(H, DC), rows=16).then_inc(d_pe, 1)
                pe.wait_ge(d_step, 4)
                for c in range(NCH):
                    pe.transpose(PS[:, 2, c * 16:(c + 1) * 16], DT[:, c * CH:(c + 1) * CH], IDENT[0:16, 0:16])
                    pe.transpose(PS[:, 4, c * 16:(c + 1) * 16], LA[:, c * CH:(c + 1) * CH], IDENT[0:16, 0:16])
                pe.transpose(PS[0:NB, 3, 0:16], DT[:, NP_:T], IDENT[0:16, 0:16]).then_inc(d_pe, 1)
                fence()
                def group_of_heads(g, more):
                    slot = LOADS["ssm"] % 2
                    pe.wait_ge(g_done, g + 1)
                    for c in range(1, 3):
                        product(XBANK[c], tiles(slot, c * DC, DC), rows_of(H, DC)).then_inc(g_proj, 1)
                    slot = w_ready(pe, LOADS["ssm"], g, 1)
                    product(XBANK[3], tiles(slot, 0, DC), rows_of(H, DC)).then_inc(g_proj, 1)
                    for c in range(2):
                        pe.wait_ge(g_raw, g * 4 + (c + 1))
                        product(XBANK[c], tiles(slot, (c + 1) * DC, DC), rows_of(H, DC)).then_inc(g_proj, 1)
                    pe.wait_ge(g_x, g + 1)
                    pe.wait_ge(g_raw, g * 4 + 4)
                    for c in range(NCH):
                        for x in range(2):
                            pe.transpose(PS[:, 4 + c // 2, (c % 2) * 256 + x * P:(c % 2) * 256 + (x + 1) * P],
                                         CV[:, x, c * CH:(c + 1) * CH], IDENT)
                        pe.transpose(PS[:, 6, c * P:(c + 1) * P], CV[:, 2, c * CH:(c + 1) * CH], IDENT)
                    for x in range(2):
                        pe.transpose(PS[0:NB, 7, x * P:(x + 1) * P], CV[:, x, NP_:T], IDENT)
                    pe.wait_ge(g_sel, g + 1)
                    for j in range(GH):
                        last = pe.matmul(PS[:, 7, 256 + j * NB:256 + (j + 1) * NB], SELG[:, j, :], LA[:, NP_:T],
                                         start=True, stop=True)
                    last.then_inc(g_tr, 1)
                    pe.wait_ge(g_z, g * 2 + 2)
                    for j in range(GH):
                        last = pe.matmul(PS[:, j, :], SELG[:, j, :], LA[:, 0:NP_], start=True, stop=True)
                    last.then_inc(g_bc, 1)
                    pe.wait_ge(g_btk, g + 1)
                    for c in range(NCH):
                        cc = slice(c * CH, (c + 1) * CH)
                        last = pe.matmul(PS[:, 6, cc], CV[:, 2, cc], CV[:, 3, cc], start=True, stop=True)
                    last.then_inc(g_cb, 1)
                    pe.wait_ge(g_xw, g + 1)
                    for c in range(NCH):
                        last = pe.matmul(PS[:, 4 + c // 2, (c % 2) * 256:(c % 2 + 1) * 256], BTK[:, c, :],
                                         XW[:, c].rearrange("p a b -> p (a b)"), start=True, stop=True)
                    last.then_inc(g_u, 1)
                    pe.wait_ge(g_bcfree, g + 1)
                    for b in range(NB):
                        last = pe.matmul(PS[:, b // 2, (b % 2) * 256:(b % 2 + 1) * 256],
                                         const("sel", NB)[:, b * P:(b + 1) * P], XDS, start=True, stop=True)
                    last.then_inc(g_xb, 1)
                    pe.wait_ge(g_m, g * 4 + 4)
                    pe.wait_ge(g_s, g + 1)
                    for j in range(GH):
                        lo = (j % 2) * HD
                        for c in range(NCH):
                            cc = slice(c * CH, (c + 1) * CH)
                            out = PS[lo:lo + HD, 6 + j // 2, cc]
                            last = pe.matmul(out, XD[:, c, j, :], SEG[:, j, cc], start=True, stop=(c == 0))
                            if c:
                                last = pe.matmul(out, SS[:, c - 1, j, :], CEX[:, j, cc], start=False, stop=True)
                    last.then_inc(g_y, 1)
                    pe.wait_ge(g_uu, g * 2 + 2)
                    for x in range(2):
                        for b in range(NB):
                            last = pe.matmul(PS[:, 4, x * NB + b:x * NB + b + 1],
                                             SM0[:, b, 2 * x:2 * x + 2, :].rearrange("p a b -> p (a b)"),
                                             CV[:, 3, NP_ + b:NP_ + b + 1], start=True, stop=True)
                    last.then_inc(g_y, 1)

                    def sums():
                        pe.wait_ge(g_sq, g + 1)
                        product(0, [ONES] * 2, rows_of(SUU, 2)).then_inc(g_ss, 1)

                    if more:
                        slot = w_ready(pe, LOADS["ssm"], g, 2)
                        split_product(XBANK[0], tiles(slot, 0, DC), sums).then_inc(g_proj, 1)
                    else:
                        sums()

                slot = w_ready(pe, LOADS["ssm"], 0, 0)
                product(XBANK[0], tiles(slot, 0, DC), rows_of(H, DC)).then_inc(g_proj, 1)
                with pe.Fori(0, SG_ - 1) as g:
                    group_of_heads(g, True)
                group_of_heads(SG_ - 1, False)
                fence()

            def mla():
                base = LOADS["latent"]
                for c in range(4):
                    if c % 2 == 0:
                        slot = w_ready(pe, base, 0, c // 2)
                    product(2 * c, tiles(slot, (c % 2) * DC, DC), rows_of(H, DC)).then_inc(m_proj, 1)
                slot = w_ready(pe, base, 0, 2)
                for c in range(3):
                    pe.wait_ge(m_copy, c + 2)
                    product(2 * (c + 1), tiles(slot, c * DC, DC), rows_of(H, DC)).then_inc(m_proj, 1)
                product(0, [ONES] * 4, rows_of(Y[:, 4:8, :], 4)).then_inc(m_ss, 1)
                pe.wait_ge(m_copy, 7)
                pe.wait_ge(m_root, 1)
                product(0, [ONES] * 2, rows_of(QN, 2)).then_inc(m_ss, 1)
                pe.wait_ge(m_cks, 48)
                product(2, [const("perm")], [QR]).then_inc(m_perm, 1)
                pe.wait_ge(m_norm, 2)
                for r in range(RC):
                    last = pe.transpose(PS[0:NB, 4, r * P:(r + 1) * P], CKV[:, r, NP_:T], IDENT)
                last.then_inc(m_perm, 1)
                fence()

                def head_pair(i, jj):
                    n = i * 2 + jj
                    slot = w_ready(pe, LOADS["pairs"], i, jj)
                    pe.wait_ge(p_oc, n * 2 + 2)
                    for c in range(3):
                        product(2 * c, tiles(slot, 4 * ((c + 2) % 3), 4), rows_of(CQ, 4)).then_inc(p_q, 1)
                    pe.wait_ge(p_qc, n * 3 + 3)
                    product(0, [const("perm")], [QR]).then_inc(p_perm, 1)
                    ukt = W[:, slot, 20 * P:24 * P].rearrange("p (a b) -> p a b", a=2)
                    for hh in range(2):
                        for r in range(RC):
                            last = pe.matmul(PS[:, 2, (hh * 2 + r) * NB:(hh * 2 + r + 1) * NB],
                                             ukt[:, hh, r * P:(r + 1) * P], QN[:, hh, NP_:T], start=True, stop=True)
                    last.then_inc(p_ql, 1)
                    uv = W[:, slot, 16 * P:20 * P].rearrange("p (a b) -> p a b", a=2)
                    for c in range(NCH):
                        for k in range(RC):
                            last = pe.matmul(PS[:, 6 + c // 2, (c % 2) * 256:(c % 2 + 1) * 256],
                                             CKV[:, k, c * CH:(c + 1) * CH], uv[:, k, :],
                                             start=(k == 0), stop=(k == RC - 1))
                    last.then_inc(p_v, 1)
                    uk = tiles(slot, 12, 4)
                    for hh in range(2):
                        for k in range(RC):
                            last = pe.matmul(PS[:, 4 + hh, :], uk[hh * 2 + k], CKV[:, k, 0:NP_],
                                             start=(k == 0), stop=(k == RC - 1))
                    last.then_inc(p_k, 1)
                    pe.wait_ge(p_kc, n + 1)
                    pe.wait_ge(p_qp, n + 1)
                    pe.wait_ge(p_qlt, n + 1)
                    pe.wait_ge(p_vc, n + 1)
                    for hh in range(2):
                        lo = hh * ROPE
                        for qb in range(4):
                            nk = (qb + 1) * P
                            out = PS[:, 4 * hh + qb, 0:nk]
                            pe.matmul(out, QN[:, hh, qb * P:(qb + 1) * P], KN[:, hh, 0:nk], start=True, stop=False)
                            pe.matmul(out, QP[lo:lo + ROPE, qb * P:(qb + 1) * P], KPE[lo:lo + ROPE, 0:nk],
                                      start=False, stop=True).then_inc(p_sc, 1)
                    for hh in range(2):
                        pe.wait_ge(p_pn, n * 8 + (hh * 4 + 4))
                        for kb in range(4):
                            for qb in range(kb, 4):
                                last = pe.transpose(PS[:, 4 * hh + kb, (qb - kb) * P:(qb - kb + 1) * P],
                                                    PR[:, hh, qb, kb * P:(kb + 1) * P], IDENT)
                        last.then_inc(p_pt, 1)
                        pe.wait_ge(p_ptc, n * 2 + (hh + 1))
                        for kb in range(4):
                            last = pe.matmul(PS[:, 4 * hh, kb * P:NP_], VT[:, kb, hh, :], PTR[:, kb, 0:NP_ - kb * P],
                                             start=(kb == 0), stop=(kb == 3))
                        last.then_inc(p_o, 1)

                def decode(b2, bb):
                    b = b2 * 2 + bb
                    pe.wait_ge(b_q, b + 1)
                    pe.wait_ge(k_in[bb], b2 * (16 * NPAGE) + 16 * NPAGE)
                    for j in range(4):
                        for part in range(4):
                            for q in range(QUARTERS):
                                page = PAGES[bb][4 * q + j]
                                out = PS[q * QR_:(q + 1) * QR_, 0, j * PAGE:(j + 1) * PAGE]
                                if part < RC:
                                    pe.matmul(out, QLB[:, part, :], page[:, part * PAGE:(part + 1) * PAGE],
                                              start=(part == 0), stop=False)
                                else:
                                    half = part - RC
                                    pe.matmul(out[:, half * 64:half * 64 + 64], QPB[:, half, :],
                                              page[:, 4 * PAGE:4 * PAGE + 64], start=False, stop=(half == 1))
                    own = PS[0:QR_, 1, 0:NB]
                    for r in range(RC):
                        pe.matmul(own, QLB[:, r, :], CKV[:, r, NP_:T], start=(r == 0), stop=False)
                    pe.matmul(own, QPB[0:ROPE, 0, :], KPE[0:ROPE, NP_:T], start=False, stop=True).then_inc(b_sc, 1)
                    pe.wait_ge(b_m, b * 2 + 1)
                    pe.matmul(PS[0:1, 2, 0:P], DST[:, 2:3], IDENT, start=True, stop=True).then_inc(b_mt, 1)
                    pe.wait_ge(b_m, b * 2 + 2)
                    pe.matmul(PS[:, 3, 0:1], ROW[:, QR_:QR_ + P], ONES[0:1, 0:1], start=True, stop=True)\
                        .then_inc(b_mt, 1)
                    pe.wait_ge(b_ex, b + 1)
                    for j in range(4):
                        pe.transpose(PS[:, 4, j * P:(j + 1) * P], PD[:, j, :], IDENT)
                    pe.transpose(PS[0:NB, 5, 0:QR_], PDO, IDENT[0:QR_, 0:QR_]).then_inc(b_pt, 1)
                    pe.wait_ge(b_sum, b + 1)
                    pe.matmul(PS[:, 7, 0:1], const("fold"), DST[:, 6:7], start=True, stop=True).then_inc(b_tot, 1)
                    pe.wait_ge(b_ptc, b + 1)
                    for j in range(4):
                        for q in range(QUARTERS):
                            pe.matmul(PS[q * QR_:(q + 1) * QR_, 6, 0:RC * P], PTD[:, j, q * QR_:(q + 1) * QR_],
                                      PAGES[bb][4 * q + j][:, 2 * PAGE:4 * PAGE], start=(j == 0),
                                      stop=(j == 3 and q > 0))
                    pe.matmul(PS[0:QR_, 6, 0:RC * P], PTO, CKVS.rearrange("p a b -> p (a b)"),
                              start=False, stop=True).then_inc(b_o, 1)
                    pe.wait_ge(b_on, b + 1)
                    for r in range(RC):
                        last = pe.matmul(PS[:, 7, MH + r * MH:2 * MH + r * MH], OP[:, r * P:(r + 1) * P],
                                         const("fold")[:, 0:MH], start=True, stop=True)
                    last.then_inc(b_oc, 1)

                with pe.Fori(0, MH // 4) as i:
                    for jj in range(2):
                        head_pair(i, jj)
                fence()
                for bb in range(2):
                    pe.sem_inc(k_free[bb], 1)
                with pe.Fori(0, NB // 2) as b2:
                    for bb in range(2):
                        decode(b2, bb)
                fence()
                slot = w_ready(pe, LOADS["uv"], 0, 0)
                for hh in range(8):
                    for k in range(RC):
                        last = pe.matmul(PS[:, 0, hh * NB:(hh + 1) * NB], W[:, slot, (k * 8 + hh) * P:(k * 8 + hh + 1) * P],
                                         OL[:, k, hh, :], start=(k == 0), stop=(k == RC - 1))
                last.then_inc(u_o, 1)
                pe.wait_ge(u_o, 1)
                pe.sem_inc(w_free, 1)
                slot = w_ready(pe, LOADS["uv"], 0, 1)
                for hh in range(8):
                    for k in range(RC):
                        last = pe.matmul(PS[:, 1, hh * NB:(hh + 1) * NB], W[:, slot, (k * 8 + hh) * P:(k * 8 + hh + 1) * P],
                                         OL[:, k, 8 + hh, :], start=(k == 0), stop=(k == RC - 1))
                last.then_inc(u_o, 1)
                pe.wait_ge(u_o, 2)
                pe.sem_inc(w_free, 1)
                fence()

            pe.wait_ge(const_in, 112)
            pe.wait_ge(c_exp, 2)
            modulation()
            pre_norm(0)
            for s in range(6):
                if s == 1:
                    hgrn()
                    ssm()
                    down(s, OC, 16)
                elif s == 4:
                    mla()
                    down(s, OC, 16)
                else:
                    f = FFN_OF[s]
                    ffn_up(f)
                    ffn_down(s, f)
                post_norm(s)
                if s < 5:
                    pre_norm(s + 1)
            fence()

        @block.scalar
        def _(act):
            fence = fencer(act)

            def inv_rms(done, width):
                act.activation(two(R[:, :]), pair(0), ACT.Ln, bias=const("eps"), scale=1.0 / width)
                act.drain()
                act.activation(R[:, :], R[:, :], ACT.Exp, scale=-0.5).then_inc(done, 1)

            def pre_norm(s):
                ffn = s % 3 != 1
                if ffn:
                    first = ffn_cut(FFN_OF[s], False, LOADS["up", s])
                    for j in range(2):
                        first(0, 0, j)
                for c in range(DC):
                    if s:
                        act.wait_ge(x_ready, (s - 1) * DC + c + 1)
                    act.activation(Y[:, c, :], X[:, c, :], ACT.Square).then_inc(pre_sq, 1)
                act.wait_ge(sums_ready, 2 * s + 1)
                inv_rms(root_ready, D)
                dst = NORMED if ffn else H
                for c in range(DC):
                    act.wait_ge(xr_ready, s * DC + c + 1)
                    act.activation(dst[:, c, 0:NP_], dst[:, c, 0:NP_], ACT.Identity, bias=MOD[:, c, 0:1],
                                   scale=AM[:, c, 0:1]).then_inc(hid_ready, 1)
                    if ffn:
                        act.drain()
                        act.activation(HB[:, c, :], dst[:, c, :], ACT.Copy).then_inc(bf_ready, 1)
                if not ffn:
                    fence()

            def post_norm(s):
                act.activation(const("scratch"), ONES[:, 0:1], ACT.Ln)
                act.wait_ge(sums_ready, 2 * s + 2)
                inv_rms(root_ready, D)

            def ffn_cut(f, down, base):
                def cut(i, jj, j):
                    slot = (base + jj) % 2
                    if j == 0:
                        w_ready(act, base, i, jj)
                    g, buf = group(f, down, i, jj, j)
                    n = tiles_in(down, j) * P
                    src = W[:, slot, j * DC * P:j * DC * P + n]
                    act.wait_ge(part_done, g + 1)
                    act.activation(WB[:, buf, 0:n], src, ACT.Copy)
                    act.activation(WH[:, buf, 0:n], src, ACT.Copy).then_inc(w_hi_ready, 1)
                return cut

            def ffn_up(s, f):
                def finish(i, jj):
                    act.wait_ge(part_done, group(f, False, i, jj, UP_G - 1)[0] + 3)
                    act.activation(two(SILU[:, jj, :]), pair(4 * jj), ACT.Silu).then_inc(silu_ready, 1)
                staggered(act, False, ffn_cut(f, False, LOADS["up", s]), finish,
                          cut_next=ffn_cut(f, True, LOADS["down", s]))
                fence()

            def ffn_down(s, f):
                def finish(i, jj):
                    act.wait_ge(part_done, group(f, True, i, jj, DOWN_G - 1)[0] + 3)
                    act.activation(two(Y[:, i * 2 + jj, :]), pair(2 * jj), ACT.Copy)
                    act.activation(two(H[:, i * 2 + jj, :]), pair(2 * jj), ACT.Square).then_inc(y_taken, 1)
                staggered(act, True, ffn_cut(f, True, LOADS["down", s]), finish)
                fence()

            def down(s):
                with act.Fori(0, DC // 2) as i:
                    for jj in range(2):
                        act.wait_ge(y_ready, i * 2 + (s // 3 * DC + jj + 1))
                        act.sem_inc(w_free, 1)
                        act.activation(two(Y[:, i * 2 + jj, :]), pair(2 * jj), ACT.Copy)
                        act.activation(two(H[:, i * 2 + jj, :]), pair(2 * jj), ACT.Square).then_inc(y_taken, 1)
                fence()

            def hgrn():
                act.wait_ge(lb_exp, 1)
                act.activation(LB, LB, ACT.Exp).then_inc(lb_exp, 1)
                fence()
                with act.Fori(0, HG) as h:
                    act.wait_ge(h_proj, h * 4 + 1)
                    act.activation(two(E2), pair(2), ACT.Exp, scale=-1.0).then_inc(h_exp, 1)
                    act.wait_ge(h_f, h + 1)
                    act.activation(BB, FG[:, 0:NP_], ACT.Ln).then_inc(h_lf, 1)
                    act.wait_ge(h_d, h * 9 + 1)
                    act.activation(EB, BB, ACT.Exp).then_inc(h_ex, 1)
                    act.wait_ge(h_d, h * 9 + 2)
                    act.activation(KD, KD, ACT.Exp).then_inc(h_ex, 1)
                    for n in range(len(LEVELS)):
                        act.wait_ge(h_d, h * 9 + (3 + n))
                        act.activation(DL[:, n, :], DL[:, n, :], ACT.Exp).then_inc(h_ex, 1)
                    act.wait_ge(h_proj, h * 4 + 2)
                    act.sem_inc(w_free, 1)
                    act.activation(two(QS), pair(0), ACT.Silu).then_inc(h_exp, 1)
                    act.wait_ge(h_proj, h * 4 + 3)
                    act.activation(two(GS), pair(4), ACT.Silu).then_inc(h_exp, 1)
                    act.wait_ge(h_proj, h * 4 + 4)
                    act.sem_inc(w_free, 1)
                    act.activation(VV.rearrange("p a b -> p (a b)"), PS[:, 6, :], ACT.Copy)
                    act.activation(VS, PS[0:NB, 7, 0:P], ACT.Copy).then_inc(h_v, 1)
                    act.wait_ge(h_kt, h + 1)
                    act.activation(KDT.rearrange("p a b -> p (a b)"), PS[:, 4, :], ACT.Copy).then_inc(h_kdt, 1)
                    act.wait_ge(h_o, h * 2 + 2)
                    act.activation(SQO[:, 0:NP_], PS[:, 6, :], ACT.Square)
                    act.activation(SQO[:, NP_:T], PS[:, 7, 0:NB], ACT.Square).then_inc(h_sq, 1)
                    act.wait_ge(h_ss, h + 1)
                    inv_rms(h_r, P)
                fence()

            def ssm():
                fence()
                act.wait_ge(d_step, 1)
                act.activation(DTE, DTE, ACT.Exp, scale=-1.0)
                act.activation(SMS[:, 2:3], SMS[:, 1:2], ACT.Exp).then_inc(d_act, 1)
                act.wait_ge(d_step, 2)
                act.activation(DTE, DTE, ACT.Ln).then_inc(d_act, 1)
                act.wait_ge(d_pe, 2)
                act.activation(DTT.rearrange("p a b -> p (a b)"), PS[:, 2, 0:NCH * 16], ACT.Copy)
                act.activation(BT.rearrange("p a b -> p (a b)"), PS[:, 4, 0:NCH * 16], ACT.Copy)
                act.activation(DTS, PS[0:NB, 3, 0:16], ACT.Copy)
                fence()
                with act.Fori(0, SG_) as g:
                    act.wait_ge(st_ok, g + 1)
                    for c in range(4):
                        act.wait_ge(g_proj, g * 6 + (c + 1))
                        if c == 2:
                            act.sem_inc(w_free, 1)
                        act.activation(two(XR[:, c, :]), pair(XBANK[c]), ACT.Copy).then_inc(g_raw, 1)
                    for z in range(2):
                        act.wait_ge(g_proj, g * 6 + (5 + z))
                        if z == 1:
                            act.sem_inc(w_free, 1)
                        act.activation(two(GZ[:, z, :]), pair(XBANK[z]), ACT.Silu).then_inc(g_z, 1)
                        if z == 0:
                            act.wait_ge(g_conv, g + 1)
                            act.activation(CV.rearrange("p a b -> p (a b)"), CV.rearrange("p a b -> p (a b)"),
                                           ACT.Silu).then_inc(g_x, 1)
                    act.wait_ge(g_tr, g + 1)
                    act.activation(BTK.rearrange("p a b -> p (a b)"), PS[:, 6, :], ACT.Copy).then_inc(g_btk, 1)
                    act.wait_ge(g_xt, g + 1)
                    act.activation(EA.rearrange("p a b -> p (a b)"), PS[:, 7, 256:256 + GH * NB], ACT.Exp)
                    act.wait_ge(g_bc, g + 1)
                    for j in range(GH):
                        act.activation(CEX[:, j, :], PS[:, j, :], ACT.Exp).then_inc(g_bcx, 1)
                    act.wait_ge(g_wl, g + 1)
                    act.activation(WL.rearrange("p a b -> p (a b)"), WL.rearrange("p a b -> p (a b)"), ACT.Exp)
                    act.activation(EL.rearrange("p a b -> p (a b)"), EL.rearrange("p a b -> p (a b)"),
                                   ACT.Exp).then_inc(g_wle, 1)
                    for j in range(GH):
                        act.wait_ge(g_seg, g * 4 + (j + 1))
                        act.activation(SEG[:, j, :], SEG[:, j, :], ACT.Exp).then_inc(g_sege, 1)
                    act.wait_ge(g_yv, g + 1)
                    for x in range(2):
                        act.activation(SUU[:, x, :], EV[:, x, :], ACT.Square)
                    act.drain().then_inc(g_sq, 1)
                    act.wait_ge(g_ss, g + 1)
                    inv_rms(g_r, 2 * P)
                fence()

            def mla():
                for c in range(4):
                    act.wait_ge(m_proj, c + 1)
                    if c % 2:
                        act.sem_inc(w_free, 1)
                    act.activation(two(CQ[:, c, :]), pair(2 * c), ACT.Copy)
                    act.activation(two(Y[:, 4 + c, :]), pair(2 * c), ACT.Square).then_inc(m_copy, 1)
                for c in range(RC):
                    act.wait_ge(m_proj, 5 + c)
                    act.activation(two(CKV[:, c, :]), pair(2 * c + 2), ACT.Copy)
                    act.activation(two(QN[:, c, :]), pair(2 * c + 2), ACT.Square).then_inc(m_copy, 1)
                act.wait_ge(m_proj, 7)
                act.sem_inc(w_free, 1)
                act.activation(two(QR), pair(6), ACT.Copy).then_inc(m_copy, 1)
                for n, width in enumerate((4 * P, RC * P)):
                    act.wait_ge(m_ss, n + 1)
                    if n:
                        act.wait_ge(m_norm, 1)
                    inv_rms(m_root, width)
                act.wait_ge(m_perm, 2)
                act.activation(CKVS.rearrange("p a b -> p (a b)"), PS[0:NB, 4, 0:RC * P], ACT.Copy)
                fence()
                with act.Fori(0, MH // 4) as i:
                    for jj in range(2):
                        n = i * 2 + jj
                        for c in range(3):
                            act.wait_ge(p_q, n * 3 + (c + 1))
                            dst = QR if c == 0 else QN[:, c - 1, :]
                            act.activation(two(dst), pair(2 * c), ACT.Copy).then_inc(p_qc, 1)
                        act.wait_ge(p_v, n + 1)
                        act.activation(VT.rearrange("p a b c -> p (a b c)").rearrange("p (a b) -> p a b", a=2),
                                       PS[:, 6:8, :], ACT.Copy).then_inc(p_vc, 1)
                        act.wait_ge(p_k, n + 1)
                        act.sem_inc(w_free, 1)
                        act.activation(KN, PS[:, 4:6, :], ACT.Copy).then_inc(p_kc, 1)
                        for hh in range(2):
                            for qb in range(4):
                                nk = (qb + 1) * P
                                act.wait_ge(p_mx, n * 8 + (hh * 4 + qb + 1))
                                act.activation(PR[:, hh, qb, 0:nk], PS[:, 4 * hh + qb, 0:nk], ACT.Exp,
                                               bias=SNB[:, hh, qb:qb + 1], scale=SCALE,
                                               accum_out=SRS[:, hh, qb:qb + 1]).then_inc(p_pr, 1)
                        for hh in range(2):
                            act.wait_ge(p_pt, n * 2 + (hh + 1))
                            if hh:
                                act.wait_ge(p_o, n * 2 + 1)
                            for kb in range(4):
                                last = act.activation(PTR[:, kb, 0:NP_ - kb * P], PS[:, 4 * hh + kb, 0:NP_ - kb * P],
                                                      ACT.Copy)
                            last.then_inc(p_ptc, 1)
                            act.wait_ge(p_o, n * 2 + (hh + 1))
                            act.activation(OC[:, n * 2 + hh, 0:NP_], PS[:, 4 * hh, :], ACT.Copy).then_inc(p_oc, 1)
                fence()
                with act.Fori(0, NB // 2) as b2:
                    for bb in range(2):
                        b = b2 * 2 + bb
                        act.wait_ge(b_mx, b + 1)
                        act.activation(PD.rearrange("p a b -> p (a b)"), PS[:, 0, :], ACT.Exp, bias=DST[:, 3:4],
                                       scale=SCALE, accum_out=DST[:, 4:5])
                        act.activation(PDO, PDO, ACT.Exp, bias=DST[0:QR_, 3:4], scale=SCALE,
                                       accum_out=DST[0:QR_, 5:6])
                        act.drain().then_inc(b_ex, 1)
                        act.wait_ge(b_pt, b + 1)
                        act.activation(PTD.rearrange("p a b -> p (a b)"), PS[:, 4, :], ACT.Copy)
                        act.activation(PTO, PS[0:NB, 5, 0:QR_], ACT.Copy).then_inc(b_ptc, 1)
                        act.wait_ge(b_o, b + 1)
                        act.sem_inc(k_free[bb], 1)
                fence()
                act.wait_ge(u_o, 2)
                for n in range(2):
                    act.activation(OC[:, 8 * n:8 * n + 8, NP_:T],
                                   PS[:, n, 0:8 * NB].rearrange("p (a b) -> p a b", a=8), ACT.Copy)
                fence()

            act.wait_ge(const_in, 112)
            act.activation(CE.rearrange("p a b -> p (a b)"), CR.rearrange("p a b -> p (a b)"),
                           ACT.Exp, scale=-1.0).then_inc(c_exp, 1)
            fence()
            pre_norm(0)
            for s in range(6):
                if s == 1:
                    hgrn()
                    ssm()
                elif s == 4:
                    mla()
                else:
                    ffn_up(s, FFN_OF[s])
                    ffn_down(s, FFN_OF[s])
                if s % 3 == 1:
                    down(s)
                post_norm(s)
                if s < 5:
                    pre_norm(s + 1)
            fence()

        @block.vector
        def _(dve):
            fence = fencer(dve)
            tt, ts, stt = dve.tensor_tensor, dve.tensor_scalar, dve.scalar_tensor_tensor
            dve.sem_inc(mod_sums, 1)
            dve.sem_inc(gu_taken, 2)
            dve.sem_inc(y_taken, 2)
            dve.sem_inc(part_done, 2)
            dve.sem_inc(p_oc, 2)
            dve.sem_inc(h_done, 1)
            dve.sem_inc(h_ptk, 4)

            def bcast(ap, axis, n):
                ap = ap.unsqueeze(axis)
                shape = list(ap.shape)
                shape[axis] = n
                return ap.to_broadcast(shape)

            def mod_copy(s, i, jj):
                dve.wait_ge(mod_sums, i * 2 + (s * 8 + jj + 2))
                if s == 0:
                    dve.sem_inc(w_free, 1)
                dve.tensor_copy(MS, PS[:, 4, 0:3 * P]).then_inc(mod_copied, 1)

            def mod_bias(s, i, jj):
                dve.wait_ge(mod_ready, i * 2 + (s * 8 + jj + 1))
                start = i * 6 + 3 * jj
                tt(MOD[:, bass.ds(start, 3), :], PS[:, 5, 0:3 * NSEQ].rearrange("p (a b) -> p a b", a=3),
                   bcast(ADB[:, s, bass.ds(start, 3)], 2, NSEQ), ALU.add)

            def modulation(s):
                with dve.Fori(0, NMOD // 6) as i:
                    for jj in range(2):
                        mod_copy(s, i, jj)
                        mod_bias(s, i, jj)
                        if s:
                            add_squares(s - 1, i, jj)
                if s:
                    acc_done()
                fence()

            def clear_sum():
                dve.memset(R[:, :], 0.0)
                dve.drain()

            def add_squares(s, i, jj):
                dve.wait_ge(y_taken, i * 2 + (s * DC + jj + 3))
                tt(R[:, :], R[:, :], H[:, i * 2 + jj, :], ALU.add)
                dve.drain()

            def acc_done():
                dve.sem_inc(acc_ready, 1)

            def ffn_cut(f, down, base):
                def cut(i, jj, j):
                    slot = (base + jj) % 2
                    g, buf = group(f, down, i, jj, j)
                    n = tiles_in(down, j) * P
                    dve.wait_ge(w_hi_ready, g + 1)
                    tt(WL_[:, buf, 0:n], W[:, slot, j * DC * P:j * DC * P + n], WH[:, buf, 0:n].bitcast(F32),
                       ALU.subtract).then_inc(w_rest_ready, 1)
                    if j == (DOWN_G if down else UP_G) - 1:
                        dve.drain().then_inc(w_free, 1)
                return cut

            def pre_norm(s):
                ffn = s % 3 != 1
                ts(AM[:, :, :], MOD[:, DC:2 * DC, :], 1.0, None, ALU.add)
                ts(GM[:, :, :], MOD[:, 2 * DC:3 * DC, :], 1.0 if s % 3 == 1 else 0.5, None, ALU.mult)
                dve.drain()
                tt(AM[:, :, :], AM[:, :, :], bcast(NPRE[:, s, :], 2, NSEQ), ALU.mult)
                tt(GM[:, :, :], GM[:, :, :], bcast(NPOST[:, s, :], 2, NSEQ), ALU.mult)
                if ffn:
                    first = ffn_cut(FFN_OF[s], False, LOADS["up", s])
                    for j in range(2):
                        first(0, 0, j)
                dst = NORMED if ffn else H
                dve.wait_ge(root_ready, 2 * s + 1)
                tt(dst[:, :, NP_:T], X[:, :, NP_:T], bcast(R[:, NP_:T], 1, DC), ALU.mult)
                dve.drain()
                tt(dst[:, :, NP_:T], dst[:, :, NP_:T], AM[:, :, 1:NSEQ], ALU.mult)
                dve.drain()
                tt(dst[:, :, NP_:T], dst[:, :, NP_:T], MOD[:, 0:DC, 1:NSEQ], ALU.add)
                dve.drain()

                def scaled(c):
                    tt(dst[:, c, 0:NP_], X[:, c, 0:NP_], R[:, 0:NP_], ALU.mult).then_inc(xr_ready, 1)

                if ffn:
                    scaled(0)
                    scaled(1)
                    for c in range(DC):
                        dve.wait_ge(hid_ready, s * DC + c + 1)
                        dve.tensor_copy(HH[:, c, :], NORMED[:, c, :])
                        dve.drain()
                        tt(HL[:, c, :], NORMED[:, c, :], HH[:, c, :].bitcast(F32), ALU.subtract)\
                            .then_inc(rest_ready, 1)
                        if c + 2 < DC:
                            scaled(c + 2)
                else:
                    for c in range(DC):
                        scaled(c)
                    fence()

            def post_norm(s):
                dve.wait_ge(root_ready, 2 * s + 2)
                tt(Y[:, :, NP_:T], Y[:, :, NP_:T], GM[:, :, 1:NSEQ], ALU.mult)
                dve.drain()
                tt(Y[:, :, NP_:T], Y[:, :, NP_:T], bcast(R[:, NP_:T], 1, DC), ALU.mult)
                for c in range(0, DC, 2):
                    for cc in range(c, c + 2):
                        stt(Y[:, cc, 0:NP_], Y[:, cc, 0:NP_], GM[:, cc, 0:1], R[:, 0:NP_], ALU.mult, ALU.mult)
                    dve.drain()
                    for cc in range(c, c + 2):
                        tt(X[:, cc, :], X[:, cc, :], Y[:, cc, :], ALU.add).then_inc(x_ready, 1)

            def ffn_up(s, f):
                def finish(i, jj):
                    n = i * 2 + jj
                    dve.wait_ge(silu_ready, n + (f * FC + 1))
                    gu = SILU[:, jj, :]
                    tt(two(gu), pair(4 * jj + 2), two(gu), ALU.mult).then_inc(gu_taken, 1)
                    dve.drain()
                    dve.tensor_copy(GB[:, n, :], gu)
                    dve.tensor_copy(GH_[:, n, :], gu)
                    dve.drain()
                    tt(GL[:, n, :], gu, GH_[:, n, :].bitcast(F32), ALU.subtract)
                staggered(dve, False, ffn_cut(f, False, LOADS["up", s]), finish,
                          cut_next=ffn_cut(f, True, LOADS["down", s]))
                fence()

            def ffn_down(s, f):
                def begin(i, jj):
                    if s < 5:
                        mod_copy(s + 1, i, jj)

                def finish(i, jj):
                    if s < 5:
                        mod_bias(s + 1, i, jj)
                    add_squares(s, i, jj)
                clear_sum()
                staggered(dve, True, ffn_cut(f, True, LOADS["down", s]), finish, begin)
                acc_done()
                fence()

            def sigmoid(e):
                ts(e, e, 1.0, None, ALU.add)
                dve.drain()
                dve.reciprocal(e, e)
                dve.drain()

            def hgrn():
                dve.wait_ge(vec_in, 64)
                tt(LMX, LB[:, 0, :], LB[:, 1, :], ALU.max)
                dve.drain()
                tt(LMX, LMX, LB[:, 2, :], ALU.max)
                dve.drain()
                tt(LB, LB, bcast(LMX, 1, 3), ALU.subtract).then_inc(lb_exp, 1)
                dve.wait_ge(lb_exp, 2)
                tt(LMX, LB[:, 0, :], LB[:, 1, :], ALU.add)
                dve.drain()
                tt(LMX, LMX, LB[:, 2, :], ALU.add)
                dve.drain()
                dve.reciprocal(LMX, LMX)
                dve.drain()
                tt(HVEC[:, 0, :], LB[:, 0, :], LMX, ALU.mult)
                dve.drain()
                ts(HVEC[:, 1, :], HVEC[:, 0, :], -1.0, 1.0, ALU.mult, ALU.add)
                fence()
                with dve.Fori(0, HG) as h:
                    dve.tensor_copy(HP, HVEC[:, :, h])
                    dve.wait_ge(h_exp, h * 3 + 1)
                    ts(E2, E2, 1e30, None, ALU.min)
                    dve.drain()
                    dve.tensor_copy(E2R, E2)
                    dve.drain()
                    sigmoid(E2R)
                    ts(FG, E2R, HP[:, 1:2], HP[:, 0:1], ALU.mult, ALU.add).then_inc(h_f, 1)
                    stt(KK, E2, HP[:, 1:2], E2R, ALU.mult, ALU.mult)
                    dve.wait_ge(h_lf, h + 1)
                    dve.tensor_copy(EB, BB)
                    dve.drain()
                    dve.tensor_tensor_scan(BB, const("reset"), EB, 0.0, ALU.mult, ALU.add)
                    dve.drain().then_inc(h_d, 1)
                    B4 = BB.rearrange("p (a b) -> p a b", b=CH)
                    tt(KD.rearrange("p (a b) -> p a b", b=CH), B4[:, :, CH - 1:CH].to_broadcast([P, NCH, CH]), B4,
                       ALU.subtract).then_inc(h_d, 1)
                    for n, m in enumerate(LEVELS):
                        b = BB.rearrange("p (a c b) -> p a c b", c=2, b=m)
                        d = DL[:, n, :].rearrange("p (a c b) -> p a c b", c=2, b=m)
                        ref = b[:, :, 0, m - 1:m].to_broadcast([P, NP_ // (2 * m), m])
                        tt(d[:, :, 1, :], b[:, :, 1, :], ref, ALU.subtract)
                        tt(d[:, :, 0, :], ref, b[:, :, 0, :], ALU.subtract).then_inc(h_d, 1)
                    dve.wait_ge(h_exp, h * 3 + 2)
                    dve.wait_ge(h_ex, h * 9 + 1)
                    tt(QI, QS[:, 0:NP_], EB, ALU.mult)
                    dve.wait_ge(h_exp, h * 3 + 3)
                    dve.wait_ge(h_ex, h * 9 + 2)
                    tt(KD, KD, KK[:, 0:NP_], ALU.mult).then_inc(h_kd, 1)
                    for n, m in enumerate(LEVELS):
                        dve.wait_ge(h_ex, h * 9 + (3 + n))
                        d = DL[:, n, :].rearrange("p (a c b) -> p a c b", c=2, b=m)
                        q = QS[:, 0:NP_].rearrange("p (a c b) -> p a c b", c=2, b=m)
                        k = KK[:, 0:NP_].rearrange("p (a c b) -> p a c b", c=2, b=m)
                        tt(d[:, :, 1, :], d[:, :, 1, :], q[:, :, 1, :], ALU.mult)
                        tt(d[:, :, 0, :], d[:, :, 0, :], k[:, :, 0, :], ALU.mult).then_inc(h_qk, 1)
                    dve.wait_ge(s_loaded, h * 16 + 16)
                    dve.wait_ge(h_vb, h + 1)
                    tt(S0, S0, bcast(FG[:, NP_:T], 2, P), ALU.mult)
                    for b in range(2):
                        tt(VK[:, 4 * b:4 * b + 4, :], PS[:, 6 + b, :].rearrange("p (a b) -> p a b", a=4),
                           bcast(KK[:, NP_ + 4 * b:NP_ + 4 * b + 4], 2, P), ALU.mult)
                    dve.drain().then_inc(h_vk, 1)
                    tt(S0, S0, VK, ALU.add).then_inc(s_new, 1)
                    ident = bcast(IDENT, 1, NCH)
                    for n in range(1 + len(LEVELS)):
                        dve.wait_ge(h_p, h * 8 + (n + 1))
                        src = PS[:, n % 4, :].rearrange("p (a b) -> p a b", a=NCH)
                        if n == 0:
                            tt(AT, src, ident, ALU.mult).then_inc(h_ptk, 1)
                            dve.drain()
                        else:
                            apart(dve)
                            dve.copy_predicated(AT, bcast(MSK[:, n - 1, :], 1, NCH), src).then_inc(h_ptk, 1)
                            dve.drain()
                    dve.sem_inc(h_att, 1)
                    dve.wait_ge(h_u, h + 1)
                    dve.wait_ge(s_stored, h + 1)
                    dve.tensor_copy(ST[:, 0, :], PS[:, 5, 0:P])
                    for c in range(1, NCH):
                        dve.drain()
                        stt(ST[:, c, :], ST[:, c - 1, :], EB[:, (c + 1) * CH - 1:(c + 1) * CH],
                            PS[:, 5, c * P:(c + 1) * P], ALU.mult, ALU.add)
                    dve.drain().then_inc(h_s, 1)
                    dve.wait_ge(h_r, h + 1)
                    tt(R[:, 0:NP_], R[:, 0:NP_], PS[:, 6, :], ALU.mult)
                    tt(R[:, NP_:T], R[:, NP_:T], PS[:, 7, 0:NB], ALU.mult)
                    dve.drain()
                    stt(OC[:, h, :], R[:, :], HP[:, 2:3], GS, ALU.mult, ALU.mult)
                    dve.drain().then_inc(h_done, 1)
                dve.wait_ge(s_stored, HG + 1)
                fence()

            def ssm():
                fence()
                dve.wait_ge(g_in, 80)
                dve.wait_ge(d_pe, 1)
                ts(two(DTV), pair(0, rows=16), SMS[:, 0:1], None, ALU.add)
                dve.drain()
                ts(DTE, DTV, -1.0, None, ALU.mult)
                dve.drain()
                tt(DTE, DTE, DTV, ALU.max).then_inc(d_step, 1)
                dve.wait_ge(d_act, 1)
                ts(SMS[:, 2:3], SMS[:, 2:3], -1.0, None, ALU.mult)
                ts(DTE, DTE, 1.0, None, ALU.add).then_inc(d_step, 1)
                dve.wait_ge(d_act, 2)
                stt(DT, DTV, 0.0, DTE, ALU.max, ALU.add)
                dve.drain()
                ts(DTV, DT, SMS[:, 2:3], None, ALU.mult)
                dve.drain().then_inc(d_step, 1)
                dve.tensor_tensor_scan(LA[:, 0:NP_], const("reset", 16), DTV[:, 0:NP_], 0.0, ALU.mult, ALU.add)
                dve.tensor_copy(LA[:, NP_:T], DTV[:, NP_:T])
                dve.drain().then_inc(d_step, 1)
                fence()
                dve.sem_inc(g_done, 1)
                with dve.Fori(0, SG_) as g:
                    dve.tensor_copy(CWG, CW[:, g])
                    dve.tensor_copy(DSN[:, 0:2], DSK[:, g])
                    dve.tensor_copy(DSN[:, 2:4], SNW[:, g])
                    dve.tensor_copy(DTG, DTT[:, :, bass.ds(g * GH, GH)])
                    dve.tensor_copy(BTG, BT[:, :, bass.ds(g * GH, GH)])
                    dve.tensor_copy(DTSG, DTS[:, bass.ds(g * GH, GH)])
                    dve.tensor_copy(SELG.rearrange("p a b -> p (a b)"), const("sel16", 16)[:, bass.ds(g * (GH * P), GH * P)])
                    dve.drain().then_inc(g_sel, 1)
                    dve.wait_ge(st_in, g * 32 + 32)
                    for c in range(4):
                        dve.wait_ge(g_raw, g * 4 + (c + 1))
                        ts(CV[:, c, :], XR[:, c, :], CWG[:, c, 3:4], CWG[:, c, 4:5], ALU.mult, ALU.add)
                        for tap in range(3):
                            dve.drain()
                            d = 3 - tap
                            stt(CV[:, c, d:NP_], XR[:, c, 0:NP_ - d], CWG[:, c, tap:tap + 1], CV[:, c, d:NP_],
                                ALU.mult, ALU.add)
                            stt(CV[:, c, NP_:T], STC[:, c, tap, :], CWG[:, c, tap:tap + 1], CV[:, c, NP_:T],
                                ALU.mult, ALU.add)
                    dve.drain().then_inc(g_conv, 1)
                    dve.wait_ge(g_tr, g + 1)
                    for x in range(2):
                        tt(XD[:, 2 * x:2 * x + 2], PS[:, 4 + x, :].rearrange("p (a b c) -> p a b c", a=2, b=GH),
                           bcast(DTG[:, 2 * x:2 * x + 2, :], 3, HD), ALU.mult)
                    tt(XDS.rearrange("p (a b) -> p a b", a=GH), PS[0:NB, 7, 0:GH * HD].rearrange("p (a b) -> p a b", a=GH),
                       bcast(DTSG, 2, HD), ALU.mult)
                    dve.drain().then_inc(g_xt, 1)
                    dve.wait_ge(g_cb, g + 1)
                    tt(CBM, PS[:, 6, :].rearrange("p (a b) -> p a b", a=NCH), bcast(const("causal"), 1, NCH), ALU.mult)
                    dve.wait_ge(g_bcx, g * 4 + 4)
                    last_b = PS[:, 0:GH, CH - 1:NP_:CH]
                    dve.tensor_copy(EL, last_b)
                    tt(WL, last_b, BTG.rearrange("p a b -> p b a"), ALU.subtract)
                    dve.drain().then_inc(g_wl, 1)
                    for j in range(GH):
                        for c in range(NCH):
                            cc = slice(c * CH, (c + 1) * CH)
                            last = ts(SEG[:, j, cc], PS[:, j, cc], BTG[:, c, j:j + 1], 0.0, ALU.subtract, ALU.min)
                        last.then_inc(g_seg, 1)
                    dve.drain().then_inc(g_bcfree, 1)
                    dve.wait_ge(g_wle, g + 1)
                    for c in range(NCH):
                        tt(XW[:, c], XD[:, c], bcast(WL[:, :, c], 2, HD), ALU.mult)
                    dve.drain().then_inc(g_xw, 1)
                    for j in range(GH):
                        tt(CEX[:, j, :], CEX[:, j, :], CV[:, 3, 0:NP_], ALU.mult)
                        dve.wait_ge(g_sege, g * 4 + (j + 1))
                        tt(SEG[:, j, :], SEG[:, j, :], CBM.rearrange("p a b -> p (a b)"), ALU.mult).then_inc(g_m, 1)
                    dve.wait_ge(g_u, g + 1)
                    u = [PS[:, 4 + c // 2, (c % 2) * 256:(c % 2 + 1) * 256].rearrange("p (a b) -> p a b", a=GH)
                         for c in range(NCH)]
                    dve.tensor_copy(SS[:, 0], u[0])
                    for c in range(1, NCH):
                        dve.drain()
                        tt(SS[:, c], SS[:, c - 1], bcast(EL[:, :, c], 2, HD), ALU.mult)
                        dve.drain()
                        tt(SS[:, c], SS[:, c], u[c], ALU.add)
                    dve.drain().then_inc(g_s, 1)
                    for j in range(GH):
                        tt(SM0[:, :, j, :], SM0[:, :, j, :], bcast(EA[:, j, :], 2, HD), ALU.mult)
                    dve.drain().then_inc(g_uu, 1)
                    dve.wait_ge(g_xb, g + 1)
                    for b in range(NB):
                        stt(SM0[:, b].rearrange("p a b -> p (a b)"), PS[:, b // 2, (b % 2) * 256:(b % 2 + 1) * 256],
                            CV[:, 2, NP_ + b:NP_ + b + 1], SM0[:, b].rearrange("p a b -> p (a b)"), ALU.mult, ALU.add)
                    dve.drain().then_inc(g_uu, 1)
                    dve.wait_ge(g_y, g * 2 + 2)
                    for x in range(2):
                        stt(EV[:, x, 0:NP_], CV[:, x, 0:NP_], DSN[:, x:x + 1], PS[:, 6 + x, :], ALU.mult, ALU.add)
                        stt(EV[:, x, NP_:T], CV[:, x, NP_:T], DSN[:, x:x + 1], PS[:, 4, x * NB:(x + 1) * NB],
                            ALU.mult, ALU.add)
                    dve.drain()
                    tt(EV[:, 0:2, :], EV[:, 0:2, :], GZ, ALU.mult)
                    dve.drain().then_inc(g_yv, 1)
                    dve.wait_ge(g_r, g + 1)
                    for x in range(2):
                        stt(OC[:, g * 2 + (HG + x), :], EV[:, x, :], DSN[:, 2 + x:3 + x], R[:, :], ALU.mult, ALU.mult)
                    dve.drain().then_inc(g_done, 1)
                dve.wait_ge(st_ok, SG_ + 1)
                fence()

            def mla():
                dve.wait_ge(m_root, 1)
                dve.wait_ge(m_cks, 48)
                for c in range(4):
                    stt(CQ[:, c, :], CQ[:, c, :], GQ[:, c:c + 1], R[:, :], ALU.mult, ALU.mult)
                dve.drain().then_inc(m_norm, 1)
                dve.wait_ge(m_root, 2)
                for c in range(RC):
                    stt(CKV[:, c, :], CKV[:, c, :], GKV[:, c:c + 1], R[:, :], ALU.mult, ALU.mult)
                dve.drain().then_inc(m_norm, 1)
                dve.wait_ge(m_perm, 1)
                rotate(KPE).then_inc(m_norm, 1)
                fence()
                with dve.Fori(0, MH // 4) as i:
                    for jj in range(2):
                        n = i * 2 + jj
                        dve.wait_ge(p_ql, n + 1)
                        dve.tensor_copy(QL[:, :, bass.ds(n * 2, 2), :].rearrange("p r h b -> p h r b"),
                                        PS[:, 2, 0:4 * NB].rearrange("p (h r b) -> p h r b", h=2, r=RC))\
                           .then_inc(p_qlt, 1)
                        rotate(QP).then_inc(p_qp, 1)
                        dve.drain()
                        for hh in range(2):
                            dve.tensor_copy(QPS[:, n * 2 + hh, :], QP[hh * ROPE:(hh + 1) * ROPE, NP_:T])
                        for hh in range(2):
                            for qb in range(4):
                                nk = (qb + 1) * P
                                dve.wait_ge(p_sc, n * 8 + (hh * 4 + qb + 1))
                                s = PS[:, 4 * hh + qb, 0:nk]
                                tt(s[:, qb * P:nk], s[:, qb * P:nk], const("neg"), ALU.add)
                                dve.drain()
                                dve.reduce_max(SMX[:, hh, qb:qb + 1], s, AX_X)
                                dve.drain()
                                ts(SNB[:, hh, qb:qb + 1], SMX[:, hh, qb:qb + 1], -SCALE, None, ALU.mult)\
                                    .then_inc(p_mx, 1)
                        for hh in range(2):
                            for qb in range(4):
                                nk = (qb + 1) * P
                                dve.wait_ge(p_pr, n * 8 + (hh * 4 + qb + 1))
                                dve.reciprocal(SRI[:, hh, qb:qb + 1], SRS[:, hh, qb:qb + 1])
                                dve.drain()
                                ts(PR[:, hh, qb, 0:nk], PR[:, hh, qb, 0:nk], SRI[:, hh, qb:qb + 1], None, ALU.mult)\
                                    .then_inc(p_pn, 1)
                fence()
                for buf, value in ((QLB, 0.0), (QPB, 0.0), (DST[:, 1:2], NEG), (DST[:, 5:6], 0.0)):
                    dve.memset(buf, value)
                dve.drain()
                with dve.Fori(0, NB) as b:
                    dve.tensor_copy(QLB[:, :, 0:MH], QL[:, :, :, b])
                    dve.tensor_copy(QPB[0:ROPE, 0, 0:MH], QPS[:, :, b])
                    dve.tensor_copy(QPB[ROPE:P, 1, 0:MH], QPS[:, :, b])
                    dve.drain().then_inc(b_q, 1)
                    dve.wait_ge(b_sc, b + 1)
                    dve.reduce_max(DST[:, 0:1], PS[:, 0, :], AX_X)
                    tt(PDO, PS[0:QR_, 1, 0:NB], const("own", QR_)[:, bass.ds(b * NB, NB)], ALU.add)
                    dve.drain()
                    dve.reduce_max(DST[0:QR_, 1:2], PDO, AX_X)
                    dve.drain()
                    tt(DST[:, 2:3], DST[:, 0:1], DST[:, 1:2], ALU.max).then_inc(b_m, 1)
                    dve.wait_ge(b_mt, b * 2 + 1)
                    dve.reduce_max(ROW[:, 0:QR_], PS[0:1, 2, 0:P].rearrange("p (a b) -> p b a", a=QUARTERS), AX_X)
                    dve.drain()
                    ts(ROW[:, QR_:QR_ + P].rearrange("p (a b) -> p a b", a=QUARTERS),
                       bcast(ROW[:, 0:QR_], 1, QUARTERS), -SCALE, None, ALU.mult).then_inc(b_m, 1)
                    dve.wait_ge(b_mt, b * 2 + 2)
                    dve.tensor_copy(DST[:, 3:4], PS[:, 3, 0:1]).then_inc(b_mx, 1)
                    dve.wait_ge(b_ex, b + 1)
                    tt(DST[:, 6:7], DST[:, 4:5], DST[:, 5:6], ALU.add).then_inc(b_sum, 1)
                    dve.wait_ge(b_tot, b + 1)
                    dve.reciprocal(DST[:, 7:8], PS[:, 7, 0:1])
                    dve.drain()
                    dve.wait_ge(b_o, b + 1)
                    ts(OP, PS[:, 6, 0:RC * P], DST[:, 7:8], None, ALU.mult).then_inc(b_on, 1)
                    dve.wait_ge(b_oc, b + 1)
                    dve.tensor_copy(OL[:, :, :, b], PS[:, 7, MH:MH + RC * MH].rearrange("p (a b) -> p a b", a=RC))
                fence()
                dve.wait_ge(out_stored, 32 * HG + 32)
                fence()

            def rotate(dst):
                bank = 2 if dst is KPE else 0
                tt(two(TMP), pair(bank), two(const("sin")), ALU.mult)
                tt(dst, QR, const("cos"), ALU.mult)
                dve.drain()
                return tt(dst, dst, TMP, ALU.add)

            dve.wait_ge(const_in, 112)
            dve.wait_ge(c_exp, 1)
            dve.memset(CS[:, :, :], 0.0)
            sigmoid(CE)
            tt(CS[:, :, 0:NSEQ], CR, CE, ALU.mult).then_inc(c_exp, 1)
            modulation(0)
            pre_norm(0)
            for s in range(6):
                if s == 1:
                    hgrn()
                    ssm()
                elif s == 4:
                    mla()
                else:
                    ffn_up(s, FFN_OF[s])
                    ffn_down(s, FFN_OF[s])
                if s % 3 == 1:
                    clear_sum()
                    modulation(s + 1)
                post_norm(s)
                if s < 5:
                    pre_norm(s + 1)
            fence()


def _tiled(w, k, n):
    return w.reshape(k, P, n, P).transpose(2, 1, 0, 3)


def _lay_out(v):
    cat = np.concatenate
    c = np.ascontiguousarray
    out = {}
    out["const"], out["mixer_const"], out["masks"] = constants()
    x = cat([v["x_prompt"][0], v["x_sample"][:, 0]])
    out["x"] = x.T.reshape(DC, P, T).transpose(1, 0, 2)
    out["c"] = cat([v["c_prompt"], v["c_sample"]]).T.reshape(DC, P, NSEQ).transpose(1, 0, 2)
    out["ada_w"] = v["ada_w"].reshape(2, DC, P, 24, 3 * P).transpose(0, 3, 2, 1, 4).reshape(48, P, 3 * DC * P)
    out["ada_b"] = v["ada_b"].reshape(6, NMOD, P).transpose(2, 0, 1)
    out["norm_pre"] = v["norm_pre"].reshape(6, DC, P).transpose(2, 0, 1)
    out["norm_post"] = v["norm_post"].reshape(6, DC, P).transpose(2, 0, 1)
    g, u = (v[n].reshape(4, DC, P, FC, P).transpose(0, 3, 2, 1, 4).reshape(4 * FC, P, DC * P)
            for n in ("ffn_wg", "ffn_wu"))
    out["ffn_gu"] = cat([g, u], axis=2)
    out["ffn_wd"] = v["ffn_wd"].reshape(4, FC, P, DC, P).transpose(0, 3, 2, 1, 4).reshape(4 * DC, P, FC * P)
    w = v["w_in_ab"]
    q, f, i, gate = (_tiled(w[:, n * 1024:(n + 1) * 1024], DC, HG) for n in range(4))
    z = _tiled(w[:, 4096:5120], DC, DC)
    xs = _tiled(w[:, 5120:6144], DC, DC)
    b = _tiled(w[:, 6144:6656], DC, SG_)
    cc = _tiled(w[:, 6656:7168], DC, SG_)
    out["w_hgrn"] = np.stack([cat([q, f], axis=2), cat([i, gate], axis=2)], axis=1).reshape(2 * HG, P, 2 * DC * P)
    out["w_ssm"] = np.stack([cat([xs[0::2], xs[1::2], b], axis=2), cat([cc, z[0::2], z[1::2]], axis=2)],
                            axis=1).reshape(2 * SG_, P, 3 * DC * P)
    out["w_dt"] = w[:, 7168:].reshape(DC, P, 16).transpose(1, 0, 2)
    out["w_out_ab"] = _tiled(v["w_out_ab"], 16, DC).reshape(DC, P, 16 * P)
    out["lb_logits"] = v["hg_lb_logits"].reshape(3, HG, P).transpose(2, 0, 1)
    out["hg_norm"] = v["hg_norm"].reshape(HG, P).T
    out["state_hgrn"] = v["state_hgrn"].transpose(1, 2, 0, 3)
    out["ssm_small"] = np.stack([v["ssm_dt_bias"], v["ssm_a_log"]], axis=1)

    def channels(a):
        n = a.shape[0]
        xs = a[:, :1024].reshape(n, SG_, 2, P)
        bc = a[:, 1024:].reshape(n, 2, SG_, P).transpose(0, 2, 1, 3)
        return cat([xs, bc], axis=2).transpose(1, 3, 2, 0)

    out["conv_w"] = cat([channels(v["ssm_conv_w"]), channels(v["ssm_conv_b"][None])], axis=3).transpose(1, 0, 2, 3)
    out["state_conv"] = channels(v["state_conv"].reshape(NB * 3, 2048)).reshape(SG_, P, 4, NB, 3).transpose(0, 1, 2, 4, 3)
    out["state_ssm"] = v["state_ssm"].reshape(NB, SG_, GH, P, HD).transpose(1, 3, 0, 2, 4)
    out["ssm_d"] = np.repeat(v["ssm_d"], HD).reshape(SG_, 2, P).transpose(2, 0, 1)
    out["ssm_norm"] = v["ssm_norm"].reshape(SG_, 2, P).transpose(2, 0, 1)
    out["mla_dq"] = _tiled(v["mla_w_dq"], DC, 4).reshape(2, 2, P, DC * P).transpose(0, 2, 1, 3)
    dkv = v["mla_w_dkv"]
    kpe = dkv[:, 256:].reshape(DC, P, ROPE).transpose(1, 0, 2)
    out["mla_dkv"] = cat([_tiled(dkv[:, :256], DC, RC).transpose(1, 0, 2, 3).reshape(P, 2 * DC, P),
                          cat([kpe, kpe], axis=2)], axis=1)
    uq = v["mla_w_uq"].reshape(4, P, 8, 2, 192)
    nope = uq[..., :128].transpose(2, 1, 3, 0, 4).reshape(8, P, -1)
    rope = uq[..., 128:].transpose(2, 1, 0, 3, 4).reshape(8, P, -1)
    uk = v["mla_w_uk"].reshape(RC, P, 8, 2, P)
    ukn = uk.transpose(2, 1, 3, 0, 4).reshape(8, P, -1)
    ukt = v["mla_w_uk"].reshape(256, 8, 2, P).transpose(1, 3, 2, 0).reshape(8, P, -1)
    uv = v["mla_w_uv"].reshape(RC, P, 8, 2, P).transpose(2, 1, 0, 3, 4).reshape(8, P, -1)
    out["mla_pairs"] = cat([nope, rope, ukn, uv, ukt], axis=2)
    out["mla_uv"] = v["mla_w_uv"].reshape(RC, P, 2, 8 * P).transpose(2, 1, 0, 3).reshape(2, P, 16 * P)
    out["mla_wo"] = _tiled(v["mla_w_o"], 16, DC).reshape(DC, P, 16 * P)
    out["mla_gq"] = v["mla_g_q"].reshape(4, P).T
    out["mla_gkv"] = v["mla_g_kv"].reshape(RC, P).T
    n_phys = v["cache_ckv"].shape[0]
    latent_t = v["cache_ckv"].reshape(n_phys, PAGE, RC, P).transpose(0, 3, 2, 1).reshape(n_phys, P, RC * PAGE)
    rope_t = v["cache_kpe"].reshape(n_phys, 2, 64, ROPE).transpose(0, 1, 3, 2).reshape(n_phys, P, 64)
    out["pages"] = cat([latent_t, v["cache_ckv"], rope_t], axis=2)
    out["page_table"] = v["page_table"].reshape(1, -1)
    shapes = {"mla_dq": (2, P, 16 * P), "mla_dkv": (P, 24 * P)}
    return {n: c(a).reshape(shapes.get(n, a.shape)) for n, a in out.items()}


_OUTS = {"y": (P, DC, T), "hgrn_prompt": (HG, P, P), "hgrn_sample": (HG, P, NB, P),
         "ssm_prompt": (SG_, P, GH, HD), "ssm_sample": (SG_, P, NB, GH, HD),
         "conv_prompt": (SG_, P, 4, 3), "conv_sample": (SG_, P, 4, 3, NB), "ckv": (P, RC, T), "kpe": (ROPE, T)}


def kernel(**inputs):
    import concourse.bacc as _bacc
    from concourse import mybir as _mybir
    from concourse.bass_utils import run_bass_kernel_spmd as _run

    arrays = _lay_out({n: np.asarray(a) for n, a in inputs.items()})
    nc = _bacc.Bacc("TRN2", target_bir_lowering=False, num_devices=1)
    A = {n: nc.dram_tensor(f"in_{n}", a.shape, _mybir.dt.from_np(a.dtype), kind="ExternalInput").ap()
         for n, a in arrays.items()}
    O = {n: nc.dram_tensor(f"out_{n}", s, F32, kind="ExternalOutput").ap() for n, s in _OUTS.items()}
    build_program(nc, A, O)
    r = _run(nc, [{f"in_{n}": a for n, a in arrays.items()}], core_ids=[0]).results[0]
    o = {n: np.asarray(r[f"out_{n}"]) for n in _OUTS}

    y = o["y"].transpose(2, 1, 0).reshape(T, D)
    ckv = o["ckv"].transpose(2, 1, 0).reshape(T, RC * P)
    kpe = o["kpe"].T

    def rows(a):
        a = a.transpose(3, 0, 2, 1)
        return np.concatenate([a[:, :, 0:2].reshape(a.shape[0], -1), a[:, :, 2].reshape(a.shape[0], -1),
                               a[:, :, 3].reshape(a.shape[0], -1)], axis=1)

    conv_s = rows(o["conv_sample"].reshape(SG_, P, 4, 3 * NB)).reshape(3, NB, 2048).transpose(1, 0, 2)
    return (y[None, :NP_], y[NP_:, None],
            o["hgrn_prompt"][None], o["hgrn_sample"].transpose(2, 0, 1, 3),
            o["ssm_prompt"].transpose(0, 2, 1, 3).reshape(1, 16, P, HD),
            o["ssm_sample"].transpose(2, 0, 3, 1, 4).reshape(NB, 16, P, HD),
            rows(o["conv_prompt"])[None], conv_s,
            ckv[None, :NP_], ckv[NP_:, None], kpe[None, :NP_], kpe[NP_:, None])
```

```python
from contextlib import ExitStack

import numpy as np

import concourse.bass as bass
from concourse import mybir

F32 = mybir.dt.float32
F32R = mybir.dt.float32r
BF16 = mybir.dt.bfloat16
I32 = mybir.dt.int32
ALU = mybir.AluOpType
ACT = mybir.ActivationFunctionType
AX_X = mybir.AxisListType.X

P = 128
D = 1024
DC = D // P
NP_ = 512
NB = 8
T = NP_ + NB
HT = T // 2
FC = 2816 // P
NSEQ = 1 + NB
NMOD = 3 * DC
EPS = 1e-6
CH = 128
NCH = NP_ // CH
LEVELS = (64, 32, 16, 8, 4, 2, 1)
HG = 8
SG_ = 4
GH = 4
HD = 64
MH = 16
RC = 2
ROPE = 64
PAGE = 128
NPAGE = 16
PAST = PAGE * NPAGE
QR_ = 32
QUARTERS = P // QR_
PAGE_W = 4 * PAGE + 64
SCALE = float((128 + 64) ** -0.5)
NEG = -1e30

_COLS = {}
_WIDTH = []
for _table, _entries in enumerate((
        (("ident", P), ("ones", P), ("fold", P), ("eps", 1), ("scratch", 1)),
        (("reset", NP_), ("sel", NB * P), ("sel16", 16 * P), ("causal", P), ("neg", P), ("cos", T), ("sin", T),
         ("perm", P), ("own", NB * NB)))):
    _at = 0
    for _name, _n in _entries:
        _COLS[_name] = (_table, _at, _at + _n)
        _at += _n
    _WIDTH.append(_at)


def constants():
    tables = [np.zeros((P, n), np.float32) for n in _WIDTH]

    def put(name, a):
        t, a0, a1 = _COLS[name]
        tables[t][:a.shape[0], a0:a1] = a.reshape(a.shape[0], a1 - a0)

    r = np.arange(P)
    put("ident", np.eye(P))
    put("ones", np.ones((P, P)))
    put("eps", np.full((P, 1), EPS))
    put("reset", np.tile((np.arange(NP_) % CH != 0), (P, 1)))
    sel = np.zeros((NB, NB, P))
    sel[np.arange(NB), np.arange(NB)] = 1
    put("sel", sel)
    sel16 = np.zeros((16, 16, P))
    sel16[np.arange(16), np.arange(16)] = 1
    put("sel16", sel16)
    put("causal", (r[:, None] <= r[None, :]).astype(np.float32))
    put("neg", np.where(r[None, :] <= r[:, None], 0.0, NEG))
    half = ROPE // 2
    inv = (10000.0 ** (-np.arange(half, dtype=np.float32) / half)).astype(np.float32)
    pos = np.concatenate([np.arange(NP_), np.full(NB, PAST)]).astype(np.float32)
    ang = (inv[:, None] * pos[None]).astype(np.float32)
    put("cos", np.tile(np.cos(ang), (4, 1)))
    put("sin", np.concatenate([-np.sin(ang), np.sin(ang)] * 2))
    perm = np.zeros((P, P))
    perm[(r // ROPE) * ROPE + (r + half) % ROPE, r] = 1
    put("perm", perm)
    put("fold", (r[:, None] % QR_ == r[None, :] % QR_).astype(np.float32))
    own = np.full((QR_, NB, NB), NEG)
    own[:, np.arange(NB), np.arange(NB)] = 0
    put("own", own)
    masks = np.zeros((P, len(LEVELS), P), np.int32)
    s, u = r[:, None], r[None, :]
    for n, m in enumerate(LEVELS):
        masks[:, n] = (s // (2 * m) == u // (2 * m)) & ((s // m) % 2 == 0) & ((u // m) % 2 == 1)
    return tables[0], tables[1], masks


FFN0_DONE, HGRN_DONE, FFN3_DONE = 3, 5, 12

WS = 24
LOADS = {}


def _plan():
    LOADS["mod"] = 0
    n = NMOD // 3
    for layer in range(2):
        for sub in range(3):
            s = layer * 3 + sub
            if sub != 1:
                LOADS["up", s] = n
                n += FC
            elif layer == 0:
                LOADS["hgrn"] = n
                n += 2 * HG
                LOADS["ssm"] = n
                n += 2 * SG_
            else:
                LOADS["latent"] = n
                n += 3
                LOADS["pairs"] = n
                n += MH // 2
                LOADS["uv"] = n
                n += 2
            LOADS["down", s] = n
            n += DC
    return n


_plan()


def build_program(nc, A, O):
    ctx = ExitStack()
    with ctx:
        def sb(name, shape, dt=F32):
            return ctx.enter_context(nc.sbuf_tensor(name, shape, dt))

        def shared(name, width, *layouts):
            seen = []
            for layout in layouts:
                with ExitStack() as inner:
                    seen.append([inner.enter_context(nc.sbuf_tensor(n, shape, dt)) for n, shape, dt in layout])
            return [sb(name, [P, width])] + seen

        def sem(name):
            return ctx.enter_context(nc.semaphore(name))

        PS = ctx.enter_context(nc.psum_tensor("PS", [P, 8, 512], F32))

        CT = sb("consts", [P, _WIDTH[0]])
        X = sb("residual", [P, DC, T])
        H, (HB, HL), (OCL,) = shared("hidden", DC * T, [("hid_bf", [P, DC, T], BF16), ("hid_rest", [P, DC, T], BF16)],
                                    [("heads_rest", [P, 2 * DC, T], BF16)])
        Y, (HH,) = shared("sub_out", DC * T, [("hid_hi", [P, DC, T], F32R)])
        H, Y = (t[:, :].rearrange("p (a b) -> p a b", a=DC) for t in (H, Y))
        R = sb("inv_rms", [P, T])
        MOD = sb("modulation", [P, NMOD, NSEQ])
        AM = sb("pre_scale", [P, DC, NSEQ])
        GM = sb("post_scale", [P, DC, NSEQ])
        CS = sb("silu_c", [P, DC, QR_])
        W = sb("weight_ring", [P, 2, WS * P])
        AD, (GWH, GWB) = shared("ada_chunks", 3 * DC * P,
                                [("hgrn_w_hi", [P, 2, DC * P], F32R), ("hgrn_w_bf", [P, 2, DC * P], BF16)])
        ADB = sb("ada_bias", [P, 6, NMOD])
        NPRE = sb("norm_pre", [P, 6, DC])
        NPOST = sb("norm_post", [P, 6, DC])
        HGRN_END = 18304
        PARTS, (WH, WB, WL_, SILU), (CT2, MSK) = shared(
            "weight_parts", _WIDTH[1] + len(LEVELS) * P,
            [("w_hi", [P, 2, DC * P], F32R), ("w_bf", [P, 2, DC * P], BF16), ("w_rest", [P, 2, DC * P], BF16),
             ("gate", [P, 2, T], F32)],
            [("mixer_consts", [P, _WIDTH[1]], F32), ("level_masks", [P, len(LEVELS), P], I32)])
        BIG, (GH_, GB, GL, MST), (_, OCH, OCB, SQ), (_, GHH, _, GHB, GHL, GWL) = shared(
            "arena", 23600,
            [("gu_hi", [P, FC, T], F32R), ("gu_bf", [P, FC, T], BF16), ("gu_rest", [P, FC, T], BF16),
             ("mod_space", [P, 3 * P + 2 * DC * NSEQ], F32)],
            [("heads", [P, 2 * DC, T], F32), ("heads_hi", [P, 2 * DC, T], F32R), ("heads_bf", [P, 2 * DC, T], BF16),
             ("squares", [P, 2, T], F32)],
            [("hgrn_heads", [P, DC, T], F32), ("hgrn_in_hi", [P, DC, T], F32R),
             ("hgrn_space", [P, HGRN_END - 2 * DC * T], F32), ("hgrn_in_bf", [P, DC, T], BF16),
             ("hgrn_in_rest", [P, DC, T], BF16), ("hgrn_w_rest", [P, 2, DC * P], BF16)])

        def const(name, rows=P):
            table, a0, a1 = _COLS[name]
            return (CT, CT2)[table][0:rows, a0:a1]

        IDENT, ONES = const("ident"), const("ones")

        class Arena:

            def __init__(self, t, start=0):
                self.t, self.at = t, start

            def take(self, *shape, rows=P):
                n = int(np.prod(shape))
                ap = self.t[0:rows, self.at:self.at + n]
                self.at += n
                assert self.at <= self.t.shape[1], self.at
                if len(shape) == 1:
                    return ap
                names = "abcd"[:len(shape)]
                return ap.rearrange(f"p ({' '.join(names)}) -> p {' '.join(names)}",
                                    **{k: v for k, v in zip(names, shape)})

        NORMED = Arena(BIG).take(DC, T)
        ar = Arena(MST)
        MS = ar.take(3 * P)
        CR = ar.take(DC, NSEQ)
        CE = ar.take(DC, NSEQ)
        ar = Arena(BIG)
        OC = ar.take(16, T)
        mix0 = ar.at
        LB = ar.take(3, HG)
        LMX = ar.take(HG)
        HVEC = ar.take(3, HG)
        HP = ar.take(3)
        E2 = ar.take(T)
        QS, KK, FG, GS = ar.take(T), ar.take(T), ar.take(T), ar.take(T)
        E2R = ar.take(T)
        BB = ar.take(NP_)
        KD = ar.take(NP_)
        KDT = ar.take(NCH, P)
        EB = ar.take(NP_)
        QI = ar.take(NP_)
        VV = ar.take(NCH, P)
        VS = ar.take(P, rows=NB)
        AT = ar.take(NCH, P)
        ST = ar.take(NCH, P)
        SQO = ar.take(T)
        VF = SQO
        assert ar.at <= HGRN_END - 2 * NB * P
        yar = Arena(Y.rearrange("p a b -> p (a b)"))
        DL = yar.take(len(LEVELS), NP_)
        S0 = ar.take(NB, P)
        VK = ar.take(NB, P)
        assert ar.at <= HGRN_END
        ar = Arena(BIG, mix0)
        CW = ar.take(SG_, 4, 5)
        CWG = ar.take(4, 5)
        DSK = ar.take(SG_, 2)
        SNW = ar.take(SG_, 2)
        DSN = ar.take(4)
        DTW = ar.take(DC, 16)
        SMS = ar.take(4, rows=16)
        DT = ar.take(T, rows=16)
        LA = ar.take(T, rows=16)
        DTT = ar.take(NCH, 16)
        BT = ar.take(NCH, 16)
        DTS = ar.take(16, rows=NB)
        DTG = ar.take(NCH, GH)
        BTG = ar.take(NCH, GH)
        DTSG = ar.take(GH, rows=NB)
        SELG = ar.take(GH, P, rows=16)
        XR = ar.take(4, T)
        DTV, DTE = XR[0:16, 0, :], XR[0:16, 1, :]
        CV = ar.take(4, T)
        STC = ar.take(4, 3, NB)
        GZ = ar.take(2, T)
        XD = ar.take(NCH, GH, HD)
        XW = ar.take(NCH, GH, HD)
        XDS = ar.take(GH * HD, rows=NB)
        BTK = ar.take(NCH, P)
        CBM = ar.take(NCH, P)
        WL = ar.take(GH, NCH)
        EL = ar.take(GH, NCH)
        EA = ar.take(GH, NB)
        SS = ar.take(NCH, GH, HD)
        EV = ar.take(4, T)
        SEG = EV[:, :, 0:NP_]
        yar = Arena(Y.rearrange("p a b -> p (a b)"))
        SM0 = yar.take(NB, GH, HD)
        CEX = yar.take(GH, NP_)
        SUU = CV[:, 0:2, :]
        ar = Arena(BIG, mix0)
        GQ = ar.take(4)
        GKV = ar.take(RC)
        CKV = ar.take(RC, T)
        KPE = ar.take(T)
        QL = ar.take(RC, MH, NB)
        QPS = ar.take(MH, NB, rows=ROPE)
        OL = ar.take(RC, MH, NB)
        CKVS = ar.take(RC, P, rows=NB)
        mla0 = ar.at
        CQ = Y[:, 0:4, :]
        TMP = ar.take(T)
        QR = ar.take(T)
        QP = ar.take(T)
        QN = ar.take(2, T)
        KN = ar.take(2, NP_)
        VT = ar.take(NCH, 2, P)
        PR = ar.take(2, 4, NP_)
        PTR = ar.take(2, 10 * P)

        def keys_of(hh, kb):
            start = (4 * kb - kb * (kb - 1) // 2) * P
            return PTR[:, hh, start:start + NP_ - kb * P]

        SMX = ar.take(2, 4)
        SNB = ar.take(2, 4)
        SRS = ar.take(2, 4)
        SRI = ar.take(2, 4)
        ar = Arena(BIG, mla0)
        QLB = ar.take(RC, QR_)
        QPB = ar.take(2, QR_)
        PTD = ar.take(4, P)
        PTO = ar.take(QR_, rows=NB)
        DST = ar.take(8)
        ROW = ar.take(QR_ + P, rows=1)
        PD = ar.take(4, PAGE)
        PDO = ar.take(NB, rows=QR_)
        OP = ar.take(RC * P)
        har = Arena(H.rearrange("p a b -> p (a b)"))
        yar = Arena(Y.rearrange("p a b -> p (a b)"))
        PAGES = [[ar.take(PAGE_W) for _ in range(NPAGE)],
                 [har.take(PAGE_W) for _ in range(7)] + [yar.take(PAGE_W) for _ in range(7)]
                 + [ar.take(PAGE_W) for _ in range(2)]]
        TABLE = sb("page_table", [1, NB * NPAGE], I32)

        stage_done = sem("stage_done")
        const_in = sem("const_in")
        wait_passed = sem("wait_passed")
        w_arrived = [sem("w_arrived0"), sem("w_arrived1")]
        w_free = sem("w_free")
        ada_arrived = sem("ada_arrived")
        mod_ready = sem("mod_ready")
        mod_sums = sem("mod_sums")
        mod_copied = sem("mod_copied")
        pre_sq = sem("pre_sq")
        sums_ready = sem("sums_ready")
        root_ready = sem("root_ready")
        xr_ready = sem("xr_ready")
        hid_ready = sem("hid_ready")
        bf_ready = sem("bf_ready")
        rest_ready = sem("rest_ready")
        acc_ready = sem("acc_ready")
        x_ready = sem("x_ready")
        w_hi_ready = sem("w_hi_ready")
        w_rest_ready = sem("w_rest_ready")
        part_done = sem("part_done")
        silu_ready = sem("silu_ready")
        gu_taken = sem("gu_taken")
        oc_bf = sem("oc_bf")
        oc_hi = sem("oc_hi")
        oc_rest = sem("oc_rest")
        y_taken = sem("y_taken")
        out_stored = sem("out_stored")
        c_exp = sem("c_exp")
        vec_in = sem("vec_in")
        lb_exp = sem("lb_exp")
        h_vf = sem("h_vf")
        h_vt = sem("h_vt")
        h_exp = sem("h_exp")
        h_v = sem("h_v")
        h_f = sem("h_f")
        h_lf = sem("h_lf")
        h_d = sem("h_d")
        h_ex = sem("h_ex")
        h_qk = sem("h_qk")
        h_kd = sem("h_kd")
        h_kt = sem("h_kt")
        h_kdt = sem("h_kdt")
        h_vb = sem("h_vb")
        h_vk = sem("h_vk")
        h_u = sem("h_u")
        h_s = sem("h_s")
        h_p = sem("h_p")
        h_ptk = sem("h_ptk")
        h_att = sem("h_att")
        h_o = sem("h_o")
        h_sq = sem("h_sq")
        h_ss = sem("h_ss")
        h_r = sem("h_r")
        h_done = sem("h_done")
        s_loaded = sem("s_loaded")
        s_new = sem("s_new")
        s_stored = sem("s_stored")
        g_in = sem("g_in")
        d_step = sem("d_step")
        d_act = sem("d_act")
        d_pe = sem("d_pe")
        g_proj = sem("g_proj")
        g_raw = sem("g_raw")
        g_conv = sem("g_conv")
        g_x = sem("g_x")
        g_z = sem("g_z")
        g_sel = sem("g_sel")
        g_tr = sem("g_tr")
        g_btk = sem("g_btk")
        g_xd = sem("g_xd")
        g_bc = sem("g_bc")
        g_cb = sem("g_cb")
        g_wl = sem("g_wl")
        g_wle = sem("g_wle")
        g_seg = sem("g_seg")
        g_sege = sem("g_sege")
        g_bcx = sem("g_bcx")
        g_m = sem("g_m")
        g_xw = sem("g_xw")
        g_u = sem("g_u")
        g_s = sem("g_s")
        g_bcfree = sem("g_bcfree")
        g_xb = sem("g_xb")
        g_uu = sem("g_uu")
        g_y = sem("g_y")
        g_yv = sem("g_yv")
        g_sq = sem("g_sq")
        g_ss = sem("g_ss")
        g_r = sem("g_r")
        g_done = sem("g_done")
        st_in = sem("st_in")
        st_out = sem("st_out")
        st_ok = sem("st_ok")
        m_proj = sem("m_proj")
        m_copy = sem("m_copy")
        m_ss = sem("m_ss")
        m_root = sem("m_root")
        m_norm = sem("m_norm")
        m_perm = sem("m_perm")
        m_cks = sem("m_cks")
        p_q = sem("p_q")
        p_qc = sem("p_qc")
        p_perm = sem("p_perm")
        p_qp = sem("p_qp")
        p_ql = sem("p_ql")
        p_qlt = sem("p_qlt")
        p_v = sem("p_v")
        p_vc = sem("p_vc")
        p_k = sem("p_k")
        p_kc = sem("p_kc")
        p_sc = sem("p_sc")
        p_mx = sem("p_mx")
        p_pr = sem("p_pr")
        p_pn = sem("p_pn")
        p_pt = sem("p_pt")
        p_ptc = sem("p_ptc")
        p_o = sem("p_o")
        p_oc = sem("p_oc")
        k_in = [sem("k_in0"), sem("k_in1")]
        k_free = [sem("k_free0"), sem("k_free1")]
        b_q = sem("b_q")
        b_sc = sem("b_sc")
        b_mx = sem("b_mx")
        b_ex = sem("b_ex")
        b_m = sem("b_m")
        b_mt = sem("b_mt")
        b_sum = sem("b_sum")
        b_tot = sem("b_tot")
        b_on = sem("b_on")
        b_pt = sem("b_pt")
        b_ptc = sem("b_ptc")
        b_o = sem("b_o")
        b_oc = sem("b_oc")
        u_o = sem("u_o")

        block = ctx.enter_context(nc.Block())

        def fencer(eng):
            state = [0]

            def fence():
                state[0] += 1
                eng.drain().then_inc(stage_done, 1)
                eng.wait_ge(stage_done, 3 * state[0])
            return fence

        def pair(bank, cols=HT, rows=P):
            return PS[0:rows, bank:bank + 2, 0:cols]

        def two(ap):
            return ap.rearrange("p (a b) -> p a b", a=2)

        def apart(eng):
            eng.sem_inc(wait_passed, 1)

        def w_ready(pe, base, i, jj):
            slot = (base + jj) % 2
            pe.wait_ge(w_arrived[slot], i * 16 + 16 * ((base + jj) // 2 + 1))
            return slot

        GROUPS = {}
        n_groups = 0
        for s in range(6):
            for stage, loads, tiles_ in ((("up", s), FC, 2 * DC), (("down", s), DC, 2 * DC if s % 3 == 1 else FC)):
                if stage == ("up", 1):
                    GROUPS["hgrn"] = (n_groups, 2 * HG, 2 * DC)
                    n_groups += 4 * HG
                if s % 3 != 1 or stage[0] == "down":
                    GROUPS[stage] = (n_groups, loads, tiles_)
                    n_groups += loads * -(-tiles_ // DC)
        FFN_OF = {0: 0, 2: 1, 3: 2, 5: 3}

        NORM_OF = {0: 0, 1: 1, 2: 2, 3: 3, 5: 4}
        FORGET, QUERY, GATE, VALUE = range(4)
        HG_TILES = ((0, DC), (0, 0), (1, DC), (1, 0))

        def hgrn_group(h, c):
            return h * 4 + (GROUPS["hgrn"][0] + c)

        def hgrn_weights(c):
            load, first = HG_TILES[c]
            return W[:, (LOADS["hgrn"] + load) % 2, first * P:(first + DC) * P]

        def per_load(stage):
            return -(-GROUPS[stage][2] // DC)

        def group(stage, i, jj, j):
            per = per_load(stage)
            fixed = GROUPS[stage][0] + jj * per + j
            return i * (2 * per) + fixed, fixed % 2

        def tiles_in(stage, j):
            return min(DC, GROUPS[stage][2] - j * DC)

        def staggered(eng, stage, cut, finish, begin=None, cut_next=None):
            loads, groups = GROUPS[stage][1], per_load(stage)

            def step(i, jj, more):
                if begin:
                    begin(i, jj)
                for j in range(2, groups):
                    cut(i, jj, j)
                for j in range(2):
                    if more:
                        cut(i, jj + 1, j)
                    elif cut_next:
                        cut_next(0, 0, j)
                finish(i, jj)

            with eng.Fori(0, loads // 2 - 1) as i:
                for jj in range(2):
                    step(i, jj, True)
            for jj in range(2):
                step(loads // 2 - 1, jj, jj == 0)

        QBANK = (2, 6, 0)
        XBANK, ZBANK = (4, 2, 0, 6), (2, 0)

        @block.sync
        def _(sp):
            sp.dma_start(CT[:, :], A["const"]).then_inc(const_in, 16)
            sp.dma_start(X[:, :, :], A["x"]).then_inc(const_in, 16)
            sp.dma_start(CR, A["c"]).then_inc(const_in, 16)
            sp.dma_start(ADB[:, :, :], A["ada_b"]).then_inc(const_in, 16)
            sp.dma_start(NPRE[:, :, :], A["norm_pre"]).then_inc(const_in, 16)
            sp.dma_start(NPOST[:, :, :], A["norm_post"]).then_inc(const_in, 16)
            sp.dma_start(TABLE[:, :], A["page_table"]).then_inc(const_in, 16)

            def load(base, i, jj, tiles, src):
                slot = (base + jj) % 2
                sp.wait_ge(w_free, i * 2 + (base + jj + 1))
                sp.dma_start(W[:, slot, 0:tiles * P], src).then_inc(w_arrived[slot], 16)

            def ffn_up(s, f):
                base = LOADS["up", s]
                with sp.Fori(0, FC // 2) as i:
                    for jj in range(2):
                        load(base, i, jj, 2 * DC, A["ffn_gu"][i * 2 + (f * FC + jj)])

            def down(s, src, tiles, first):
                base = LOADS["down", s]
                def weights(i, jj):
                    load(base, i, jj, tiles, src[i * 2 + (first + jj)])

                def ada(i, jj):
                    if s < 5:
                        sp.wait_ge(mod_sums, i * 2 + ((s + 1) * 8 + jj + 1))
                        sp.dma_start(AD[:, :], A["ada_w"][i * 2 + ((s + 1) * 8 + jj)]).then_inc(ada_arrived, 16)

                ada(0, 0)
                weights(0, 0)
                weights(0, 1)
                ada(0, 1)
                with sp.Fori(1, DC // 2) as i:
                    for jj in range(2):
                        weights(i, jj)
                        ada(i, jj)

            with sp.Fori(0, NMOD // 6) as i:
                for jj in range(2):
                    load(0, i, jj, 24, A["ada_w"][i * 2 + jj])
            for layer in range(2):
                ffn_up(layer * 3, layer * 2)
                down(layer * 3, A["ffn_wd"], FC, layer * 2 * DC)
                if layer == 0:
                    with sp.Fori(0, HG) as h:
                        for jj in range(2):
                            load(LOADS["hgrn"], h, jj, 16, A["w_hgrn"][h * 2 + jj])
                    with sp.Fori(0, SG_) as g:
                        for jj in range(2):
                            load(LOADS["ssm"], g, jj, 24, A["w_ssm"][g * 2 + jj])
                    down(1, A["w_out_ab"], 16, 0)
                else:
                    base = LOADS["latent"]
                    load(base, 0, 0, 16, A["mla_dq"][0])
                    load(base, 0, 1, 16, A["mla_dq"][1])
                    load(base, 0, 2, 24, A["mla_dkv"])
                    with sp.Fori(0, MH // 4) as i:
                        for jj in range(2):
                            load(LOADS["pairs"], i, jj, 24, A["mla_pairs"][i * 2 + jj])
                    with sp.Fori(0, NB // 2) as b:
                        for bb in range(2):
                            sp.wait_ge(k_free[bb], b + 1)
                            for pg in range(NPAGE):
                                page = sp.value_load(TABLE[0:1, bass.ds(b * (2 * NPAGE) + (bb * NPAGE + pg), 1)],
                                                     min_val=0, max_val=A["pages"].shape[0] - 1)
                                sp.dma_start(PAGES[bb][pg], A["pages"][page]).then_inc(k_in[bb], 16)
                    load(LOADS["uv"], 0, 0, 16, A["mla_uv"][0])
                    load(LOADS["uv"], 0, 1, 16, A["mla_uv"][1])
                    down(4, A["mla_wo"], 16, 0)
                ffn_up(layer * 3 + 2, layer * 2 + 1)
                down(layer * 3 + 2, A["ffn_wd"], FC, (layer * 2 + 1) * DC)

        @block.gpsimd
        def _(pool):
            pool.sem_inc(s_stored, 1)
            pool.sem_inc(st_ok, 1)

            pool.wait_ge(stage_done, 3 * FFN0_DONE)
            pool.dma_start(LB, A["lb_logits"]).then_inc(vec_in, 16)
            pool.dma_start(HVEC[:, 2, :], A["hg_norm"]).then_inc(vec_in, 16)
            pool.dma_start(CT2[:, :], A["mixer_const"]).then_inc(vec_in, 16)
            pool.dma_start(MSK[:, :, :], A["masks"]).then_inc(vec_in, 16)
            with pool.Fori(0, HG) as h:
                pool.wait_ge(h_done, h + 1)
                apart(pool)
                pool.dma_start(S0, A["state_hgrn"][h]).then_inc(s_loaded, 16)
                pool.wait_ge(h_s, h + 1)
                apart(pool)
                pool.dma_start(O["hgrn_prompt"][h], ST[:, NCH - 1, :]).then_inc(out_stored, 16)
                pool.wait_ge(s_new, h + 1)
                apart(pool)
                pool.dma_start(O["hgrn_sample"][h], S0).then_inc(out_stored, 16)
                pool.wait_ge(out_stored, h * 32 + 32)
                pool.sem_inc(s_stored, 1)
            pool.wait_ge(stage_done, 3 * HGRN_DONE)
            for dst, name in ((CW, "conv_w"), (DSK, "ssm_d"), (SNW, "ssm_norm"), (DTW, "w_dt"), (SMS[:, 0:2], "ssm_small")):
                pool.dma_start(dst, A[name]).then_inc(g_in, 16)
            with pool.Fori(0, SG_) as g:
                pool.wait_ge(g_done, g + 1)
                apart(pool)
                pool.dma_start(STC, A["state_conv"][g]).then_inc(st_in, 16)
                pool.dma_start(SM0, A["state_ssm"][g]).then_inc(st_in, 16)
                pool.wait_ge(st_in, g * 32 + 32)
                pool.wait_ge(g_raw, g * 4 + 4)
                apart(pool)
                pool.dma_start(O["conv_prompt"][g], XR[:, :, NP_ - 3:NP_]).then_inc(st_out, 16)
                pool.dma_start(O["conv_sample"][g, :, :, 0:2, :], STC[:, :, 1:3, :]).then_inc(st_out, 16)
                pool.dma_start(O["conv_sample"][g, :, :, 2, :], XR[:, :, NP_:T]).then_inc(st_out, 16)
                pool.wait_ge(g_s, g + 1)
                apart(pool)
                pool.dma_start(O["ssm_prompt"][g], SS[:, NCH - 1]).then_inc(st_out, 16)
                pool.wait_ge(g_uu, g * 2 + 2)
                apart(pool)
                pool.dma_start(O["ssm_sample"][g], SM0).then_inc(st_out, 16)
                pool.wait_ge(st_out, g * 80 + 80)
                pool.sem_inc(st_ok, 1)
            pool.wait_ge(stage_done, 3 * FFN3_DONE)
            pool.dma_start(GQ, A["mla_gq"]).then_inc(m_cks, 16)
            pool.dma_start(GKV, A["mla_gkv"]).then_inc(m_cks, 16)
            pool.dma_start(CT2[:, :], A["mixer_const"]).then_inc(m_cks, 16)
            pool.wait_ge(m_norm, 3)
            pool.dma_start(O["ckv"], CKV).then_inc(out_stored, 16)
            pool.dma_start(O["kpe"], KPE[0:ROPE, :]).then_inc(out_stored, 16)
            pool.wait_ge(out_stored, 32 * HG + 32)
            for c in range(0, DC, 2):
                pool.wait_ge(x_ready, 5 * DC + c + 2)
                pool.dma_start(O["y"][:, c:c + 2, :], X[:, c:c + 2, :]).then_inc(out_stored, 16)
            pool.wait_ge(out_stored, 32 * HG + 32 + 16 * (DC // 2))

        @block.tensor
        def _(pe):
            fence = fencer(pe)
            pe.sem_inc(w_free, 2)

            def product(bank, weights, moving, rows=P):
                n = len(weights)
                for k in range(n):
                    for hf in range(2):
                        last = pe.matmul(PS[0:rows, bank + hf, 0:HT], weights[k], moving[k][:, hf * HT:(hf + 1) * HT],
                                         start=(k == 0), stop=(k == n - 1))
                return last

            def tiles(slot, first, n):
                return [W[:, slot, (first + k) * P:(first + k + 1) * P] for k in range(n)]

            def product_of_parts(bank, buf, n, first, hi, bf, rest, start, stop, before=None,
                                 weights=None):
                w_hi, w_bf, w_rest = weights or (WH, WB, WL_)
                for k in range(n):
                    cols = slice(k * P, (k + 1) * P)
                    if before:
                        before(k)
                    for hf in range(2):
                        out = PS[:, bank + hf, 0:HT]
                        half = slice(hf * HT, (hf + 1) * HT)
                        pe.matmul(out, w_hi[:, buf, cols], hi[:, first + k, half], start=start and k == 0, stop=False)
                        pe.matmul(out, w_bf[:, buf, cols], rest[:, first + k, half], start=False, stop=False)
                        last = pe.matmul(out, w_rest[:, buf, cols], bf[:, first + k, half], start=False,
                                         stop=stop and k == n - 1)
                return last

            def rows_of(buf, n):
                return [buf[:, k, :] for k in range(n)]

            def mod_sums_of(weights):
                for k in range(DC):
                    q = k % QUARTERS
                    last = pe.matmul(PS[q * QR_:(q + 1) * QR_, 4, 0:3 * P], CS[:, k, :],
                                     weights[:, k * 3 * P:(k + 1) * 3 * P], start=(k < 4), stop=(k >= 4))
                last.then_inc(mod_sums, 1)

            def mod_fold(s, i, jj):
                pe.wait_ge(mod_copied, i * 2 + (s * 8 + jj + 1))
                for c in range(3):
                    last = pe.matmul(PS[:, 5, c * NSEQ:(c + 1) * NSEQ], MS[:, c * P:(c + 1) * P],
                                     const("fold")[:, 0:NSEQ], start=True, stop=True)
                last.then_inc(mod_ready, 1)

            def modulation():
                with pe.Fori(0, NMOD // 6) as i:
                    for jj in range(2):
                        slot = w_ready(pe, LOADS["mod"], i, jj)
                        mod_sums_of(W[:, slot, :])
                        mod_fold(0, i, jj)
                fence()

            def pre_norm(s):
                for c in range(DC):
                    pe.wait_ge(pre_sq, DC * s + c + 1)
                    for hf in range(2):
                        last = pe.matmul(PS[:, hf, 0:HT], ONES, Y[:, c, hf * HT:(hf + 1) * HT],
                                         start=(c == 0), stop=(c == DC - 1))
                last.then_inc(sums_ready, 1)
                if s % 3 == 1:
                    fence()

            def post_norm(s):
                pe.wait_ge(acc_ready, s + 1)
                product(0, [ONES], [R]).then_inc(sums_ready, 1)

            def ffn_up(s, f):
                def normed(k):
                    pe.wait_ge(bf_ready, NORM_OF[s] * DC + k + 1)
                    pe.wait_ge(rest_ready, NORM_OF[s] * DC + k + 1)

                def step(i, jj, before=None):
                    pe.wait_ge(gu_taken, i * 2 + (f * FC + jj + 1))
                    for j in range(2):
                        g, buf = group(("up", s), i, jj, j)
                        pe.wait_ge(w_rest_ready, g + 1)
                        product_of_parts(4 * jj + 2 * j, buf, DC, 0, HH, HB, HL, True, True,
                                         before if j == 0 else None).then_inc(part_done, 1)

                step(0, 0, normed)
                step(0, 1)
                with pe.Fori(1, FC // 2) as i:
                    for jj in range(2):
                        step(i, jj)
                fence()

            def down(s):
                stage, mixer = ("down", s), s % 3 == 1
                parts = (OCH, OCB, OCL) if mixer else (GH_, GB, GL)

                def heads(k):
                    pe.wait_ge(oc_bf, s // 3 * 2 * DC + k + 1)
                    pe.wait_ge(oc_rest, s // 3 * 2 * DC + k + 1)

                def step(i, jj, before=None):
                    if s < 5:
                        pe.wait_ge(ada_arrived, i * 32 + (16 * (8 * s + jj + 1)))
                        mod_sums_of(AD)
                    pe.wait_ge(y_taken, i * 2 + (s * DC + jj + 1))
                    groups = per_load(stage)
                    for j in range(groups):
                        g, buf = group(stage, i, jj, j)
                        pe.wait_ge(w_rest_ready, g + 1)
                        product_of_parts(2 * jj, buf, tiles_in(stage, j), j * DC, *parts, j == 0, j == groups - 1,
                                         (lambda k: before(j * DC + k)) if before else None).then_inc(part_done, 1)
                    if s < 5:
                        mod_fold(s + 1, i, jj)

                step(0, 0, heads if mixer else None)
                step(0, 1)
                with pe.Fori(1, DC // 2) as i:
                    for jj in range(2):
                        step(i, jj)
                fence()

            def split_product(bank, weights, between):
                half = DC // 2
                for k in range(DC):
                    if k == half:
                        between()
                    for hf in range(2):
                        last = pe.matmul(PS[:, bank + hf, 0:HT], weights[k], H[:, k, hf * HT:(hf + 1) * HT],
                                         start=(k == 0), stop=(k == DC - 1))
                return last

            def hgrn():
                def project(h, c, bank, before=None):
                    g = hgrn_group(h, c)
                    pe.wait_ge(w_rest_ready, g + 1)
                    product_of_parts(bank, c % 2, DC, 0, GHH, GHB, GHL, True, True, before, (GWH, GWB, GWL))\
                        .then_inc(part_done, 1)

                def head(h, more):
                    pe.wait_ge(h_done, h + 1)
                    project(h, GATE, 4)
                    project(h, VALUE, 6)
                    pe.wait_ge(h_vf, h + 1)
                    for c in range(NCH):
                        pe.transpose(PS[:, 6, c * P:(c + 1) * P], VF[:, c * CH:(c + 1) * CH], IDENT)
                    pe.transpose(PS[0:NB, 7, 0:P], VF[:, NP_:T], IDENT).then_inc(h_vt, 1)
                    pe.wait_ge(h_v, h + 1)
                    for b in range(NB):
                        last = pe.matmul(PS[:, 6 + b // 4, (b % 4) * P:(b % 4 + 1) * P],
                                         const("sel", NB)[:, b * P:(b + 1) * P], VS, start=True, stop=True)
                    last.then_inc(h_vb, 1)
                    pe.wait_ge(h_kd, h + 1)
                    for c in range(NCH):
                        last = pe.transpose(PS[:, 4, c * P:(c + 1) * P], KD[:, c * CH:(c + 1) * CH], IDENT)
                    last.then_inc(h_kt, 1)
                    for n in range(1 + len(LEVELS)):
                        if n >= 1:
                            pe.wait_ge(h_qk, h * 7 + n)
                        pe.wait_ge(h_ptk, h * 8 + (n + 1))
                        for c in range(NCH):
                            cc = slice(c * CH, (c + 1) * CH)
                            lhs, rhs = (KK[:, cc], QS[:, cc]) if n == 0 else (DL[:, n - 1, cc], DL[:, n - 1, cc])
                            last = pe.matmul(PS[:, n % 2, cc], lhs, rhs, start=True, stop=True)
                        last.then_inc(h_p, 1)
                        if n == 0:
                            pe.wait_ge(h_kdt, h + 1)
                            for c in range(NCH):
                                last = pe.matmul(PS[:, 5, c * P:(c + 1) * P], KDT[:, c, :], VV[:, c, :],
                                                 start=True, stop=True)
                            last.then_inc(h_u, 1)
                    if more:
                        project(h + 1, FORGET, 2)
                    pe.wait_ge(h_vk, h + 1)
                    pe.wait_ge(h_att, h + 1)
                    pe.wait_ge(h_s, h + 1)
                    for c in range(NCH):
                        cc = slice(c * CH, (c + 1) * CH)
                        last = pe.matmul(PS[:, 6, cc], VV[:, c, :], AT[:, c, :], start=True, stop=(c == 0))
                        if c:
                            last = pe.matmul(PS[:, 6, cc], ST[:, c - 1, :], QI[:, cc], start=False, stop=True)
                    last.then_inc(h_o, 1)
                    pe.wait_ge(s_new, h + 1)
                    for b in range(NB):
                        last = pe.matmul(PS[:, 7, b:b + 1], S0[:, b, :], QS[:, NP_ + b:NP_ + b + 1],
                                         start=True, stop=True)
                    last.then_inc(h_o, 1)

                    def sums():
                        pe.wait_ge(h_sq, h + 1)
                        product(4, [ONES], [SQO]).then_inc(h_ss, 1)

                    if more:
                        project(h + 1, QUERY, 0, lambda k: sums() if k == DC // 2 else None)
                    else:
                        sums()

                project(0, FORGET, 2)
                project(0, QUERY, 0)
                pe.wait_ge(vec_in, 64)
                with pe.Fori(0, HG - 1) as h:
                    head(h, True)
                head(HG - 1, False)
                fence()

            def ssm():
                slot = w_ready(pe, LOADS["ssm"], 0, 0)
                product(XBANK[0], tiles(slot, 0, DC), rows_of(H, DC)).then_inc(g_proj, 1)
                pe.wait_ge(g_in, 80)
                product(0, [DTW[:, k, :] for k in range(DC)], rows_of(H, DC), rows=16).then_inc(d_pe, 1)
                product(XBANK[1], tiles(slot, DC, DC), rows_of(H, DC)).then_inc(g_proj, 1)
                pe.wait_ge(d_step, 4)
                for c in range(NCH):
                    pe.transpose(PS[:, 6, c * 16:(c + 1) * 16], DT[:, c * CH:(c + 1) * CH], IDENT[0:16, 0:16])
                    pe.transpose(PS[:, 7, c * 16:(c + 1) * 16], LA[:, c * CH:(c + 1) * CH], IDENT[0:16, 0:16])
                pe.transpose(PS[0:NB, 7, NCH * 16:(NCH + 1) * 16], DT[:, NP_:T], IDENT[0:16, 0:16]).then_inc(d_pe, 1)
                fence()
                def group_of_heads(g, more):
                    slot = LOADS["ssm"] % 2
                    pe.wait_ge(g_done, g + 1)
                    product(XBANK[2], tiles(slot, 2 * DC, DC), rows_of(H, DC)).then_inc(g_proj, 1)
                    slot = w_ready(pe, LOADS["ssm"], g, 1)
                    product(XBANK[3], tiles(slot, 0, DC), rows_of(H, DC)).then_inc(g_proj, 1)
                    for c in range(2):
                        pe.wait_ge(g_raw, g * 4 + (c + 2))
                        product(ZBANK[c], tiles(slot, (c + 1) * DC, DC), rows_of(H, DC)).then_inc(g_proj, 1)
                    pe.wait_ge(g_x, g + 1)
                    pe.wait_ge(g_raw, g * 4 + 4)
                    for c in range(NCH):
                        for x in range(2):
                            pe.transpose(PS[:, 4 + c // 2, (c % 2) * 256 + x * P:(c % 2) * 256 + (x + 1) * P],
                                         CV[:, x, c * CH:(c + 1) * CH], IDENT)
                        pe.transpose(PS[:, 6, c * P:(c + 1) * P], CV[:, 2, c * CH:(c + 1) * CH], IDENT)
                    for x in range(2):
                        pe.transpose(PS[0:NB, 7, x * P:(x + 1) * P], CV[:, x, NP_:T], IDENT)
                    pe.wait_ge(g_sel, g + 1)
                    for j in range(GH):
                        last = pe.matmul(PS[:, 7, 256 + j * NB:256 + (j + 1) * NB], SELG[:, j, :], LA[:, NP_:T],
                                         start=True, stop=True)
                    last.then_inc(g_tr, 1)
                    pe.wait_ge(g_z, g * 2 + 2)
                    for j in range(GH):
                        last = pe.matmul(PS[:, j, :], SELG[:, j, :], LA[:, 0:NP_], start=True, stop=True)
                    last.then_inc(g_bc, 1)
                    pe.wait_ge(g_btk, g + 1)
                    for c in range(NCH):
                        cc = slice(c * CH, (c + 1) * CH)
                        last = pe.matmul(PS[:, 6, cc], CV[:, 2, cc], CV[:, 3, cc], start=True, stop=True)
                    last.then_inc(g_cb, 1)
                    if more:
                        pe.wait_ge(g_xd, g + 1)
                        slot = w_ready(pe, LOADS["ssm"], g, 2)
                        product(XBANK[0], tiles(slot, 0, DC), rows_of(H, DC)).then_inc(g_proj, 1)
                    pe.wait_ge(g_xw, g + 1)
                    for c in range(NCH):
                        last = pe.matmul(PS[:, 6 + c // 2, (c % 2) * 256:(c % 2 + 1) * 256], BTK[:, c, :],
                                         XW[:, c].rearrange("p a b -> p (a b)"), start=True, stop=True)
                    last.then_inc(g_u, 1)
                    pe.wait_ge(g_bcfree, g + 1)
                    for b in range(NB):
                        last = pe.matmul(PS[:, b // 2, (b % 2) * 256:(b % 2 + 1) * 256],
                                         const("sel", NB)[:, b * P:(b + 1) * P], XDS, start=True, stop=True)
                    last.then_inc(g_xb, 1)
                    pe.wait_ge(g_m, g * 4 + 4)
                    pe.wait_ge(g_s, g + 1)
                    for j in range(GH):
                        lo = (j % 2) * HD
                        for c in range(NCH):
                            cc = slice(c * CH, (c + 1) * CH)
                            out = PS[lo:lo + HD, 6 + j // 2, cc]
                            last = pe.matmul(out, XD[:, c, j, :], SEG[:, j, cc], start=True, stop=(c == 0))
                            if c:
                                last = pe.matmul(out, SS[:, c - 1, j, :], CEX[:, j, cc], start=False, stop=True)
                    last.then_inc(g_y, 1)
                    pe.wait_ge(g_uu, g * 2 + 2)
                    for x in range(2):
                        for b in range(NB):
                            last = pe.matmul(PS[:, 1, x * NB + b:x * NB + b + 1],
                                             SM0[:, b, 2 * x:2 * x + 2, :].rearrange("p a b -> p (a b)"),
                                             CV[:, 3, NP_ + b:NP_ + b + 1], start=True, stop=True)
                    last.then_inc(g_y, 1)

                    def sums():
                        pe.wait_ge(g_sq, g + 1)
                        product(0, [ONES] * 2, rows_of(SUU, 2)).then_inc(g_ss, 1)

                    if more:
                        split_product(XBANK[1], tiles(slot, DC, DC), sums).then_inc(g_proj, 1)
                    else:
                        sums()

                with pe.Fori(0, SG_ - 1) as g:
                    group_of_heads(g, True)
                group_of_heads(SG_ - 1, False)
                fence()

            def mla():
                base = LOADS["latent"]
                for c in range(4):
                    if c % 2 == 0:
                        slot = w_ready(pe, base, 0, c // 2)
                    product(2 * c, tiles(slot, (c % 2) * DC, DC), rows_of(H, DC)).then_inc(m_proj, 1)
                slot = w_ready(pe, base, 0, 2)
                for c in range(3):
                    pe.wait_ge(m_copy, c + 2)
                    product(2 * (c + 1), tiles(slot, c * DC, DC), rows_of(H, DC)).then_inc(m_proj, 1)
                product(0, [ONES] * 4, rows_of(Y[:, 4:8, :], 4)).then_inc(m_ss, 1)
                pe.wait_ge(m_copy, 7)
                pe.wait_ge(m_root, 1)
                product(0, [ONES] * 2, rows_of(QN, 2)).then_inc(m_ss, 1)
                pe.wait_ge(m_cks, 48)
                product(2, [const("perm")], [QR]).then_inc(m_perm, 1)
                pe.wait_ge(m_norm, 2)
                for r in range(RC):
                    last = pe.transpose(PS[0:NB, 4, r * P:(r + 1) * P], CKV[:, r, NP_:T], IDENT)
                last.then_inc(m_perm, 1)
                fence()

                def head_pair(i, jj):
                    n = i * 2 + jj
                    slot = w_ready(pe, LOADS["pairs"], i, jj)
                    for c in range(3):
                        if c == 2:
                            pe.wait_ge(p_oc, n * 2 + 1)
                        product(QBANK[c], tiles(slot, 4 * ((c + 2) % 3), 4), rows_of(CQ, 4)).then_inc(p_q, 1)
                    pe.wait_ge(p_qc, n * 3 + 3)
                    product(2, [const("perm")], [QR]).then_inc(p_perm, 1)
                    ukt = W[:, slot, 20 * P:24 * P].rearrange("p (a b) -> p a b", a=2)
                    for hh in range(2):
                        for r in range(RC):
                            last = pe.matmul(PS[:, 0, (hh * 2 + r) * NB:(hh * 2 + r + 1) * NB],
                                             ukt[:, hh, r * P:(r + 1) * P], QN[:, hh, NP_:T], start=True, stop=True)
                    last.then_inc(p_ql, 1)
                    uv = W[:, slot, 16 * P:20 * P].rearrange("p (a b) -> p a b", a=2)
                    for c in range(NCH):
                        for k in range(RC):
                            last = pe.matmul(PS[:, 6 + c // 2, (c % 2) * 256:(c % 2 + 1) * 256],
                                             CKV[:, k, c * CH:(c + 1) * CH], uv[:, k, :],
                                             start=(k == 0), stop=(k == RC - 1))
                    last.then_inc(p_v, 1)
                    pe.wait_ge(p_oc, n * 2 + 2)
                    uk = tiles(slot, 12, 4)
                    for hh in range(2):
                        for k in range(RC):
                            last = pe.matmul(PS[:, 4 + hh, :], uk[hh * 2 + k], CKV[:, k, 0:NP_],
                                             start=(k == 0), stop=(k == RC - 1))
                    last.then_inc(p_k, 1)
                    pe.wait_ge(p_kc, n + 1)
                    pe.wait_ge(p_qp, n + 1)
                    pe.wait_ge(p_qlt, n + 1)
                    pe.wait_ge(p_vc, n + 1)
                    for hh in range(2):
                        lo = hh * ROPE
                        for qb in range(4):
                            nk = (qb + 1) * P
                            out = PS[:, 4 * hh + qb, 0:nk]
                            pe.matmul(out, QN[:, hh, qb * P:(qb + 1) * P], KN[:, hh, 0:nk], start=True, stop=False)
                            pe.matmul(out, QP[lo:lo + ROPE, qb * P:(qb + 1) * P], KPE[lo:lo + ROPE, 0:nk],
                                      start=False, stop=True).then_inc(p_sc, 1)
                    for hh in range(2):
                        pe.wait_ge(p_pn, n * 8 + (hh * 4 + 4))
                        for kb in range(4):
                            for qb in range(kb, 4):
                                last = pe.transpose(PS[:, 4 * hh + kb, (qb - kb) * P:(qb - kb + 1) * P],
                                                    PR[:, hh, qb, kb * P:(kb + 1) * P], IDENT)
                        last.then_inc(p_pt, 1)
                    for hh in range(2):
                        pe.wait_ge(p_ptc, n * 2 + (hh + 1))
                        for kb in range(4):
                            last = pe.matmul(PS[:, 4 * hh, kb * P:NP_], VT[:, kb, hh, :], keys_of(hh, kb),
                                             start=(kb == 0), stop=(kb == 3))
                        last.then_inc(p_o, 1)

                def decode(b2, bb):
                    b = b2 * 2 + bb
                    pe.wait_ge(b_q, b + 1)
                    pe.wait_ge(k_in[bb], b2 * (16 * NPAGE) + 16 * NPAGE)
                    for j in range(4):
                        for part in range(4):
                            for q in range(QUARTERS):
                                page = PAGES[bb][4 * q + j]
                                out = PS[q * QR_:(q + 1) * QR_, 0, j * PAGE:(j + 1) * PAGE]
                                if part < RC:
                                    pe.matmul(out, QLB[:, part, :], page[:, part * PAGE:(part + 1) * PAGE],
                                              start=(part == 0), stop=False)
                                else:
                                    half = part - RC
                                    pe.matmul(out[:, half * 64:half * 64 + 64], QPB[:, half, :],
                                              page[:, 4 * PAGE:4 * PAGE + 64], start=False, stop=(half == 1))
                    own = PS[0:QR_, 1, 0:NB]
                    for r in range(RC):
                        pe.matmul(own, QLB[:, r, :], CKV[:, r, NP_:T], start=(r == 0), stop=False)
                    pe.matmul(own, QPB[0:ROPE, 0, :], KPE[0:ROPE, NP_:T], start=False, stop=True).then_inc(b_sc, 1)
                    pe.wait_ge(b_m, b * 2 + 1)
                    pe.matmul(PS[0:1, 2, 0:P], DST[:, 2:3], IDENT, start=True, stop=True).then_inc(b_mt, 1)
                    pe.wait_ge(b_m, b * 2 + 2)
                    pe.matmul(PS[:, 3, 0:1], ROW[:, QR_:QR_ + P], ONES[0:1, 0:1], start=True, stop=True)\
                        .then_inc(b_mt, 1)
                    pe.wait_ge(b_ex, b + 1)
                    for j in range(4):
                        pe.transpose(PS[:, 4, j * P:(j + 1) * P], PD[:, j, :], IDENT)
                    pe.transpose(PS[0:NB, 5, 0:QR_], PDO, IDENT[0:QR_, 0:QR_]).then_inc(b_pt, 1)
                    pe.wait_ge(b_sum, b + 1)
                    pe.matmul(PS[:, 7, 0:1], const("fold"), DST[:, 6:7], start=True, stop=True).then_inc(b_tot, 1)
                    pe.wait_ge(b_ptc, b + 1)
                    for j in range(4):
                        for q in range(QUARTERS):
                            pe.matmul(PS[q * QR_:(q + 1) * QR_, 6, 0:RC * P], PTD[:, j, q * QR_:(q + 1) * QR_],
                                      PAGES[bb][4 * q + j][:, 2 * PAGE:4 * PAGE], start=(j == 0),
                                      stop=(j == 3 and q > 0))
                    pe.matmul(PS[0:QR_, 6, 0:RC * P], PTO, CKVS.rearrange("p a b -> p (a b)"),
                              start=False, stop=True).then_inc(b_o, 1)
                    pe.wait_ge(b_on, b + 1)
                    for r in range(RC):
                        last = pe.matmul(PS[:, 7, MH + r * MH:2 * MH + r * MH], OP[:, r * P:(r + 1) * P],
                                         const("fold")[:, 0:MH], start=True, stop=True)
                    last.then_inc(b_oc, 1)

                with pe.Fori(0, MH // 4) as i:
                    for jj in range(2):
                        head_pair(i, jj)
                fence()
                for bb in range(2):
                    pe.sem_inc(k_free[bb], 1)
                with pe.Fori(0, NB // 2) as b2:
                    for bb in range(2):
                        decode(b2, bb)
                fence()
                slot = w_ready(pe, LOADS["uv"], 0, 0)
                for hh in range(8):
                    for k in range(RC):
                        last = pe.matmul(PS[:, 0, hh * NB:(hh + 1) * NB], W[:, slot, (k * 8 + hh) * P:(k * 8 + hh + 1) * P],
                                         OL[:, k, hh, :], start=(k == 0), stop=(k == RC - 1))
                last.then_inc(u_o, 1)
                pe.wait_ge(u_o, 1)
                pe.sem_inc(w_free, 1)
                slot = w_ready(pe, LOADS["uv"], 0, 1)
                for hh in range(8):
                    for k in range(RC):
                        last = pe.matmul(PS[:, 1, hh * NB:(hh + 1) * NB], W[:, slot, (k * 8 + hh) * P:(k * 8 + hh + 1) * P],
                                         OL[:, k, 8 + hh, :], start=(k == 0), stop=(k == RC - 1))
                last.then_inc(u_o, 1)
                pe.wait_ge(u_o, 2)
                pe.sem_inc(w_free, 1)
                fence()

            pe.wait_ge(const_in, 112)
            pe.wait_ge(c_exp, 2)
            modulation()
            pre_norm(0)
            for s in range(6):
                if s == 1:
                    hgrn()
                    ssm()
                elif s == 4:
                    mla()
                else:
                    ffn_up(s, FFN_OF[s])
                down(s)
                post_norm(s)
                if s < 5:
                    pre_norm(s + 1)
            fence()

        @block.scalar
        def _(act):
            fence = fencer(act)

            def inv_rms(done, width, bank=0):
                act.activation(two(R[:, :]), pair(bank), ACT.Ln, bias=const("eps"), scale=1.0 / width)
                act.drain()
                act.activation(R[:, :], R[:, :], ACT.Exp, scale=-0.5).then_inc(done, 1)

            def pre_norm(s):
                ffn = s % 3 != 1
                bf = HB if ffn else GHB
                for c in range(DC):
                    if ffn and c in (2, 4):
                        cut_of(("up", s))(0, 0, c // 2 - 1)
                    if s:
                        act.wait_ge(x_ready, (s - 1) * DC + c + 1)
                    act.activation(Y[:, c, :], X[:, c, :], ACT.Square).then_inc(pre_sq, 1)
                act.wait_ge(sums_ready, 2 * s + 1)
                inv_rms(root_ready, D)
                dst = NORMED if ffn else H
                for c in range(DC):
                    act.wait_ge(xr_ready, s * DC + c + 1)
                    act.activation(dst[:, c, 0:NP_], dst[:, c, 0:NP_], ACT.Identity, bias=MOD[:, c, 0:1],
                                   scale=AM[:, c, 0:1]).then_inc(hid_ready, 1)
                    if s in NORM_OF:
                        act.drain()
                        act.activation(bf[:, c, :], dst[:, c, :], ACT.Copy).then_inc(bf_ready, 1)
                if not ffn:
                    fence()

            def post_norm(s):
                act.activation(const("scratch"), ONES[:, 0:1], ACT.Ln)
                act.wait_ge(sums_ready, 2 * s + 2)
                inv_rms(root_ready, D)

            def cut_group(g, buf, src, n, hi, bf):
                act.wait_ge(part_done, g + 1)
                act.activation(bf[:, buf, 0:n], src, ACT.Copy)
                act.activation(hi[:, buf, 0:n], src, ACT.Copy).then_inc(w_hi_ready, 1)

            def cut_of(stage):
                base = LOADS[stage]

                def cut(i, jj, j):
                    slot = (base + jj) % 2
                    if j == 0:
                        w_ready(act, base, i, jj)
                    g, buf = group(stage, i, jj, j)
                    n = tiles_in(stage, j) * P
                    src = W[:, slot, j * DC * P:j * DC * P + n]
                    cut_group(g, buf, src, n, WH, WB)
                return cut

            def ffn_up(s, f):
                def finish(i, jj):
                    act.wait_ge(part_done, group(("up", s), i, jj, 1)[0] + 3)
                    act.activation(two(SILU[:, jj, :]), pair(4 * jj), ACT.Silu).then_inc(silu_ready, 1)
                staggered(act, ("up", s), cut_of(("up", s)), finish, cut_next=cut_of(("down", s)))
                fence()

            def down(s):
                stage, mixer = ("down", s), s % 3 == 1

                def finish(i, jj):
                    act.wait_ge(part_done, group(stage, i, jj, per_load(stage) - 1)[0] + 3)
                    act.activation(two(Y[:, i * 2 + jj, :]), pair(2 * jj), ACT.Copy)
                    squares = SQ[:, jj, :] if mixer else H[:, i * 2 + jj, :]
                    act.activation(two(squares), pair(2 * jj), ACT.Square).then_inc(y_taken, 1)

                if mixer:
                    for c in range(2 * DC):
                        if c % DC == 0:
                            cut_of(stage)(0, 0, c // DC)
                        if c % 2:
                            act.activation(OCH[:, c, :], OC[:, c, :], ACT.Copy).then_inc(oc_hi, 1)
                        act.activation(OCB[:, c, :], OC[:, c, :], ACT.Copy).then_inc(oc_bf, 1)
                staggered(act, stage, cut_of(stage), finish)
                fence()

            def hgrn():
                def cut(h, c, ahead=0):
                    if c in (FORGET, GATE):
                        w_ready(act, LOADS["hgrn"], h, 2 * ahead + HG_TILES[c][0])
                    cut_group(hgrn_group(h, c) + 4 * ahead, c % 2, hgrn_weights(c), DC * P, GWH, GWB)

                def projected(h, c):
                    act.wait_ge(part_done, hgrn_group(h, c) + 3)

                for c in (FORGET, QUERY):
                    cut(0, c)
                act.wait_ge(lb_exp, 1)
                act.activation(LB, LB, ACT.Exp).then_inc(lb_exp, 1)

                def forget_exp(h, ahead=0):
                    act.wait_ge(part_done, hgrn_group(h, FORGET) + (4 * ahead + 3))
                    act.activation(two(E2), pair(2), ACT.Exp, scale=-1.0).then_inc(h_exp, 1)

                def forget_log(h, ahead=0):
                    act.wait_ge(h_f, h + (ahead + 1))
                    act.activation(EB, FG[:, 0:NP_], ACT.Ln).then_inc(h_lf, 1)

                forget_exp(0)
                cut(0, GATE)
                forget_log(0)

                def head(h, more):
                    cut(h, VALUE)
                    act.wait_ge(h_d, h * 9 + 1)
                    act.activation(EB, BB, ACT.Exp).then_inc(h_ex, 1)
                    act.wait_ge(h_d, h * 9 + 2)
                    act.activation(KD, KD, ACT.Exp).then_inc(h_ex, 1)
                    for n in range(len(LEVELS)):
                        act.wait_ge(h_d, h * 9 + (3 + n))
                        act.activation(DL[:, n, :], DL[:, n, :], ACT.Exp).then_inc(h_ex, 1)
                    projected(h, QUERY)
                    act.activation(two(QS), pair(0), ACT.Silu).then_inc(h_exp, 1)
                    projected(h, GATE)
                    act.activation(two(GS), pair(4), ACT.Silu).then_inc(h_exp, 1)
                    projected(h, VALUE)
                    act.activation(two(VF), pair(6), ACT.Copy).then_inc(h_vf, 1)
                    act.wait_ge(h_vt, h + 1)
                    act.activation(VV.rearrange("p a b -> p (a b)"), PS[:, 6, :], ACT.Copy)
                    act.activation(VS, PS[0:NB, 7, 0:P], ACT.Copy).then_inc(h_v, 1)
                    if more:
                        cut(h, FORGET, 1)
                        cut(h, QUERY, 1)
                    act.wait_ge(h_kt, h + 1)
                    act.activation(KDT.rearrange("p a b -> p (a b)"), PS[:, 4, :], ACT.Copy).then_inc(h_kdt, 1)
                    if more:
                        act.activation(const("scratch"), ONES[:, 0:1], ACT.Exp)
                        forget_exp(h, 1)
                        cut(h, GATE, 1)
                    act.wait_ge(h_o, h * 2 + 2)
                    act.activation(SQO[:, 0:NP_], PS[:, 6, :], ACT.Square)
                    act.activation(SQO[:, NP_:T], PS[:, 7, 0:NB], ACT.Square).then_inc(h_sq, 1)
                    if more:
                        forget_log(h, 1)
                    act.wait_ge(h_ss, h + 1)
                    inv_rms(h_r, P, bank=4)

                with act.Fori(0, HG - 1) as h:
                    head(h, True)
                head(HG - 1, False)
                fence()

            def ssm():
                act.wait_ge(d_step, 1)
                act.activation(DTE, DTE, ACT.Exp, scale=-1.0)
                act.activation(SMS[:, 2:3], SMS[:, 1:2], ACT.Exp).then_inc(d_act, 1)
                act.wait_ge(d_step, 2)
                act.activation(DTE, DTE, ACT.Ln).then_inc(d_act, 1)
                act.wait_ge(d_pe, 2)
                act.activation(DTT.rearrange("p a b -> p (a b)"), PS[:, 6, 0:NCH * 16], ACT.Copy)
                act.activation(BT.rearrange("p a b -> p (a b)"), PS[:, 7, 0:NCH * 16], ACT.Copy)
                act.activation(DTS, PS[0:NB, 7, NCH * 16:(NCH + 1) * 16], ACT.Copy)
                fence()
                with act.Fori(0, SG_) as g:
                    act.wait_ge(st_ok, g + 1)
                    for c in range(4):
                        act.wait_ge(g_proj, g * 6 + (c + 1))
                        if c == 2:
                            act.sem_inc(w_free, 1)
                        act.activation(two(XR[:, c, :]), pair(XBANK[c]), ACT.Copy).then_inc(g_raw, 1)
                    for z in range(2):
                        act.wait_ge(g_proj, g * 6 + (5 + z))
                        if z == 1:
                            act.sem_inc(w_free, 1)
                        act.activation(two(GZ[:, z, :]), pair(ZBANK[z]), ACT.Silu).then_inc(g_z, 1)
                        if z == 0:
                            act.wait_ge(g_conv, g + 1)
                            act.activation(CV.rearrange("p a b -> p (a b)"), CV.rearrange("p a b -> p (a b)"),
                                           ACT.Silu).then_inc(g_x, 1)
                    act.wait_ge(g_tr, g + 1)
                    act.activation(BTK.rearrange("p a b -> p (a b)"), PS[:, 6, :], ACT.Copy).then_inc(g_btk, 1)
                    act.wait_ge(g_xd, g + 1)
                    act.activation(EA.rearrange("p a b -> p (a b)"), PS[:, 7, 256:256 + GH * NB], ACT.Exp)
                    act.wait_ge(g_bc, g + 1)
                    for j in range(GH):
                        act.activation(CEX[:, j, :], PS[:, j, :], ACT.Exp).then_inc(g_bcx, 1)
                    act.wait_ge(g_wl, g + 1)
                    act.activation(WL.rearrange("p a b -> p (a b)"), WL.rearrange("p a b -> p (a b)"), ACT.Exp)
                    act.activation(EL.rearrange("p a b -> p (a b)"), EL.rearrange("p a b -> p (a b)"),
                                   ACT.Exp).then_inc(g_wle, 1)
                    for j in range(GH):
                        act.wait_ge(g_seg, g * 4 + (j + 1))
                        act.activation(SEG[:, j, :], SEG[:, j, :], ACT.Exp).then_inc(g_sege, 1)
                    act.wait_ge(g_yv, g + 1)
                    for x in range(2):
                        act.activation(SUU[:, x, :], EV[:, x, :], ACT.Square)
                    act.drain().then_inc(g_sq, 1)
                    act.wait_ge(g_ss, g + 1)
                    inv_rms(g_r, 2 * P)
                fence()

            def mla():
                for c in range(4):
                    act.wait_ge(m_proj, c + 1)
                    if c % 2:
                        act.sem_inc(w_free, 1)
                    act.activation(two(CQ[:, c, :]), pair(2 * c), ACT.Copy)
                    act.activation(two(Y[:, 4 + c, :]), pair(2 * c), ACT.Square).then_inc(m_copy, 1)
                for c in range(RC):
                    act.wait_ge(m_proj, 5 + c)
                    act.activation(two(CKV[:, c, :]), pair(2 * c + 2), ACT.Copy)
                    act.activation(two(QN[:, c, :]), pair(2 * c + 2), ACT.Square).then_inc(m_copy, 1)
                act.wait_ge(m_proj, 7)
                act.sem_inc(w_free, 1)
                act.activation(two(QR), pair(6), ACT.Copy).then_inc(m_copy, 1)
                for n, width in enumerate((4 * P, RC * P)):
                    act.wait_ge(m_ss, n + 1)
                    if n:
                        act.wait_ge(m_norm, 1)
                    inv_rms(m_root, width)
                act.wait_ge(m_perm, 2)
                act.activation(CKVS.rearrange("p a b -> p (a b)"), PS[0:NB, 4, 0:RC * P], ACT.Copy)
                fence()
                with act.Fori(0, MH // 4) as i:
                    for jj in range(2):
                        n = i * 2 + jj
                        for c in range(3):
                            act.wait_ge(p_q, n * 3 + (c + 1))
                            dst = QR if c == 0 else QN[:, c - 1, :]
                            act.activation(two(dst), pair(QBANK[c]), ACT.Copy).then_inc(p_qc, 1)
                        act.wait_ge(p_v, n + 1)
                        act.activation(VT.rearrange("p a b c -> p (a b c)").rearrange("p (a b) -> p a b", a=2),
                                       PS[:, 6:8, :], ACT.Copy).then_inc(p_vc, 1)
                        act.wait_ge(p_k, n + 1)
                        act.sem_inc(w_free, 1)
                        act.activation(KN, PS[:, 4:6, :], ACT.Copy).then_inc(p_kc, 1)
                        for hh in range(2):
                            for qb in range(4):
                                nk = (qb + 1) * P
                                act.wait_ge(p_mx, n * 8 + (hh * 4 + qb + 1))
                                act.activation(PR[:, hh, qb, 0:nk], PS[:, 4 * hh + qb, 0:nk], ACT.Exp,
                                               bias=SNB[:, hh, qb:qb + 1], scale=SCALE,
                                               accum_out=SRS[:, hh, qb:qb + 1]).then_inc(p_pr, 1)
                        for hh in range(2):
                            act.wait_ge(p_pt, n * 2 + (hh + 1))
                            for kb in range(4):
                                last = act.activation(keys_of(hh, kb),
                                                      PS[:, 4 * hh + kb, 0:NP_ - kb * P], ACT.Copy)
                            last.then_inc(p_ptc, 1)
                        for hh in range(2):
                            act.wait_ge(p_o, n * 2 + (hh + 1))
                            act.activation(OC[:, n * 2 + hh, 0:NP_], PS[:, 4 * hh, :], ACT.Copy).then_inc(p_oc, 1)
                fence()
                with act.Fori(0, NB // 2) as b2:
                    for bb in range(2):
                        b = b2 * 2 + bb
                        act.wait_ge(b_mx, b + 1)
                        act.activation(PD.rearrange("p a b -> p (a b)"), PS[:, 0, :], ACT.Exp, bias=DST[:, 3:4],
                                       scale=SCALE, accum_out=DST[:, 4:5])
                        act.activation(PDO, PDO, ACT.Exp, bias=DST[0:QR_, 3:4], scale=SCALE,
                                       accum_out=DST[0:QR_, 5:6])
                        act.drain().then_inc(b_ex, 1)
                        act.wait_ge(b_pt, b + 1)
                        act.activation(PTD.rearrange("p a b -> p (a b)"), PS[:, 4, :], ACT.Copy)
                        act.activation(PTO, PS[0:NB, 5, 0:QR_], ACT.Copy).then_inc(b_ptc, 1)
                        act.wait_ge(b_o, b + 1)
                        act.sem_inc(k_free[bb], 1)
                fence()
                act.wait_ge(u_o, 2)
                for n in range(2):
                    act.activation(OC[:, 8 * n:8 * n + 8, NP_:T],
                                   PS[:, n, 0:8 * NB].rearrange("p (a b) -> p a b", a=8), ACT.Copy)
                fence()

            act.wait_ge(const_in, 112)
            act.activation(CE.rearrange("p a b -> p (a b)"), CR.rearrange("p a b -> p (a b)"),
                           ACT.Exp, scale=-1.0).then_inc(c_exp, 1)
            fence()
            pre_norm(0)
            for s in range(6):
                if s == 1:
                    hgrn()
                    ssm()
                elif s == 4:
                    mla()
                else:
                    ffn_up(s, FFN_OF[s])
                down(s)
                post_norm(s)
                if s < 5:
                    pre_norm(s + 1)
            fence()

        @block.vector
        def _(dve):
            fence = fencer(dve)
            tt, ts, stt = dve.tensor_tensor, dve.tensor_scalar, dve.scalar_tensor_tensor
            dve.sem_inc(mod_sums, 1)
            dve.sem_inc(gu_taken, 2)
            dve.sem_inc(y_taken, 2)
            dve.sem_inc(part_done, 2)
            dve.sem_inc(p_oc, 2)
            dve.sem_inc(h_done, 1)
            dve.sem_inc(h_ptk, 2)

            def bcast(ap, axis, n):
                ap = ap.unsqueeze(axis)
                shape = list(ap.shape)
                shape[axis] = n
                return ap.to_broadcast(shape)

            def mod_copy(s, i, jj):
                dve.wait_ge(mod_sums, i * 2 + (s * 8 + jj + 2))
                if s == 0:
                    dve.sem_inc(w_free, 1)
                dve.tensor_copy(MS, PS[:, 4, 0:3 * P]).then_inc(mod_copied, 1)

            def mod_bias(s, i, jj):
                dve.wait_ge(mod_ready, i * 2 + (s * 8 + jj + 1))
                start = i * 6 + 3 * jj
                tt(MOD[:, bass.ds(start, 3), :], PS[:, 5, 0:3 * NSEQ].rearrange("p (a b) -> p a b", a=3),
                   bcast(ADB[:, s, bass.ds(start, 3)], 2, NSEQ), ALU.add)

            def modulation(s):
                with dve.Fori(0, NMOD // 6) as i:
                    for jj in range(2):
                        mod_copy(s, i, jj)
                        mod_bias(s, i, jj)
                fence()

            def clear_sum():
                dve.memset(R[:, :], 0.0)
                dve.drain()

            def add_squares(s, i, jj):
                dve.wait_ge(y_taken, i * 2 + (s * DC + jj + 3))
                squares = SQ[:, jj, :] if s % 3 == 1 else H[:, i * 2 + jj, :]
                tt(R[:, :], R[:, :], squares, ALU.add)
                dve.drain()

            def cut_of(stage):
                base = LOADS[stage]

                def cut(i, jj, j):
                    slot = (base + jj) % 2
                    g, buf = group(stage, i, jj, j)
                    n = tiles_in(stage, j) * P
                    dve.wait_ge(w_hi_ready, g + 1)
                    tt(WL_[:, buf, 0:n], W[:, slot, j * DC * P:j * DC * P + n], WH[:, buf, 0:n].bitcast(F32),
                       ALU.subtract).then_inc(w_rest_ready, 1)
                    if j == per_load(stage) - 1:
                        dve.drain().then_inc(w_free, 1)
                return cut

            def pre_norm(s):
                ffn = s % 3 != 1
                ts(AM[:, :, :], MOD[:, DC:2 * DC, :], 1.0, None, ALU.add)
                ts(GM[:, :, :], MOD[:, 2 * DC:3 * DC, :], 1.0 if s % 3 == 1 else 0.5, None, ALU.mult)
                dve.drain()
                tt(AM[:, :, :], AM[:, :, :], bcast(NPRE[:, s, :], 2, NSEQ), ALU.mult)
                tt(GM[:, :, :], GM[:, :, :], bcast(NPOST[:, s, :], 2, NSEQ), ALU.mult)
                if ffn:
                    for j in range(2):
                        cut_of(("up", s))(0, 0, j)
                dst = NORMED if ffn else H
                dve.wait_ge(root_ready, 2 * s + 1)
                tt(dst[:, :, NP_:T], X[:, :, NP_:T], bcast(R[:, NP_:T], 1, DC), ALU.mult)
                dve.drain()
                tt(dst[:, :, NP_:T], dst[:, :, NP_:T], AM[:, :, 1:NSEQ], ALU.mult)
                dve.drain()
                tt(dst[:, :, NP_:T], dst[:, :, NP_:T], MOD[:, 0:DC, 1:NSEQ], ALU.add)
                dve.drain()

                def scaled(c):
                    tt(dst[:, c, 0:NP_], X[:, c, 0:NP_], R[:, 0:NP_], ALU.mult).then_inc(xr_ready, 1)

                if s in NORM_OF:
                    hi, rest = (HH, HL) if ffn else (GHH, GHL)
                    scaled(0)
                    scaled(1)
                    for c in range(DC):
                        dve.wait_ge(hid_ready, s * DC + c + 1)
                        dve.tensor_copy(hi[:, c, :], dst[:, c, :])
                        dve.drain()
                        tt(rest[:, c, :], dst[:, c, :], hi[:, c, :].bitcast(F32), ALU.subtract)\
                            .then_inc(rest_ready, 1)
                        if c + 2 < DC:
                            scaled(c + 2)
                else:
                    for c in range(DC):
                        scaled(c)
                if not ffn:
                    fence()

            def post_norm(s):
                dve.wait_ge(root_ready, 2 * s + 2)
                tt(Y[:, :, NP_:T], Y[:, :, NP_:T], GM[:, :, 1:NSEQ], ALU.mult)
                dve.drain()
                tt(Y[:, :, NP_:T], Y[:, :, NP_:T], bcast(R[:, NP_:T], 1, DC), ALU.mult)
                for c in range(0, DC, 2):
                    for cc in range(c, c + 2):
                        stt(Y[:, cc, 0:NP_], Y[:, cc, 0:NP_], GM[:, cc, 0:1], R[:, 0:NP_], ALU.mult, ALU.mult)
                    dve.drain()
                    for cc in range(c, c + 2):
                        tt(X[:, cc, :], X[:, cc, :], Y[:, cc, :], ALU.add).then_inc(x_ready, 1)

            def ffn_up(s, f):
                def finish(i, jj):
                    n = i * 2 + jj
                    dve.wait_ge(silu_ready, n + (f * FC + 1))
                    gu = SILU[:, jj, :]
                    tt(two(gu), pair(4 * jj + 2), two(gu), ALU.mult).then_inc(gu_taken, 1)
                    dve.drain()
                    dve.tensor_copy(GB[:, n, :], gu)
                    dve.tensor_copy(GH_[:, n, :], gu)
                    dve.drain()
                    tt(GL[:, n, :], gu, GH_[:, n, :].bitcast(F32), ALU.subtract)
                staggered(dve, ("up", s), cut_of(("up", s)), finish, cut_next=cut_of(("down", s)))
                fence()

            def down(s):
                stage = ("down", s)

                def begin(i, jj):
                    if s < 5:
                        mod_copy(s + 1, i, jj)

                def finish(i, jj):
                    if s < 5:
                        mod_bias(s + 1, i, jj)
                    add_squares(s, i, jj)
                clear_sum()
                if s % 3 == 1:
                    for c in range(2 * DC):
                        if c % DC == 0:
                            cut_of(stage)(0, 0, c // DC)
                        if c % 2:
                            dve.wait_ge(oc_hi, s // 3 * DC + c // 2 + 1)
                        else:
                            dve.tensor_copy(OCH[:, c, :], OC[:, c, :])
                            dve.drain()
                        tt(OCL[:, c, :], OC[:, c, :], OCH[:, c, :].bitcast(F32), ALU.subtract).then_inc(oc_rest, 1)
                staggered(dve, stage, cut_of(stage), finish, begin)
                dve.sem_inc(acc_ready, 1)
                fence()

            def sigmoid(e):
                ts(e, e, 1.0, None, ALU.add)
                dve.drain()
                dve.reciprocal(e, e)
                dve.drain()

            def hgrn():
                def cut(h, c, ahead=0):
                    dve.wait_ge(w_hi_ready, hgrn_group(h, c) + (4 * ahead + 1))
                    tt(GWL[:, c % 2, :], hgrn_weights(c), GWH[:, c % 2, :].bitcast(F32), ALU.subtract)\
                        .then_inc(w_rest_ready, 1)
                    if c in (QUERY, VALUE):
                        dve.drain().then_inc(w_free, 1)

                for c in (FORGET, QUERY):
                    cut(0, c)
                dve.wait_ge(vec_in, 64)
                tt(LMX, LB[:, 0, :], LB[:, 1, :], ALU.max)
                dve.drain()
                tt(LMX, LMX, LB[:, 2, :], ALU.max)
                dve.drain()
                tt(LB, LB, bcast(LMX, 1, 3), ALU.subtract).then_inc(lb_exp, 1)
                dve.wait_ge(lb_exp, 2)
                tt(LMX, LB[:, 0, :], LB[:, 1, :], ALU.add)
                dve.drain()
                tt(LMX, LMX, LB[:, 2, :], ALU.add)
                dve.drain()
                dve.reciprocal(LMX, LMX)
                dve.drain()
                tt(HVEC[:, 0, :], LB[:, 0, :], LMX, ALU.mult)
                dve.drain()
                ts(HVEC[:, 1, :], HVEC[:, 0, :], -1.0, 1.0, ALU.mult, ALU.add)
                dve.drain()
                def forget(h, ahead=0):
                    dve.tensor_copy(HP[:, 0:2], HVEC[:, 0:2, bass.ds(h + ahead, 1)].rearrange("p a b -> p (a b)"))
                    dve.wait_ge(h_exp, h * 3 + (3 * ahead + 1))
                    ts(E2R, E2, 1e30, 1.0, ALU.min, ALU.add)
                    ts(E2, E2, 1e30, None, ALU.min)
                    dve.drain()
                    dve.reciprocal(E2R, E2R)
                    dve.drain()
                    ts(FG, E2R, HP[:, 1:2], HP[:, 0:1], ALU.mult, ALU.add).then_inc(h_f, 1)
                    stt(KK, E2, HP[:, 1:2], E2R, ALU.mult, ALU.mult)
                    cut(h, GATE, ahead)
                    dve.wait_ge(h_lf, h + (ahead + 1))
                    dve.tensor_tensor_scan(BB, const("reset"), EB, 0.0, ALU.mult, ALU.add)
                    dve.drain().then_inc(h_d, 1)

                forget(0)

                def head(h, more):
                    dve.tensor_copy(HP[:, 2:3], HVEC[:, 2, bass.ds(h, 1)])
                    cut(h, VALUE)
                    B4 = BB.rearrange("p (a b) -> p a b", b=CH)
                    tt(KD.rearrange("p (a b) -> p a b", b=CH), B4[:, :, CH - 1:CH].to_broadcast([P, NCH, CH]), B4,
                       ALU.subtract).then_inc(h_d, 1)
                    for n, m in enumerate(LEVELS):
                        b = BB.rearrange("p (a c b) -> p a c b", c=2, b=m)
                        d = DL[:, n, :].rearrange("p (a c b) -> p a c b", c=2, b=m)
                        ref = b[:, :, 0, m - 1:m].to_broadcast([P, NP_ // (2 * m), m])
                        tt(d[:, :, 1, :], b[:, :, 1, :], ref, ALU.subtract)
                        tt(d[:, :, 0, :], ref, b[:, :, 0, :], ALU.subtract).then_inc(h_d, 1)
                    dve.wait_ge(h_exp, h * 3 + 2)
                    dve.wait_ge(h_ex, h * 9 + 1)
                    tt(QI, QS[:, 0:NP_], EB, ALU.mult)
                    dve.wait_ge(h_exp, h * 3 + 3)
                    dve.wait_ge(h_ex, h * 9 + 2)
                    tt(KD, KD, KK[:, 0:NP_], ALU.mult).then_inc(h_kd, 1)
                    for n, m in enumerate(LEVELS):
                        dve.wait_ge(h_ex, h * 9 + (3 + n))
                        d = DL[:, n, :].rearrange("p (a c b) -> p a c b", c=2, b=m)
                        q = QS[:, 0:NP_].rearrange("p (a c b) -> p a c b", c=2, b=m)
                        k = KK[:, 0:NP_].rearrange("p (a c b) -> p a c b", c=2, b=m)
                        tt(d[:, :, 1, :], d[:, :, 1, :], q[:, :, 1, :], ALU.mult)
                        tt(d[:, :, 0, :], d[:, :, 0, :], k[:, :, 0, :], ALU.mult).then_inc(h_qk, 1)
                    if more:
                        cut(h, FORGET, 1)
                        cut(h, QUERY, 1)
                    ident = bcast(IDENT, 1, NCH)
                    for n in range(1 + len(LEVELS)):
                        dve.wait_ge(h_p, h * 8 + (n + 1))
                        src = PS[:, n % 2, :].rearrange("p (a b) -> p a b", a=NCH)
                        if n == 0:
                            tt(AT, src, ident, ALU.mult).then_inc(h_ptk, 1)
                            dve.drain()
                        else:
                            apart(dve)
                            dve.copy_predicated(AT, bcast(MSK[:, n - 1, :], 1, NCH), src).then_inc(h_ptk, 1)
                            dve.drain()
                    dve.sem_inc(h_att, 1)
                    dve.wait_ge(s_loaded, h * 16 + 16)
                    dve.wait_ge(h_vb, h + 1)
                    tt(S0, S0, bcast(FG[:, NP_:T], 2, P), ALU.mult)
                    for b in range(2):
                        tt(VK[:, 4 * b:4 * b + 4, :], PS[:, 6 + b, :].rearrange("p (a b) -> p a b", a=4),
                           bcast(KK[:, NP_ + 4 * b:NP_ + 4 * b + 4], 2, P), ALU.mult)
                    dve.drain().then_inc(h_vk, 1)
                    tt(S0, S0, VK, ALU.add).then_inc(s_new, 1)
                    dve.wait_ge(h_u, h + 1)
                    dve.wait_ge(s_stored, h + 1)
                    dve.tensor_copy(ST[:, 0, :], PS[:, 5, 0:P])
                    for c in range(1, NCH):
                        dve.drain()
                        stt(ST[:, c, :], ST[:, c - 1, :], EB[:, (c + 1) * CH - 1:(c + 1) * CH],
                            PS[:, 5, c * P:(c + 1) * P], ALU.mult, ALU.add)
                    dve.drain().then_inc(h_s, 1)
                    if more:
                        forget(h, 1)
                    dve.wait_ge(h_r, h + 1)
                    tt(R[:, 0:NP_], R[:, 0:NP_], PS[:, 6, :], ALU.mult)
                    tt(R[:, NP_:T], R[:, NP_:T], PS[:, 7, 0:NB], ALU.mult)
                    dve.drain()
                    stt(OC[:, h, :], R[:, :], HP[:, 2:3], GS, ALU.mult, ALU.mult)
                    dve.drain().then_inc(h_done, 1)

                with dve.Fori(0, HG - 1) as h:
                    head(h, True)
                head(HG - 1, False)
                dve.wait_ge(s_stored, HG + 1)
                fence()

            def ssm():
                dve.wait_ge(g_in, 80)
                dve.wait_ge(d_pe, 1)
                ts(two(DTV), pair(0, rows=16), SMS[:, 0:1], None, ALU.add)
                dve.drain()
                ts(DTE, DTV, -1.0, None, ALU.mult)
                dve.drain()
                tt(DTE, DTE, DTV, ALU.max).then_inc(d_step, 1)
                dve.wait_ge(d_act, 1)
                ts(SMS[:, 2:3], SMS[:, 2:3], -1.0, None, ALU.mult)
                ts(DTE, DTE, 1.0, None, ALU.add).then_inc(d_step, 1)
                dve.wait_ge(d_act, 2)
                stt(DT, DTV, 0.0, DTE, ALU.max, ALU.add)
                dve.drain()
                ts(DTV, DT, SMS[:, 2:3], None, ALU.mult)
                dve.drain().then_inc(d_step, 1)
                dve.tensor_tensor_scan(LA[:, 0:NP_], const("reset", 16), DTV[:, 0:NP_], 0.0, ALU.mult, ALU.add)
                dve.tensor_copy(LA[:, NP_:T], DTV[:, NP_:T])
                dve.drain().then_inc(d_step, 1)
                fence()
                dve.sem_inc(g_done, 1)
                with dve.Fori(0, SG_) as g:
                    dve.tensor_copy(CWG, CW[:, g])
                    dve.tensor_copy(DSN[:, 0:2], DSK[:, g])
                    dve.tensor_copy(DSN[:, 2:4], SNW[:, g])
                    dve.tensor_copy(DTG, DTT[:, :, bass.ds(g * GH, GH)])
                    dve.tensor_copy(BTG, BT[:, :, bass.ds(g * GH, GH)])
                    dve.tensor_copy(DTSG, DTS[:, bass.ds(g * GH, GH)])
                    dve.tensor_copy(SELG.rearrange("p a b -> p (a b)"), const("sel16", 16)[:, bass.ds(g * (GH * P), GH * P)])
                    dve.drain().then_inc(g_sel, 1)
                    dve.wait_ge(st_in, g * 32 + 32)
                    for c in range(4):
                        dve.wait_ge(g_raw, g * 4 + (c + 1))
                        ts(CV[:, c, :], XR[:, c, :], CWG[:, c, 3:4], CWG[:, c, 4:5], ALU.mult, ALU.add)
                        for tap in range(3):
                            dve.drain()
                            d = 3 - tap
                            stt(CV[:, c, d:NP_], XR[:, c, 0:NP_ - d], CWG[:, c, tap:tap + 1], CV[:, c, d:NP_],
                                ALU.mult, ALU.add)
                            stt(CV[:, c, NP_:T], STC[:, c, tap, :], CWG[:, c, tap:tap + 1], CV[:, c, NP_:T],
                                ALU.mult, ALU.add)
                    dve.drain().then_inc(g_conv, 1)
                    dve.wait_ge(g_tr, g + 1)
                    for x in range(2):
                        tt(XD[:, 2 * x:2 * x + 2], PS[:, 4 + x, :].rearrange("p (a b c) -> p a b c", a=2, b=GH),
                           bcast(DTG[:, 2 * x:2 * x + 2, :], 3, HD), ALU.mult)
                    tt(XDS.rearrange("p (a b) -> p a b", a=GH), PS[0:NB, 7, 0:GH * HD].rearrange("p (a b) -> p a b", a=GH),
                       bcast(DTSG, 2, HD), ALU.mult)
                    dve.drain().then_inc(g_xd, 1)
                    dve.wait_ge(g_cb, g + 1)
                    tt(CBM, PS[:, 6, :].rearrange("p (a b) -> p a b", a=NCH), bcast(const("causal"), 1, NCH), ALU.mult)
                    dve.wait_ge(g_bcx, g * 4 + 4)
                    last_b = PS[:, 0:GH, CH - 1:NP_:CH]
                    dve.tensor_copy(EL, last_b)
                    tt(WL, last_b, BTG.rearrange("p a b -> p b a"), ALU.subtract)
                    dve.drain().then_inc(g_wl, 1)
                    for j in range(GH):
                        for c in range(NCH):
                            cc = slice(c * CH, (c + 1) * CH)
                            last = ts(SEG[:, j, cc], PS[:, j, cc], BTG[:, c, j:j + 1], 0.0, ALU.subtract, ALU.min)
                        last.then_inc(g_seg, 1)
                    dve.drain().then_inc(g_bcfree, 1)
                    dve.wait_ge(g_wle, g + 1)
                    for c in range(NCH):
                        tt(XW[:, c], XD[:, c], bcast(WL[:, :, c], 2, HD), ALU.mult)
                    dve.drain().then_inc(g_xw, 1)
                    for j in range(GH):
                        tt(CEX[:, j, :], CEX[:, j, :], CV[:, 3, 0:NP_], ALU.mult)
                        dve.wait_ge(g_sege, g * 4 + (j + 1))
                        tt(SEG[:, j, :], SEG[:, j, :], CBM.rearrange("p a b -> p (a b)"), ALU.mult).then_inc(g_m, 1)
                    dve.wait_ge(g_u, g + 1)
                    u = [PS[:, 6 + c // 2, (c % 2) * 256:(c % 2 + 1) * 256].rearrange("p (a b) -> p a b", a=GH)
                         for c in range(NCH)]
                    dve.tensor_copy(SS[:, 0], u[0])
                    for c in range(1, NCH):
                        dve.drain()
                        tt(SS[:, c], SS[:, c - 1], bcast(EL[:, :, c], 2, HD), ALU.mult)
                        dve.drain()
                        tt(SS[:, c], SS[:, c], u[c], ALU.add)
                    dve.drain().then_inc(g_s, 1)
                    for j in range(GH):
                        tt(SM0[:, :, j, :], SM0[:, :, j, :], bcast(EA[:, j, :], 2, HD), ALU.mult)
                    dve.drain().then_inc(g_uu, 1)
                    dve.wait_ge(g_xb, g + 1)
                    for b in range(NB):
                        stt(SM0[:, b].rearrange("p a b -> p (a b)"), PS[:, b // 2, (b % 2) * 256:(b % 2 + 1) * 256],
                            CV[:, 2, NP_ + b:NP_ + b + 1], SM0[:, b].rearrange("p a b -> p (a b)"), ALU.mult, ALU.add)
                    dve.drain().then_inc(g_uu, 1)
                    dve.wait_ge(g_y, g * 2 + 2)
                    for x in range(2):
                        stt(EV[:, x, 0:NP_], CV[:, x, 0:NP_], DSN[:, x:x + 1], PS[:, 6 + x, :], ALU.mult, ALU.add)
                        stt(EV[:, x, NP_:T], CV[:, x, NP_:T], DSN[:, x:x + 1], PS[:, 1, x * NB:(x + 1) * NB],
                            ALU.mult, ALU.add)
                    dve.drain()
                    tt(EV[:, 0:2, :], EV[:, 0:2, :], GZ, ALU.mult)
                    dve.drain().then_inc(g_yv, 1)
                    dve.wait_ge(g_r, g + 1)
                    for x in range(2):
                        stt(OC[:, g * 2 + (HG + x), :], EV[:, x, :], DSN[:, 2 + x:3 + x], R[:, :], ALU.mult, ALU.mult)
                    dve.drain().then_inc(g_done, 1)
                dve.wait_ge(st_ok, SG_ + 1)
                fence()

            def mla():
                dve.wait_ge(m_root, 1)
                dve.wait_ge(m_cks, 48)
                for c in range(4):
                    stt(CQ[:, c, :], CQ[:, c, :], GQ[:, c:c + 1], R[:, :], ALU.mult, ALU.mult)
                dve.drain().then_inc(m_norm, 1)
                dve.wait_ge(m_root, 2)
                for c in range(RC):
                    stt(CKV[:, c, :], CKV[:, c, :], GKV[:, c:c + 1], R[:, :], ALU.mult, ALU.mult)
                dve.drain().then_inc(m_norm, 1)
                dve.wait_ge(m_perm, 1)
                rotate(KPE).then_inc(m_norm, 1)
                fence()
                def row_max(n, hh, qb):
                    dve.wait_ge(p_sc, n * 8 + (hh * 4 + qb + 1))
                    s = PS[:, 4 * hh + qb, 0:(qb + 1) * P]
                    tt(s[:, qb * P:], s[:, qb * P:], const("neg"), ALU.add)
                    dve.drain()
                    dve.reduce_max(SMX[:, hh, qb:qb + 1], s, AX_X)
                    dve.drain()
                    ts(SNB[:, hh, qb:qb + 1], SMX[:, hh, qb:qb + 1], -SCALE, None, ALU.mult).then_inc(p_mx, 1)

                def normalise(n, hh, qb):
                    p = PR[:, hh, qb, 0:(qb + 1) * P]
                    dve.wait_ge(p_pr, n * 8 + (hh * 4 + qb + 1))
                    dve.reciprocal(SRI[:, hh, qb:qb + 1], SRS[:, hh, qb:qb + 1])
                    dve.drain()
                    ts(p, p, SRI[:, hh, qb:qb + 1], None, ALU.mult).then_inc(p_pn, 1)

                with dve.Fori(0, MH // 4) as i:
                    for jj in range(2):
                        n = i * 2 + jj
                        dve.wait_ge(p_ql, n + 1)
                        dve.tensor_copy(QL[:, :, bass.ds(n * 2, 2), :].rearrange("p r h b -> p h r b"),
                                        PS[:, 0, 0:4 * NB].rearrange("p (h r b) -> p h r b", h=2, r=RC))\
                           .then_inc(p_qlt, 1)
                        rotate(QP).then_inc(p_qp, 1)
                        dve.drain()
                        for hh in range(2):
                            dve.tensor_copy(QPS[:, n * 2 + hh, :], QP[hh * ROPE:(hh + 1) * ROPE, NP_:T])
                        for qb in range(4):
                            row_max(n, 0, qb)
                        for qb in range(4):
                            row_max(n, 1, qb)
                            normalise(n, 0, qb)
                        for qb in range(4):
                            normalise(n, 1, qb)
                fence()
                for buf, value in ((QLB, 0.0), (QPB, 0.0), (DST[:, 1:2], NEG), (DST[:, 5:6], 0.0)):
                    dve.memset(buf, value)
                dve.drain()
                with dve.Fori(0, NB) as b:
                    dve.tensor_copy(QLB[:, :, 0:MH], QL[:, :, :, b])
                    dve.tensor_copy(QPB[0:ROPE, 0, 0:MH], QPS[:, :, b])
                    dve.tensor_copy(QPB[ROPE:P, 1, 0:MH], QPS[:, :, b])
                    dve.drain().then_inc(b_q, 1)
                    dve.wait_ge(b_sc, b + 1)
                    dve.reduce_max(DST[:, 0:1], PS[:, 0, :], AX_X)
                    tt(PDO, PS[0:QR_, 1, 0:NB], const("own", QR_)[:, bass.ds(b * NB, NB)], ALU.add)
                    dve.drain()
                    dve.reduce_max(DST[0:QR_, 1:2], PDO, AX_X)
                    dve.drain()
                    tt(DST[:, 2:3], DST[:, 0:1], DST[:, 1:2], ALU.max).then_inc(b_m, 1)
                    dve.wait_ge(b_mt, b * 2 + 1)
                    dve.reduce_max(ROW[:, 0:QR_], PS[0:1, 2, 0:P].rearrange("p (a b) -> p b a", a=QUARTERS), AX_X)
                    dve.drain()
                    ts(ROW[:, QR_:QR_ + P].rearrange("p (a b) -> p a b", a=QUARTERS),
                       bcast(ROW[:, 0:QR_], 1, QUARTERS), -SCALE, None, ALU.mult).then_inc(b_m, 1)
                    dve.wait_ge(b_mt, b * 2 + 2)
                    dve.tensor_copy(DST[:, 3:4], PS[:, 3, 0:1]).then_inc(b_mx, 1)
                    dve.wait_ge(b_ex, b + 1)
                    tt(DST[:, 6:7], DST[:, 4:5], DST[:, 5:6], ALU.add).then_inc(b_sum, 1)
                    dve.wait_ge(b_tot, b + 1)
                    dve.reciprocal(DST[:, 7:8], PS[:, 7, 0:1])
                    dve.drain()
                    dve.wait_ge(b_o, b + 1)
                    ts(OP, PS[:, 6, 0:RC * P], DST[:, 7:8], None, ALU.mult).then_inc(b_on, 1)
                    dve.wait_ge(b_oc, b + 1)
                    dve.tensor_copy(OL[:, :, :, b], PS[:, 7, MH:MH + RC * MH].rearrange("p (a b) -> p a b", a=RC))
                fence()
                dve.wait_ge(out_stored, 32 * HG + 32)
                fence()

            def rotate(dst):
                tt(two(TMP), pair(2), two(const("sin")), ALU.mult)
                tt(dst, QR, const("cos"), ALU.mult)
                dve.drain()
                return tt(dst, dst, TMP, ALU.add)

            dve.wait_ge(const_in, 112)
            dve.wait_ge(c_exp, 1)
            dve.memset(CS[:, :, :], 0.0)
            sigmoid(CE)
            tt(CS[:, :, 0:NSEQ], CR, CE, ALU.mult).then_inc(c_exp, 1)
            modulation(0)
            pre_norm(0)
            for s in range(6):
                if s == 1:
                    hgrn()
                    ssm()
                elif s == 4:
                    mla()
                else:
                    ffn_up(s, FFN_OF[s])
                down(s)
                post_norm(s)
                if s < 5:
                    pre_norm(s + 1)
            fence()


def _tiled(w, k, n):
    return w.reshape(k, P, n, P).transpose(2, 1, 0, 3)


def _lay_out(v):
    cat = np.concatenate
    c = np.ascontiguousarray
    out = {}
    out["const"], out["mixer_const"], out["masks"] = constants()
    x = cat([v["x_prompt"][0], v["x_sample"][:, 0]])
    out["x"] = x.T.reshape(DC, P, T).transpose(1, 0, 2)
    out["c"] = cat([v["c_prompt"], v["c_sample"]]).T.reshape(DC, P, NSEQ).transpose(1, 0, 2)
    out["ada_w"] = v["ada_w"].reshape(2, DC, P, 24, 3 * P).transpose(0, 3, 2, 1, 4).reshape(48, P, 3 * DC * P)
    out["ada_b"] = v["ada_b"].reshape(6, NMOD, P).transpose(2, 0, 1)
    out["norm_pre"] = v["norm_pre"].reshape(6, DC, P).transpose(2, 0, 1)
    out["norm_post"] = v["norm_post"].reshape(6, DC, P).transpose(2, 0, 1)
    g, u = (v[n].reshape(4, DC, P, FC, P).transpose(0, 3, 2, 1, 4).reshape(4 * FC, P, DC * P)
            for n in ("ffn_wg", "ffn_wu"))
    out["ffn_gu"] = cat([g, u], axis=2)
    out["ffn_wd"] = v["ffn_wd"].reshape(4, FC, P, DC, P).transpose(0, 3, 2, 1, 4).reshape(4 * DC, P, FC * P)
    w = v["w_in_ab"]
    q, f, i, gate = (_tiled(w[:, n * 1024:(n + 1) * 1024], DC, HG) for n in range(4))
    z = _tiled(w[:, 4096:5120], DC, DC)
    xs = _tiled(w[:, 5120:6144], DC, DC)
    b = _tiled(w[:, 6144:6656], DC, SG_)
    cc = _tiled(w[:, 6656:7168], DC, SG_)
    out["w_hgrn"] = np.stack([cat([q, f], axis=2), cat([i, gate], axis=2)], axis=1).reshape(2 * HG, P, 2 * DC * P)
    out["w_ssm"] = np.stack([cat([xs[0::2], xs[1::2], b], axis=2), cat([cc, z[0::2], z[1::2]], axis=2)],
                            axis=1).reshape(2 * SG_, P, 3 * DC * P)
    out["w_dt"] = w[:, 7168:].reshape(DC, P, 16).transpose(1, 0, 2)
    out["w_out_ab"] = _tiled(v["w_out_ab"], 16, DC).reshape(DC, P, 16 * P)
    out["lb_logits"] = v["hg_lb_logits"].reshape(3, HG, P).transpose(2, 0, 1)
    out["hg_norm"] = v["hg_norm"].reshape(HG, P).T
    out["state_hgrn"] = v["state_hgrn"].transpose(1, 2, 0, 3)
    out["ssm_small"] = np.stack([v["ssm_dt_bias"], v["ssm_a_log"]], axis=1)

    def channels(a):
        n = a.shape[0]
        xs = a[:, :1024].reshape(n, SG_, 2, P)
        bc = a[:, 1024:].reshape(n, 2, SG_, P).transpose(0, 2, 1, 3)
        return cat([xs, bc], axis=2).transpose(1, 3, 2, 0)

    out["conv_w"] = cat([channels(v["ssm_conv_w"]), channels(v["ssm_conv_b"][None])], axis=3).transpose(1, 0, 2, 3)
    out["state_conv"] = channels(v["state_conv"].reshape(NB * 3, 2048)).reshape(SG_, P, 4, NB, 3).transpose(0, 1, 2, 4, 3)
    out["state_ssm"] = v["state_ssm"].reshape(NB, SG_, GH, P, HD).transpose(1, 3, 0, 2, 4)
    out["ssm_d"] = np.repeat(v["ssm_d"], HD).reshape(SG_, 2, P).transpose(2, 0, 1)
    out["ssm_norm"] = v["ssm_norm"].reshape(SG_, 2, P).transpose(2, 0, 1)
    out["mla_dq"] = _tiled(v["mla_w_dq"], DC, 4).reshape(2, 2, P, DC * P).transpose(0, 2, 1, 3)
    dkv = v["mla_w_dkv"]
    kpe = dkv[:, 256:].reshape(DC, P, ROPE).transpose(1, 0, 2)
    out["mla_dkv"] = cat([_tiled(dkv[:, :256], DC, RC).transpose(1, 0, 2, 3).reshape(P, 2 * DC, P),
                          cat([kpe, kpe], axis=2)], axis=1)
    uq = v["mla_w_uq"].reshape(4, P, 8, 2, 192)
    nope = uq[..., :128].transpose(2, 1, 3, 0, 4).reshape(8, P, -1)
    rope = uq[..., 128:].transpose(2, 1, 0, 3, 4).reshape(8, P, -1)
    uk = v["mla_w_uk"].reshape(RC, P, 8, 2, P)
    ukn = uk.transpose(2, 1, 3, 0, 4).reshape(8, P, -1)
    ukt = v["mla_w_uk"].reshape(256, 8, 2, P).transpose(1, 3, 2, 0).reshape(8, P, -1)
    uv = v["mla_w_uv"].reshape(RC, P, 8, 2, P).transpose(2, 1, 0, 3, 4).reshape(8, P, -1)
    out["mla_pairs"] = cat([nope, rope, ukn, uv, ukt], axis=2)
    out["mla_uv"] = v["mla_w_uv"].reshape(RC, P, 2, 8 * P).transpose(2, 1, 0, 3).reshape(2, P, 16 * P)
    out["mla_wo"] = _tiled(v["mla_w_o"], 16, DC).reshape(DC, P, 16 * P)
    out["mla_gq"] = v["mla_g_q"].reshape(4, P).T
    out["mla_gkv"] = v["mla_g_kv"].reshape(RC, P).T
    n_phys = v["cache_ckv"].shape[0]
    latent_t = v["cache_ckv"].reshape(n_phys, PAGE, RC, P).transpose(0, 3, 2, 1).reshape(n_phys, P, RC * PAGE)
    rope_t = v["cache_kpe"].reshape(n_phys, 2, 64, ROPE).transpose(0, 1, 3, 2).reshape(n_phys, P, 64)
    out["pages"] = cat([latent_t, v["cache_ckv"], rope_t], axis=2)
    out["page_table"] = v["page_table"].reshape(1, -1)
    shapes = {"mla_dq": (2, P, 16 * P), "mla_dkv": (P, 24 * P)}
    return {n: c(a).reshape(shapes.get(n, a.shape)) for n, a in out.items()}


_OUTS = {"y": (P, DC, T), "hgrn_prompt": (HG, P, P), "hgrn_sample": (HG, P, NB, P),
         "ssm_prompt": (SG_, P, GH, HD), "ssm_sample": (SG_, P, NB, GH, HD),
         "conv_prompt": (SG_, P, 4, 3), "conv_sample": (SG_, P, 4, 3, NB), "ckv": (P, RC, T), "kpe": (ROPE, T)}


def kernel(**inputs):
    import concourse.bacc as _bacc
    from concourse import mybir as _mybir
    from concourse.bass_utils import run_bass_kernel_spmd as _run

    arrays = _lay_out({n: np.asarray(a) for n, a in inputs.items()})
    nc = _bacc.Bacc("TRN2", target_bir_lowering=False, num_devices=1)
    A = {n: nc.dram_tensor(f"in_{n}", a.shape, _mybir.dt.from_np(a.dtype), kind="ExternalInput").ap()
         for n, a in arrays.items()}
    O = {n: nc.dram_tensor(f"out_{n}", s, F32, kind="ExternalOutput").ap() for n, s in _OUTS.items()}
    build_program(nc, A, O)
    r = _run(nc, [{f"in_{n}": a for n, a in arrays.items()}], core_ids=[0]).results[0]
    o = {n: np.asarray(r[f"out_{n}"]) for n in _OUTS}

    y = o["y"].transpose(2, 1, 0).reshape(T, D)
    ckv = o["ckv"].transpose(2, 1, 0).reshape(T, RC * P)
    kpe = o["kpe"].T

    def rows(a):
        a = a.transpose(3, 0, 2, 1)
        return np.concatenate([a[:, :, 0:2].reshape(a.shape[0], -1), a[:, :, 2].reshape(a.shape[0], -1),
                               a[:, :, 3].reshape(a.shape[0], -1)], axis=1)

    conv_s = rows(o["conv_sample"].reshape(SG_, P, 4, 3 * NB)).reshape(3, NB, 2048).transpose(1, 0, 2)
    return (y[None, :NP_], y[NP_:, None],
            o["hgrn_prompt"][None], o["hgrn_sample"].transpose(2, 0, 1, 3),
            o["ssm_prompt"].transpose(0, 2, 1, 3).reshape(1, 16, P, HD),
            o["ssm_sample"].transpose(2, 0, 3, 1, 4).reshape(NB, 16, P, HD),
            rows(o["conv_prompt"])[None], conv_s,
            ckv[None, :NP_], ckv[NP_:, None], kpe[None, :NP_], kpe[NP_:, None])
```
